# Optimizing a Trainium2 kernel written in Bass

```python
import math
import jax, jax.numpy as jnp
from jax import lax
import numpy as np

D_MODEL = 1024
BATCH = 1
SEQ = 512
DEPTH = 1
DEC_BATCH = 1
DEC_SEQ = 64
PAST_LEN = 512

CHUNK = 64
N_META = 16
QBLOCK = 128
EPS = 1e-6
D_SSM = 2 * D_MODEL
SSM_HEAD_DIM = 64
SSM_HEADS = D_SSM // SSM_HEAD_DIM
SSM_GROUPS = 8
SSM_HPG = SSM_HEADS // SSM_GROUPS
D_STATE = 128
CONV_W = 4
D_CONV = D_SSM + 2 * SSM_GROUPS * D_STATE
ATTN_HEADS = 16
ATTN_HEAD_DIM = 64
D_ATTN = ATTN_HEADS * ATTN_HEAD_DIM
D_FF = 2816
OFF_XBC = D_SSM
OFF_DT = OFF_XBC + D_CONV
OFF_Q = OFF_DT + SSM_HEADS
OFF_K = OFF_Q + D_ATTN
OFF_V = OFF_K + D_ATTN
OFF_F = OFF_V + D_ATTN
OFF_GS = OFF_F + ATTN_HEADS
OFF_GA = OFF_GS + D_MODEL
D_IN_PROJ = OFF_GA + D_MODEL

kernel_name = 'fox_ssd_gated_hybrid_stream'

def rmsnorm(x, g):
    xf = x.astype(jnp.float32)
    y = xf * lax.rsqrt(jnp.mean(xf * xf, axis=-1, keepdims=True) + EPS)
    return (y * g.astype(jnp.float32)).astype(x.dtype)

def swiglu(x, w_in, w_out):
    a, b = jnp.split(x @ w_in, 2, axis=-1)
    return (jax.nn.silu(a) * b) @ w_out

def pad_time(a, front, back):
    cfg = [(0, 0)] * a.ndim
    cfg[1] = (front, back)
    return jnp.pad(a, cfg)

def causal_conv(xbc, hist, w, b):
    L = xbc.shape[1]
    xp = jnp.concatenate([hist.astype(xbc.dtype), xbc], axis=1)
    out = b + w[0] * xp[:, 0:L]
    for j in range(1, CONV_W):
        out = out + w[j] * xp[:, j:j + L]
    return jax.nn.silu(out), xp[:, -(CONV_W - 1):]

def ssd_chunked(x, dt, a, bmat, cmat, init):
    b, L = x.shape[:2]
    nc = L // CHUNK
    xd = (x * dt[..., None]).reshape(b, nc, CHUNK, SSM_GROUPS, SSM_HPG, SSM_HEAD_DIM)
    adt = (a * dt).reshape(b, nc, CHUNK, SSM_GROUPS, SSM_HPG)
    a_cs = jnp.cumsum(jnp.moveaxis(adt, 2, -1), axis=-1)
    bc = bmat.reshape(b, nc, CHUNK, SSM_GROUPS, D_STATE)
    cc = cmat.reshape(b, nc, CHUNK, SSM_GROUPS, D_STATE)
    seg = a_cs[..., :, None] - a_cs[..., None, :]
    causal = jnp.tril(jnp.ones((CHUNK, CHUNK), bool))
    ldec = jnp.exp(jnp.where(causal, seg, -jnp.inf))
    cb = jnp.einsum('bclgn,bcsgn->bcgls', cc, bc)
    y_diag = jnp.einsum('bcgls,bcgrls,bcsgrp->bclgrp', cb, ldec, xd)
    decay_st = jnp.exp(a_cs[..., -1:] - a_cs)
    st = jnp.einsum('bcsgn,bcgrs,bcsgrp->bcgrpn', bc, decay_st, xd)
    chunk_dec = jnp.exp(a_cs[..., -1])

    def step(carry, inp):
        s_c, d_c = inp
        return carry * d_c[..., None, None] + s_c, carry

    init_g = init.astype(jnp.float32).reshape(b, SSM_GROUPS, SSM_HPG, SSM_HEAD_DIM, D_STATE)
    final, prev = lax.scan(step, init_g, (jnp.moveaxis(st, 1, 0), jnp.moveaxis(chunk_dec, 1, 0)))
    prev = jnp.moveaxis(prev, 0, 1)
    y_off = jnp.einsum('bclgn,bcgrpn,bcgrl->bclgrp', cc, prev, jnp.exp(a_cs))
    y = (y_diag + y_off).reshape(b, L, SSM_HEADS, SSM_HEAD_DIM)
    return y, final.reshape(b, SSM_HEADS, SSM_HEAD_DIM, D_STATE)

def ssm_branch(z, xbc, dt_raw, conv_hist, ssm_init, front, back, lw):
    b, L = z.shape[:2]
    f32 = jnp.float32
    xbc, conv_state = causal_conv(xbc, conv_hist, lw['conv_w'], lw['conv_b'])
    xs, bm, cm = jnp.split(xbc, [D_SSM, D_SSM + SSM_GROUPS * D_STATE], axis=-1)
    xs = xs.reshape(b, L, SSM_HEADS, SSM_HEAD_DIM).astype(f32)
    bm = bm.reshape(b, L, SSM_GROUPS, D_STATE).astype(f32)
    cm = cm.reshape(b, L, SSM_GROUPS, D_STATE).astype(f32)
    dt = jax.nn.softplus(dt_raw.astype(f32) + lw['dt_bias'].astype(f32))
    a = -jnp.exp(lw['a_log'].astype(f32))
    y, final = ssd_chunked(pad_time(xs, front, back), pad_time(dt, front, back), a,
                           pad_time(bm, front, back), pad_time(cm, front, back), ssm_init)
    y = y[:, front:front + L] + lw['d_skip'].astype(f32)[:, None] * xs
    y = y.reshape(b, L, D_SSM) * jax.nn.silu(z.astype(f32))
    yg = y.reshape(b, L, SSM_GROUPS, D_SSM // SSM_GROUPS)
    yg = yg * lax.rsqrt(jnp.mean(yg * yg, axis=-1, keepdims=True) + EPS)
    y = yg.reshape(b, L, D_SSM) * lw['ssm_norm'].astype(f32)
    return y.astype(z.dtype), conv_state, final.astype(z.dtype)

def fox_attend(q, k, v, cq, ck, q_pos, k_pos):
    b, Lq = q.shape[:2]
    nb = -(-Lq // QBLOCK)
    pad = nb * QBLOCK - Lq
    qb = jnp.moveaxis(pad_time(q, 0, pad).reshape(b, nb, QBLOCK, ATTN_HEADS, ATTN_HEAD_DIM), 1, 0)
    cqb = jnp.moveaxis(pad_time(cq, 0, pad).reshape(b, nb, QBLOCK, ATTN_HEADS), 1, 0)
    pb = jnp.pad(q_pos, (0, pad), mode='edge').reshape(nb, QBLOCK)
    ckh = jnp.moveaxis(ck, 1, 2)
    scale = ATTN_HEAD_DIM ** -0.5

    def block(args):
        qi, cqi, pi = args
        s = jnp.einsum('bqhd,bkhd->bhqk', qi, k, preferred_element_type=jnp.float32) * scale
        s = s + jnp.moveaxis(cqi, 1, 2)[..., None] - ckh[:, :, None, :]
        s = jnp.where(k_pos[None, :] <= pi[:, None], s, -jnp.inf)
        p = jax.nn.softmax(s, axis=-1)
        return jnp.einsum('bhqk,bkhd->bqhd', p.astype(v.dtype), v)

    out = lax.map(block, (qb, cqb, pb))
    return jnp.moveaxis(out, 0, 1).reshape(b, nb * QBLOCK, ATTN_HEADS, ATTN_HEAD_DIM)[:, :Lq]

def pre_mix(h, lw):
    h = h + 0.5 * swiglu(rmsnorm(h, lw['norm_ffn1']), lw['ffn1_w_in'], lw['ffn1_w_out'])
    return h, rmsnorm(h, lw['norm_mix'])

def split_kvf(p, f_bias):
    b, L = p.shape[:2]
    k, v, f = jnp.split(p, [D_ATTN, 2 * D_ATTN], axis=-1)
    logf = jax.nn.log_sigmoid(f.astype(jnp.float32) + f_bias.astype(jnp.float32))
    return (k.reshape(b, L, ATTN_HEADS, ATTN_HEAD_DIM), v.reshape(b, L, ATTN_HEADS, ATTN_HEAD_DIM), logf)

def empty_history(b, dtype):
    return (jnp.zeros((b, CONV_W - 1, D_CONV), dtype),
            jnp.zeros((b, SSM_HEADS, SSM_HEAD_DIM, D_STATE), jnp.float32),
            jnp.zeros((b, 0, ATTN_HEADS, ATTN_HEAD_DIM), dtype),
            jnp.zeros((b, 0, ATTN_HEADS, ATTN_HEAD_DIM), dtype),
            jnp.zeros((b, 0, ATTN_HEADS), jnp.float32))

def layer(h, lw, conv_hist, ssm_init, k_pre, v_pre, logf_pre, front, back):
    b, L = h.shape[:2]
    h, u = pre_mix(h, lw)
    proj = u @ lw['w_in']
    z, xbc, dt_raw, q, kvf, g_ssm, g_attn = jnp.split(proj, [OFF_XBC, OFF_DT, OFF_Q, OFF_K, OFF_GS, OFF_GA], axis=-1)
    k, v, logf = split_kvf(kvf, lw['f_bias'])
    q = q.reshape(b, L, ATTN_HEADS, ATTN_HEAD_DIM)
    o_ssm, conv_state, ssm_state = ssm_branch(z, xbc, dt_raw, conv_hist, ssm_init, front, back, lw)
    P = k_pre.shape[1]
    k_all = jnp.concatenate([k_pre.astype(k.dtype), k], axis=1)
    v_all = jnp.concatenate([v_pre.astype(v.dtype), v], axis=1)
    c_all = jnp.cumsum(jnp.concatenate([logf_pre.astype(jnp.float32), logf], axis=1), axis=1)
    o_attn = fox_attend(q, k_all, v_all, c_all[:, P:], c_all, P + jnp.arange(L), jnp.arange(P + L))
    merged = (jax.nn.sigmoid(g_ssm) * (o_ssm @ lw['w_br_ssm'])
              + jax.nn.sigmoid(g_attn) * (o_attn.reshape(b, L, D_ATTN) @ lw['w_br_attn']))
    h = h + merged @ lw['w_out']
    h = h + 0.5 * swiglu(rmsnorm(h, lw['norm_ffn2']), lw['ffn2_w_in'], lw['ffn2_w_out'])
    return h, k, v, logf, ssm_state, conv_state

def setup_inputs(seed: int = 0) -> dict:
    key = jax.random.key(seed)
    ks = jax.random.split(key, 27)
    f32 = jnp.float32

    def nrm(k, shape, scale=1.0):
        return jax.random.normal(k, shape, f32) * scale

    def gain(k, shape):
        return 1.0 + 0.02 * jax.random.normal(k, shape, f32)

    dt0 = jnp.exp(jax.random.uniform(ks[15], (DEPTH, SSM_HEADS), f32, math.log(1e-3), math.log(1e-1)))
    return {
        'x_prompt': nrm(ks[0], (BATCH, SEQ, D_MODEL)),
        'x_sample': nrm(ks[1], (DEC_BATCH, DEC_SEQ, D_MODEL)),
        'cache_k': nrm(ks[2], (DEPTH, DEC_BATCH, PAST_LEN, ATTN_HEADS, ATTN_HEAD_DIM)),
        'cache_v': nrm(ks[3], (DEPTH, DEC_BATCH, PAST_LEN, ATTN_HEADS, ATTN_HEAD_DIM)),
        'cache_logf': jax.nn.log_sigmoid(2.0 + nrm(ks[4], (DEPTH, DEC_BATCH, PAST_LEN, ATTN_HEADS))),
        'state_ssm': nrm(ks[5], (DEPTH, DEC_BATCH, SSM_HEADS, SSM_HEAD_DIM, D_STATE), 0.5),
        'state_conv': nrm(ks[6], (DEPTH, DEC_BATCH, CONV_W - 1, D_CONV)),
        'meta_tokens': nrm(ks[7], (N_META, D_MODEL)),
        'norm_ffn1': gain(ks[8], (DEPTH, D_MODEL)),
        'ffn1_w_in': nrm(ks[9], (DEPTH, D_MODEL, 2 * D_FF), D_MODEL ** -0.5),
        'ffn1_w_out': nrm(ks[10], (DEPTH, D_FF, D_MODEL), D_FF ** -0.5),
        'norm_mix': gain(ks[11], (DEPTH, D_MODEL)),
        'w_in': nrm(ks[12], (DEPTH, D_MODEL, D_IN_PROJ), D_MODEL ** -0.5),
        'conv_w': nrm(ks[13], (DEPTH, CONV_W, D_CONV), CONV_W ** -0.5),
        'conv_b': nrm(ks[14], (DEPTH, D_CONV), 0.02),
        'dt_bias': dt0 + jnp.log(-jnp.expm1(-dt0)),
        'a_log': jnp.log(jax.random.uniform(ks[16], (DEPTH, SSM_HEADS), f32, 1.0, 16.0)),
        'd_skip': gain(ks[17], (DEPTH, SSM_HEADS)),
        'f_bias': jax.random.uniform(ks[18], (DEPTH, ATTN_HEADS), f32, 0.5, 3.0),
        'ssm_norm': gain(ks[19], (DEPTH, D_SSM)),
        'w_br_ssm': nrm(ks[20], (DEPTH, D_SSM, D_MODEL), D_SSM ** -0.5),
        'w_br_attn': nrm(ks[21], (DEPTH, D_ATTN, D_MODEL), D_ATTN ** -0.5),
        'w_out': nrm(ks[22], (DEPTH, D_MODEL, D_MODEL), D_MODEL ** -0.5),
        'norm_ffn2': gain(ks[23], (DEPTH, D_MODEL)),
        'ffn2_w_in': nrm(ks[24], (DEPTH, D_MODEL, 2 * D_FF), D_MODEL ** -0.5),
        'ffn2_w_out': nrm(ks[25], (DEPTH, D_FF, D_MODEL), D_FF ** -0.5),
        'norm_final': gain(ks[26], (D_MODEL,)),
    }

def reference(x_prompt, x_sample, cache_k, cache_v, cache_logf, state_ssm, state_conv, meta_tokens,
              norm_ffn1, ffn1_w_in, ffn1_w_out, norm_mix, w_in, conv_w, conv_b, dt_bias, a_log, d_skip,
              f_bias, ssm_norm, w_br_ssm, w_br_attn, w_out, norm_ffn2, ffn2_w_in, ffn2_w_out, norm_final):
    bp = x_prompt.shape[0]
    bs = x_sample.shape[0]
    hp = jnp.concatenate([jnp.broadcast_to(meta_tokens[None].astype(x_prompt.dtype), (bp, N_META, D_MODEL)), x_prompt], axis=1)
    hs = x_sample
    meta_h = meta_tokens[None]
    st_p = []
    st_s = []
    for l in range(DEPTH):
        lw = {'norm_ffn1': norm_ffn1[l], 'ffn1_w_in': ffn1_w_in[l], 'ffn1_w_out': ffn1_w_out[l],
              'norm_mix': norm_mix[l], 'w_in': w_in[l], 'conv_w': conv_w[l], 'conv_b': conv_b[l],
              'dt_bias': dt_bias[l], 'a_log': a_log[l], 'd_skip': d_skip[l], 'f_bias': f_bias[l],
              'ssm_norm': ssm_norm[l], 'w_br_ssm': w_br_ssm[l], 'w_br_attn': w_br_attn[l], 'w_out': w_out[l],
              'norm_ffn2': norm_ffn2[l], 'ffn2_w_in': ffn2_w_in[l], 'ffn2_w_out': ffn2_w_out[l]}
        hp, kp, vp, lfp, sp, cp = layer(hp, lw, *empty_history(bp, hp.dtype), (-hp.shape[1]) % CHUNK, 0)
        st_p.append((kp, vp, lfp, sp, cp))
        _, u_m = pre_mix(meta_h, lw)
        k_m, v_m, lf_m = split_kvf(u_m @ lw['w_in'][:, OFF_K:OFF_GS], lw['f_bias'])
        k_pre = jnp.concatenate([jnp.broadcast_to(k_m, (bs,) + k_m.shape[1:]).astype(cache_k.dtype), cache_k[l]], axis=1)
        v_pre = jnp.concatenate([jnp.broadcast_to(v_m, (bs,) + v_m.shape[1:]).astype(cache_v.dtype), cache_v[l]], axis=1)
        lf_pre = jnp.concatenate([jnp.broadcast_to(lf_m, (bs,) + lf_m.shape[1:]), cache_logf[l].astype(jnp.float32)], axis=1)
        hs, ks_, vs_, lfs, ss, cs = layer(hs, lw, state_conv[l], state_ssm[l], k_pre, v_pre, lf_pre, 0, (-hs.shape[1]) % CHUNK)
        st_s.append((ks_, vs_, lfs, ss, cs))
        if l + 1 < DEPTH:
            meta_h = layer(meta_h, lw, *empty_history(1, meta_h.dtype), (-N_META) % CHUNK, 0)[0]
    y_prompt = rmsnorm(hp[:, N_META:], norm_final)
    y_sample = rmsnorm(hs, norm_final)
    k_prompt = jnp.stack([s[0] for s in st_p])
    v_prompt = jnp.stack([s[1] for s in st_p])
    logf_prompt = jnp.stack([s[2] for s in st_p])
    ssm_prompt = jnp.stack([s[3] for s in st_p])
    conv_prompt = jnp.stack([s[4] for s in st_p])
    k_sample = jnp.stack([s[0] for s in st_s])
    v_sample = jnp.stack([s[1] for s in st_s])
    logf_sample = jnp.stack([s[2] for s in st_s])
    ssm_sample = jnp.stack([s[3] for s in st_s])
    conv_sample = jnp.stack([s[4] for s in st_s])
    return (y_prompt, y_sample, k_prompt, v_prompt, logf_prompt, ssm_prompt, conv_prompt,
            k_sample, v_sample, logf_sample, ssm_sample, conv_sample)


_drawn_inputs = setup_inputs


def setup_inputs(seed=0):
    import zlib

    import numpy as np

    out = dict(_drawn_inputs(seed))
    spreads = {}
    factors = {'cache_logf': 42.04,
     'norm_ffn1': 4.837,
     'd_skip': 200.0,
     'ssm_norm': 33.457,
     'norm_ffn2': 21.722,
     'norm_final': 21.925,
     'cache_k': 8.0,
     'cache_v': 6.876}
    for name, (base, spread) in spreads.items():
        noise = np.random.default_rng([zlib.crc32(name.encode()), seed]).standard_normal(out[name].shape)
        drawn = base * np.exp(spread * noise) if base else spread * noise
        out[name] = __import__('jax').numpy.asarray(drawn.astype(out[name].dtype))
    for name, factor in factors.items():
        out[name] = (out[name] * factor).astype(out[name].dtype)
    return out
```

```python
from contextlib import ExitStack, contextmanager

import concourse.bass as bass
from concourse import mybir

F32 = mybir.dt.float32
F32R = mybir.dt.float32r
BF16 = mybir.dt.bfloat16
ALU = mybir.AluOpType
ACT = mybir.ActivationFunctionType
AX = mybir.AxisListType

P = 128
D = 1024
SAMPLE = 64
META = 16
SEQ = 512
PROMPT = META + SEQ
TOK = SAMPLE + PROMPT
PAST = 512
KT = D // P
FF = 2816
HEADS = 16
HD = 64
SSM_HEADS = 32
GROUPS = 8
NSTATE = 128
D_SSM = 2048
D_CONV = 4096
OFF_XBC = D_SSM
OFF_DT = OFF_XBC + D_CONV
OFF_Q = OFF_DT + SSM_HEADS
OFF_K = OFF_Q + D
OFF_V = OFF_K + D
OFF_F = OFF_V + D
OFF_GS = OFF_F + HEADS
OFF_GA = OFF_GS + D
EPS = 1e-6
NEG = -1e30
SCALE = float(HD) ** -0.5

TILES = 5
ROWS = [128, 128, 128, 128, TOK - 512]
HALF = TOK // 2
BANK = 512
PC_CONVW, PC_CONVB, PC_NORM, PC_SSMN, PC_STATE, PC_END = 0, 128, 160, 192, 208, 304
NORM_FFN1, NORM_MIX, NORM_FFN2, NORM_FINAL = range(4)
CS_ = 3
CP_ = CS_ + SAMPLE + 3
CW = CP_ + PROMPT
CO = CW - 3
CHUNKS = [(0, 64), (64, 128), (128, 256), (256, 384), (384, 512), (512, TOK)]
THIRDS = [(0, 8), (8, 8), (16, 6)]


class Count:

    def __init__(self, start=0):
        self.n, self.i, self.per = start, None, 0

    def __call__(self, more=0):
        v = self.n + more
        return v if self.i is None or self.per == 0 else self.i * self.per + v

    def up(self, k=1):
        self.n += k
        return self()


@contextmanager
def looped(eng, iters, counts, pers):
    base = [c.n for c in counts]
    with eng.Fori(0, iters) as i:
        for c, p in zip(counts, pers):
            c.i, c.per = i, p
        yield i
        moved = [c.n - b for c, b in zip(counts, base)]
        assert moved == list(pers), (moved, list(pers))
    for c, b, p in zip(counts, base, pers):
        c.i, c.per, c.n = None, 0, b + p * iters


class Stream:

    def __init__(self):
        self.duo = Count()
        self.uses = [Count(), Count()]
        self.out = Count(KT)
        self.act = Count(KT)
        self.dve = Count()

    def all(self):
        return [self.duo, *self.uses, self.out, self.act, self.dve]


PRIMED = 2

MID = ["z", "x", "bc", "z", "x", "bc", "q", "k", "v"]
MID_SLOT = [1, 0, 1, 0, 1, 0, 1, 0, 1]
OUTS = {"z": TILES, "v": TILES, "x": 2, "bc": 2, "q": 2, "k": 2}
MID_OUTS = sum(OUTS[k] for k in MID)
OUT_AT = [sum(OUTS[k] for k in MID[:n]) for n in range(9)]
MID_PER = [9, 4, 5, MID_OUTS, MID_OUTS, 0]
JOBS = 4 * TILES


def mid_steps():
    def window(duos, ssd):
        pieces = [(n, t) for n in duos for t in range(OUTS[MID[n]])]
        order = []
        for at, (n, t) in enumerate(pieces):
            order += ssd.get(at, [])
            if t == 1 and n < 8:
                order.append(("split", n))
            order.append(("lin", n, t))
        return order + ssd.get(len(pieces), [])

    def ssd(g):
        return {
            0: [("prep", g), ("convA", g, 0), ("convA", g, 1)],
            1: [("convB", g, 0), ("cst", g)],
            2: [("convA", g, 2), ("convB", g, 1)],
            3: [("convA", g, 3), ("convB", g, 2)],
            4: [("convB", g, 3)],
            5: [("s1", g, 0)],
            6: [("s1", g, 1), ("s2", g, 0)],
            7: [("s1", g, 2), ("s2", g, 1)],
            8: [("s1", g, 3), ("s2", g, 2)],
            9: [("s1", g, 4), ("s2", g, 3), ("s2", g, 4), ("s3", g)],
        }
    return window([0, 1, 2], {}) + window([3, 4, 5], ssd(0)) + window([6, 7, 8], ssd(1)) + [("heads",)]


STEPS = mid_steps()


def freed(i, n, t):
    return i * MID_OUTS + (KT + 1 + OUT_AT[n] + t + 1)


def conv_in(i, g, j):
    return freed(i, 3 * g + 1 + j // 2, j % 2)


def conv_tile(i, g, j):
    return i * 4 + (2 * g + j) if j < 2 else i * 2 + (2 * KT + (j - 2) * GROUPS + g)


def score_span(t):
    before = PAST if t == 0 else t * P - SAMPLE
    return before, before + ROWS[t]


def key_blocks(t):
    return TILES if t == 0 else t + 1


def fox_ssd_hybrid_kernel(nc, x_prompt, x_sample, cache_k, cache_v, cache_logf, state_ssm, state_conv,
                          meta_tokens, norm_ffn1, ffn1_w_in, ffn1_w_out, norm_mix, w_in, conv_w, conv_b,
                          dt_bias, a_log, d_skip, f_bias, ssm_norm, w_br_ssm, w_br_attn, w_out, norm_ffn2,
                          ffn2_w_in, ffn2_w_out, norm_final,
                          y_prompt, y_sample, k_prompt, v_prompt, logf_prompt, ssm_prompt, conv_prompt,
                          k_sample, v_sample, logf_sample, ssm_sample, conv_sample):
    ctx = ExitStack()
    with ctx:
        def sb(name, shape, dt=F32, scope=ctx):
            return scope.enter_context(nc.sbuf_tensor(name, shape, dt))

        def sem(name):
            return ctx.enter_context(nc.semaphore(name))

        h_spill = nc.dram_tensor("h_spill", [P, KT * TOK], F32).ap()
        oa_spill = nc.dram_tensor("oa_spill", [KT, P, TOK], F32).ap()
        os_spill = nc.dram_tensor("os_spill", [2 * KT, P, TOK], F32).ap()
        acs_rows = nc.dram_tensor("acs_rows", [SSM_HEADS, TOK], F32).ap()
        bias0_rows = nc.dram_tensor("bias0_rows", [HEADS, 2, PAST + P], F32).ap()
        biasp_rows = nc.dram_tensor("biasp_rows", [HEADS, PROMPT], F32).ap()

        raw = sb("raw", [P, 2, KT, 256])
        wh = sb("wh", [P, 2, KT, 256], F32R)
        wl = sb("wl", [P, 2, KT, 256], F32R)
        xah = sb("xah", [P, KT, TOK], F32R)
        xal = sb("xal", [P, KT, TOK], F32R)
        ident = sb("ident", [P, P])
        ones = sb("ones", [P, P])
        identb = sb("identb", [P, P], BF16)
        negmask = sb("negmask", [P, 2, P], BF16)
        mask01 = sb("mask01", [P, 2, P])
        par = sb("par", [P, PC_END])
        parh = sb("parh", [P, PC_NORM])
        dsk = sb("dsk", [P, SSM_HEADS])
        tokt = sb("tokt", [P, TILES, P])
        scanm = sb("scanm", [48, TOK])

        ps = ctx.enter_context(nc.psum_tensor("ps", [P, 8 * BANK], F32))

        passed = sem("passed")

        def bank(b, n, rows=P, at=0):
            return ps[0:rows, b * BANK + at:b * BANK + at + n]

        def halves(b, rows=P):
            return ps[0:rows, b * BANK:(b + 2) * BANK].rearrange("p (a n) -> p a n", a=2)[:, :, 0:HALF]

        def in_halves(ap):
            return ap.rearrange("p (a n) -> p a n", a=2)

        def ffn_buffers(scope, tag):
            return {"h": sb("h" + tag, [P, KT, TOK], F32, scope),
                    "xbh": sb("xbh" + tag, [P, KT, TOK], F32R, scope),
                    "xbl": sb("xbl" + tag, [P, KT, TOK], F32R, scope),
                    "act": sb("act" + tag, [P, TOK], F32, scope),
                    "full": sb("full" + tag, [P, 2, TOK], F32, scope),
                    "rs": sb("rs" + tag, [P, TOK], F32, scope)}

        with ExitStack() as s:
            F1 = ffn_buffers(s, "1")
            xin = sb("xin", [P, TILES, 512], F32, s)
            prow = sb("prow", [P, 3, P], F32, s)
        with ExitStack() as s:
            tcol = sb("tcol", [48, 8], F32, s)
            tx = sb("tx", [48, TOK], F32, s)
            tb = sb("tb", [48, TOK], F32, s)
            tsteps = sb("tsteps", [48, TOK], F32, s)
            tsum = sb("tsum", [48, TOK], F32, s)
            tdec = sb("tdec", [32, TOK], F32, s)
            tstack = sb("tstack", [P, TOK], F32, s)
            tcm = sb("tcm", [16, SAMPLE + META], F32, s)
            tcs = sb("tcs", [16, PAST + SAMPLE + META], F32, s)
            nb0 = sb("nb0", [16, 2, PAST + P], F32, s)
            nbp = sb("nbp", [16, PROMPT], F32, s)
            clf = sb("clf", [P, 4, 16], F32, s)
            lft = sb("lft", [P, TILES, 64], F32, s)
            one16 = sb("one16", [16, PAST], F32, s)
        with ExitStack() as s:
            qT = sb("qT", [P, 2, TOK], F32, s)
            kT = sb("kT", [P, 2, TOK], F32, s)
            vt = sb("vt", [P, TILES, 256], F32, s)
            kcT = sb("kcT", [P, 2, PAST], F32, s)
            vc = sb("vc", [P, 4, 256], F32, s)
            with ExitStack() as g:
                xp = sb("xp", [P, 4, CW], F32, g)
                cvt = sb("cvt", [P, 2, CO], F32, g)
                th = sb("th", [P, CO], F32, g)
                cv = sb("cv", [P, 4, TOK], F32, g)
                brow = sb("brow", [P, 4, TOK], F32, g)
                zs = sb("zs", [P, 2, TILES, 256], F32, g)
                zt = sb("zt", [P, 2, 256], F32, g)
                zr = sb("zr", [P, 2, 256], F32, g)
                xbt = sb("xbt", [P, 2, 384], F32, g)
                xd = sb("xd", [P, 2, 256], F32, g)
                xdd = sb("xdd", [P, 2, 256], F32, g)
                xsk = sb("xsk", [P, 2, 256], F32, g)
                eb = sb("eb", [P, 4, P], F32, g)
                mb = sb("mb", [P, 2, 4, P], F32, g)
                cbm = sb("cbm", [P, P], F32, g)
                y1 = sb("y1", [P, 256], F32, g)
                y2 = sb("y2", [P, 256], F32, g)
                yg = sb("yg", [P, TILES, 256], F32, g)
                junk = sb("junk", [P, 256], F32, g)
                ssq = sb("ssq", [P, 8], F32, g)
                sini = sb("sini", [P, 256], F32, g)
                sfin = sb("sfin", [P, 256], F32, g)
                spr = sb("spr", [P, 2, 256], F32, g)
                sraw = sb("sraw", [P, 2, P], F32, g)
                sto = sb("sto", [P, 4, P], F32, g)
                dec = sb("dec", [P, 4, TILES], F32, g)
                yT = sb("yT", [P, 2, TOK], F32, g)
                cst = sb("cst", [3, 2, 512], F32, g)
            with ExitStack() as g:
                bias = sb("bias", [P, 2, PAST + P + PROMPT], F32, g)
                kcr = sb("kcr", [P, 4, 256], F32, g)
                p0 = sb("p0", [P, PAST + P], F32, g)
                pp = sb("pp", [P, 2, TOK], F32, g)
                pt = sb("pt", [P, 2, TILES * P], F32, g)
                otok = sb("otok", [P, TILES, 256], F32, g)
                ktok = sb("ktok", [P, TILES, 256], F32, g)
                oT = sb("oT", [P, 2, TOK], F32, g)
                mx = sb("mx", [P, 4], F32, g)
                rsum = sb("rsum", [P, 4], F32, g)
                rinv = sb("rinv", [P, 4], F32, g)
        with ExitStack() as s:
            G2 = ffn_buffers(s, "2")
            gates = sb("gates", [P, 2 * KT, TOK], F32, s)
            ytok = gates[:, 0:9, :].rearrange("p a b -> p (a b)")[:, 0:TILES * D].rearrange(
                "p (t c) -> p t c", t=TILES)

        x_in = [sem("x_in0"), sem("x_in1")]
        par_in, consts, par_T, par_ready = sem("par_in"), sem("consts"), sem("par_T"), sem("par_ready")
        raw_ready = [sem("raw_ready0"), sem("raw_ready1")]
        hi_ready, split_done = sem("hi_ready"), sem("split_done")
        lin_out, act_free, dve_free = sem("lin_out"), sem("act_free"), sem("dve_free")
        gated, full_ready, xhi_ready, x_ready = sem("gated"), sem("full_ready"), sem("xhi_ready"), sem("x_ready")
        sq_ready, sq_summed, rinv_ready, rs_ready = sem("sq_ready"), sem("sq_summed"), sem("rinv_ready"), sem("rs_ready")
        h_out, h_back = sem("h_out"), sem("h_back")
        dch, ach, gch = sem("dch"), sem("ach"), sem("gch")
        t_pool, t_dve, t_act, t_pe, t_in, t_out = (sem("t_" + n) for n in ("pool", "dve", "act", "pe", "in", "out"))
        heads_left, ssd_left = sem("heads_left"), sem("ssd_left")
        z_used, hist_ready = sem("z_used"), sem("hist_ready")
        tap0_ready, taps_done, tanh_ready, cv_done = sem("tap0_ready"), sem("taps_done"), sem("tanh_ready"), sem("cv_done")
        brow_in, sraw_in, sraw_T, sini_ready = sem("brow_in"), sem("sraw_in"), sem("sraw_T"), sem("sini_ready")
        dec_ready, cst_T, cst_ready, cst_out = sem("dec_ready"), sem("cst_T"), sem("cst_ready"), sem("cst_out")
        xb_T, xb_ready, cb_ready, cbm_ready = sem("xb_T"), sem("xb_ready"), sem("cb_ready"), sem("cbm_ready")
        seg_ready, e_ready, m_ready, xd_ready = sem("seg_ready"), sem("e_ready"), sem("m_ready"), sem("xd_ready")
        st_ready, s_ready, yo_ready, yd_ready = sem("st_ready"), sem("s_ready"), sem("yo_ready"), sem("yd_ready")
        y_used, yg_ready, sq_done, rv_ready = sem("y_used"), sem("yg_ready"), sem("sq_done"), sem("rv_ready")
        rt_ready, yn_ready, yT_T, yT_ready, yT_out = (sem(n) for n in ("rt_ready", "yn_ready", "yT_T", "yT_ready", "yT_out"))
        st_sample = sem("st_sample")
        sf_T, sto_ready, sto_out = sem("sf_T"), sem("sto_ready"), sem("sto_out")
        kc_in, vc_in, kc_T, kc_ready = sem("kc_in"), sem("vc_in"), sem("kc_T"), sem("kc_ready")
        ktok_T, ktok_ready, k_out, v_out = sem("ktok_T"), sem("ktok_ready"), sem("k_out"), sem("v_out")
        bias_in = [sem("bias_in0"), sem("bias_in1")]
        qk_ready, s_free, mx_ready, p_ready, p_T = (sem(n) for n in ("qk_ready", "s_free", "mx_ready", "p_ready", "p_T"))
        pt_ready, pv_ready, o_ready, pz_ready = sem("pt_ready"), sem("pv_ready"), sem("o_ready"), sem("pz_ready")
        o_T, oT_ready, oT_out = sem("o_T"), sem("oT_ready"), sem("oT_out")
        stage_in = [sem("stage_in0"), sem("stage_in1")]
        fin_T, fin_ready, y_out = sem("fin_T"), sem("fin_ready"), sem("y_out")

        def rows_of(w):
            return w[0].rearrange("(k p) n -> p k n", p=P)

        win1, wout1, winp = rows_of(ffn1_w_in), rows_of(ffn1_w_out), rows_of(w_in)
        win2, wout2 = rows_of(ffn2_w_in), rows_of(ffn2_w_out)
        wbs, wba, wo = rows_of(w_br_ssm), rows_of(w_br_attn), rows_of(w_out)

        def state_rows(s, g):
            return s[0, 0].rearrange("(g h) p n -> g (h p) n", h=4)[bass.ds(g, 1)].rearrange(
                "g (j q) n -> q (g j) n", q=P)

        def scores(t):
            before, n = score_span(t)
            return p0[:, 0:n] if t == 0 else pp[0:ROWS[t], t % 2, SAMPLE:SAMPLE + n]

        X_MIX = KT + FF // P + KT

        block = ctx.enter_context(nc.Block())

        @block.sync
        def _(sp):
            st = Stream()

            def load(slot, parts, back=1):
                sp.wait_ge(split_done, st.duo(back))
                for dst, src in parts:
                    sp.dma_start(dst, src).then_inc(raw_ready[slot], 16)
                st.duo.up()
                st.uses[slot].up()

            def r(slot, k0, k1, c0, c1):
                return raw[:, slot, k0:k1, c0:c1]

            def wide(s, w, c, back=1):
                load(s, [(r(s, 0, 4, 0, 256), w[:, 0:4, bass.ds(c, 256)]),
                         (r(s, 4, KT, 0, 256), w[:, 4:KT, bass.ds(c, 256)])], back)

            def pair(s, w, c, apart, back=1):
                load(s, [(r(s, 0, KT, 0, P), w[:, :, bass.ds(c, P)]),
                         (r(s, 0, KT, P, 256), w[:, :, bass.ds(c + apart, P)])], back)

            def ffn(win, wout, slots):
                for t0, nt in THIRDS:
                    with looped(sp, nt // 2, st.all(), [2, 1, 1, 0, 0, 0]) as i:
                        for n, s in enumerate(slots):
                            pair(s, win, i * 256 + (t0 + n) * P, FF)
                    with looped(sp, 2, st.all(), [2, 1, 1, 0, 0, 0]) as i:
                        for n, s in enumerate(slots):
                            c, m = i * 512 + n * 256, nt // 2
                            load(s, [(r(s, 0, m, 0, 256), wout[:, t0:t0 + m, bass.ds(c, 256)]),
                                     (r(s, m, nt, 0, 256), wout[:, t0 + m:t0 + nt, bass.ds(c, 256)])])

            ffn(win1, wout1, (0, 1))
            load(0, [(r(0, 0, KT, 0, SSM_HEADS), winp[:, :, OFF_DT:OFF_DT + SSM_HEADS]),
                     (r(0, 0, KT, SSM_HEADS, 48), winp[:, :, OFF_F:OFF_F + HEADS])])
            with looped(sp, 4, st.all(), MID_PER[:3] + [0, 0, 0]) as i:
                for n, kind in enumerate(MID):
                    s, g, back = MID_SLOT[n], n // 3, 2 if n == 0 else 1
                    if kind == "z":
                        wide(s, winp, i * 512 + g * 256, back)
                    elif kind == "x":
                        wide(s, winp, i * 512 + (OFF_XBC + g * 256))
                    elif kind == "bc":
                        pair(s, winp, i * 256 + (OFF_XBC + D_SSM + g * P), GROUPS * NSTATE)
                    else:
                        wide(s, winp, i * 256 + {"q": OFF_Q, "k": OFF_K, "v": OFF_V}[kind])
            first = 2
            for w, off in ((winp, OFF_GA), (winp, OFF_GS), (wba, 0), (wbs[:, 0:KT], 0), (wbs[:, KT:2 * KT], 0), (wo, 0)):
                with looped(sp, 2, st.all(), [2, 1, 1, 0, 0, 0]) as i:
                    for n, s in enumerate((1, 0)):
                        wide(s, w, i * 512 + (off + n * 256), first if n == 0 else 1)
                first = 1
            ffn(win2, wout2, (1, 0))

        @block.gpsimd
        def _(pool):
            chain = Count()

            def link(ins):
                ins.then_inc(gch, 1)
                pool.wait_ge(gch, chain.up())

            def settle():
                pool.sem_inc(passed, 1)

            pool.sem_inc(z_used, PRIMED)

            for half in range(2):
                c = slice(512 * half, 512 * half + 512)
                if half:
                    pool.wait_ge(lin_out, 4)
                for dst, src in ((xin[0:64, 0, :], x_sample[0, :, c]), (xin[64:80, 0, :], meta_tokens[:, c]),
                                 (xin[80:128, 0, :], x_prompt[0, 0:48, c]),
                                 (xin[:, 1:4, :], x_prompt[0, 48:432, c].rearrange("(t p) c -> p t c", p=P)),
                                 (xin[0:80, 4, :], x_prompt[0, 432:512, c])):
                    pool.dma_start(dst, src).then_inc(x_in[half], 16)
                if half:
                    continue
                for dst, src in (
                        (prow[:, 0, :], conv_w[0].rearrange("j (t c) -> (j t) c", c=P)),
                        (prow[0:32, 1, :], conv_b[0].rearrange("(t c) -> t c", c=P)),
                        (prow[32:40, 1, :], norm_ffn1[0].rearrange("(t c) -> t c", c=P)),
                        (prow[40:48, 1, :], norm_mix[0].rearrange("(t c) -> t c", c=P)),
                        (prow[48:56, 1, :], norm_ffn2[0].rearrange("(t c) -> t c", c=P)),
                        (prow[56:64, 1, :], norm_final.rearrange("(t c) -> t c", c=P)),
                        (prow[64:80, 1, :], ssm_norm[0].rearrange("(t c) -> t c", c=P)),
                        (prow[0:96, 2, :], state_conv[0, 0].rearrange("r (t c) -> (r t) c", c=P)),
                        (dsk[:, :], d_skip[0:1, :].to_broadcast([P, SSM_HEADS]))):
                    pool.dma_start(dst, src).then_inc(par_in, 16)
                link(pool.memset(ident[:, :], 0.0))
                link(pool.affine_select(out=ident[:, :], in_=ident[:, :], compare_op=ALU.not_equal, fill=1.0,
                                        base=0, pattern=[[-1, P]], channel_multiplier=1))
                pool.tensor_copy(identb[:, :], ident[:, :])
                pool.memset(ones[:, :], 1.0).then_inc(consts, 1)
                link(pool.memset(negmask[:, :, :], 0.0))
                link(pool.affine_select(out=negmask[:, :, :], in_=negmask[:, :, :], compare_op=ALU.is_ge,
                                        fill=NEG, base=0, pattern=[[0, 2], [-1, P]], channel_multiplier=1))
                link(pool.memset(negmask[0:64, 0, 64:80], 0.0))
                link(pool.memset(mask01[:, :, :], 1.0))
                link(pool.affine_select(out=mask01[:, :, :], in_=mask01[:, :, :], compare_op=ALU.is_ge,
                                        fill=0.0, base=0, pattern=[[0, 2], [1, P]], channel_multiplier=-1))
                link(pool.memset(mask01[0:64, 0, 64:128], 0.0))
                link(pool.memset(scanm[:, :], 1.0))
                for c0, _ in CHUNKS:
                    pool.memset(scanm[0:32, c0:c0 + 1], 0.0)
                pool.memset(scanm[32:48, 64:65], 0.0).then_inc(consts, 1)

            pool.wait_ge(x_ready, X_MIX)
            pool.dma_start(h_spill, F1["h"][:, :, :].rearrange("p k t -> p (k t)")).then_inc(h_out, 16)
            pool.wait_ge(h_out, 16)
            for dst, src in ((clf[:, :, :], cache_logf[0, 0].rearrange("(a p) h -> p a h", p=P)),
                             (tcol[0:32, 0:1], dt_bias.rearrange("o h -> h o")),
                             (tcol[32:48, 0:1], f_bias.rearrange("o h -> h o")),
                             (tcol[0:32, 1:2], a_log.rearrange("o h -> h o"))):
                pool.dma_start(dst, src).then_inc(t_in, 16)
            pool.memset(one16[:, :], 1.0)
            pool.memset(tcol[0:32, 2:3], 1.0)
            link(pool.memset(tcol[32:48, 2:3], -1.0))
            pool.memset(tcol[:, 3:4], -1.0)
            pool.memset(nb0[:, 1, 0:PAST + SAMPLE], NEG)
            pool.memset(nb0[:, 0, PAST + SAMPLE + META:], NEG).then_inc(t_pool, 1)
            pool.wait_ge(t_dve, 4)
            pool.dma_start(acs_rows, tsum[0:32, :]).then_inc(t_out, 16)
            pool.dma_start(bias0_rows, nb0[:, :, :]).then_inc(t_out, 16)
            pool.dma_start(biasp_rows, nbp[:, :]).then_inc(t_out, 16)
            pool.wait_ge(t_act, 4)
            pool.dma_start(logf_sample[0, 0], lft[0:64, 0, 32:48]).then_inc(t_out, 16)
            pool.dma_start(logf_prompt[0, 0, 0:64], lft[64:128, 0, 32:48]).then_inc(t_out, 16)
            pool.dma_start(logf_prompt[0, 0, 64:448].rearrange("(t p) h -> p t h", p=P), lft[:, 1:4, 32:48]).then_inc(t_out, 16)
            pool.dma_start(logf_prompt[0, 0, 448:528], lft[0:80, 4, 32:48]).then_inc(t_out, 16)
            pool.wait_ge(t_out, 16 * 7)
            pool.sem_inc(heads_left, 1)

            with looped(pool, 4, [chain], [2 * TILES]) as i:
                for step in STEPS:
                    kind, g = step[0], step[1] if len(step) > 1 else 0
                    if kind == "lin" and MID[g] == "z":
                        t, g = step[2], g // 3
                        m, b = ROWS[t], (g + t) % 2
                        pool.wait_ge(act_free, freed(i, step[1], t))
                        settle()
                        link(pool.tensor_scalar(zt[0:m, b, :], zt[0:m, b, :], 1.0, None, ALU.add))
                        pool.tensor_tensor(zs[0:m, g, t, :], zt[0:m, b, :], zr[0:m, b, :], ALU.mult).then_inc(z_used, 1)
                    elif kind == "lin" and MID[g] == "x" and step[2] == 0:
                        g = g // 3
                        pool.wait_ge(taps_done, i * 8 + (PRIMED + 4 * g))
                        pool.wait_ge(cst_T, i * 2 + (PRIMED + g))
                        settle()
                        hist = par[:, PC_STATE:PC_STATE + 96].rearrange("p (r t) -> p t r", r=3)
                        pool.memset(xp[:, :, CS_ + SAMPLE:CP_], 0.0)
                        pool.tensor_copy(xp[:, 0:2, 0:3], hist[:, bass.ds(i * 4 + 2 * g, 2), :])
                        pool.tensor_copy(xp[:, 2:3, 0:3], hist[:, bass.ds(i * 2 + (16 + g), 1), :])
                        pool.tensor_copy(xp[:, 3:4, 0:3], hist[:, bass.ds(i * 2 + (24 + g), 1), :]).then_inc(hist_ready, 1)
                    elif kind == "prep":
                        pool.wait_ge(seg_ready, i * 10 + (PRIMED + 5 * g))
                        pool.wait_ge(dec_ready, i * 2 + (PRIMED + g))
                        pool.wait_ge(sraw_T, i * 2 + (PRIMED + g))
                        settle()
                        pool.dma_start(brow[:, :, :], acs_rows[bass.ds(i * 8 + 4 * g, 4), :].partition_broadcast(P))\
                            .then_inc(brow_in, 16)
                        pool.dma_start(sraw[:, :, :], state_rows(state_ssm, i * 2 + g)).then_inc(sraw_in, 16)
                    elif kind == "cst":
                        pool.wait_ge(cst_ready, i * 2 + (PRIMED + g + 1))
                        settle()
                        for k, dst in enumerate((conv_sample[0, 0], conv_prompt[0, 0])):
                            for c0, n, off in ((0, 256, i * 512 + 256 * g), (256, P, i * 256 + (D_SSM + P * g)),
                                               (384, P, i * 256 + (D_SSM + D + P * g))):
                                pool.dma_start(dst[:, bass.ds(off, n)], cst[:, k, c0:c0 + n]).then_inc(cst_out, 16)
                    elif kind == "s1":
                        t = step[2]
                        m, b, hs, tau = ROWS[t], (t + g) % 2, i * 8 + 4 * g, PRIMED + 5 * g + t
                        xv = xbt[0:m, b, 0:256].rearrange("p (h c) -> p h c", h=4)
                        pool.wait_ge(xb_ready, i * 10 + (tau + 1))
                        pool.wait_ge(yd_ready, i * 10 + (tau - 1))
                        pool.wait_ge(y_used, i * 10 + (tau - 1))
                        for dst, src in ((xd, tokt[0:m, t, bass.ds(hs + 32, 4)]), (xdd, tokt[0:m, t, bass.ds(hs + 64, 4)]),
                                         (xsk, dsk[0:m, bass.ds(hs, 4)])):
                            last = pool.tensor_tensor(dst[0:m, b, :].rearrange("p (h c) -> p h c", h=4), xv,
                                                      src.unsqueeze(2).to_broadcast([m, 4, HD]), ALU.mult)
                        last.then_inc(xd_ready, 1)
                    elif kind == "s3":
                        pool.wait_ge(yT_ready, i * 4 + (PRIMED + 2 * g + 2))
                        settle()
                        pool.dma_start(os_spill[bass.ds(i * 4 + 2 * g, 2)].rearrange("j p t -> p j t"), yT[:, :, :])\
                            .then_inc(yT_out, 16)
                        pool.wait_ge(sto_ready, i * 2 + (PRIMED + g + 1))
                        settle()
                        for k, dst in enumerate((ssm_sample, ssm_prompt)):
                            pool.dma_start(state_rows(dst, i * 2 + g), sto[:, 2 * k:2 * k + 2, :]).then_inc(sto_out, 16)
                    elif kind == "heads":
                        c = i * 256

                        def cached(cache):
                            return cache[0, 0].rearrange("(a p) h d -> p a (h d)", p=P)[:, :, bass.ds(c, 256)]

                        def load_bias(hh):
                            b, hd = hh % 2, i * 4 + hh
                            for q in range(2):
                                pool.dma_start(bias[64 * q:64 * q + 64, b, 0:PAST + P],
                                               bias0_rows[bass.ds(hd, 1), q, :].to_broadcast([64, PAST + P]))\
                                    .then_inc(bias_in[b], 16)
                            pool.dma_start(bias[:, b, PAST + P:], biasp_rows[bass.ds(hd, 1), :].to_broadcast([P, PROMPT]))\
                                .then_inc(bias_in[b], 16)

                        def store_rows(to_sample, to_prompt, src, s):
                            to_s = to_sample[0, 0].rearrange("t h d -> t (h d)")[:, bass.ds(c, 256)]
                            to_p = to_prompt[0, 0].rearrange("t h d -> t (h d)")[:, bass.ds(c, 256)]
                            pool.dma_start(to_s, src[0:64, 0, :]).then_inc(s, 16)
                            pool.dma_start(to_p[0:64], src[64:128, 0, :]).then_inc(s, 16)
                            pool.dma_start(to_p[64:448].rearrange("(t p) c -> p t c", p=P), src[:, 1:4, :]).then_inc(s, 16)
                            pool.dma_start(to_p[448:528], src[0:80, 4, :]).then_inc(s, 16)

                        pool.wait_ge(yT_out, i * 32 + 32)
                        pool.wait_ge(sto_out, i * 64 + 64)
                        pool.wait_ge(cst_out, i * 192 + 192)
                        pool.sem_inc(ssd_left, 1)
                        pool.dma_start(kcr[:, :, :], cached(cache_k)).then_inc(kc_in, 16)
                        load_bias(0)
                        load_bias(1)
                        pool.memset(pp[:, :, 0:SAMPLE], 0.0).then_inc(pz_ready, 1)
                        pool.dma_start(vc[:, :, :], cached(cache_v)).then_inc(vc_in, 16)
                        pool.wait_ge(act_free, i * MID_OUTS + (KT + 1 + MID_OUTS))
                        settle()
                        store_rows(v_sample, v_prompt, vt, v_out)
                        pool.wait_ge(ktok_ready, i * TILES + TILES)
                        settle()
                        store_rows(k_sample, k_prompt, ktok, k_out)
                        for hh in (2, 3):
                            pool.wait_ge(s_free, i * JOBS + (PRIMED + 5 * (hh - 1)))
                            settle()
                            load_bias(hh)
                        pool.wait_ge(oT_ready, i * 2 + (PRIMED + 2))
                        settle()
                        pool.dma_start(oa_spill[bass.ds(i * 2, 2)].rearrange("j p t -> p j t"), oT[:, :, :]).then_inc(oT_out, 16)
                        pool.wait_ge(k_out, i * 64 + 64)
                        pool.wait_ge(v_out, i * 64 + 64)
                        pool.wait_ge(oT_out, i * 16 + 16)
                        pool.sem_inc(heads_left, 1)

            n = X_MIX
            for src, t0 in ((oa_spill, 0), (os_spill, 0), (os_spill, KT)):
                with looped(pool, 4, [], []) as i:
                    for b in range(2):
                        pool.wait_ge(x_ready, i * 2 + (n + b - 1))
                        settle()
                        pool.dma_start(G2["full"][:, b, :], src[bass.ds(i * 2 + (t0 + b), 1)].rearrange("o p t -> p (o t)"))\
                            .then_inc(stage_in[b], 16)
                n += KT
            pool.wait_ge(x_ready, n + KT)
            pool.dma_start(G2["h"][:, :, :].rearrange("p k t -> p (k t)"), h_spill).then_inc(h_back, 16)

            pool.wait_ge(fin_ready, KT)
            pool.dma_start(y_sample[0], ytok[0:64, 0, :]).then_inc(y_out, 16)
            pool.dma_start(y_prompt[0, 0:48], ytok[80:128, 0, :]).then_inc(y_out, 16)
            pool.dma_start(y_prompt[0, 48:432].rearrange("(t p) c -> p t c", p=P), ytok[:, 1:4, :]).then_inc(y_out, 16)
            pool.dma_start(y_prompt[0, 432:512], ytok[0:80, 4, :]).then_inc(y_out, 16)
            pool.wait_ge(y_out, 64)

        @block.scalar
        def _(act):
            st = Stream()
            chain, full, sq, rinvs, summed = Count(), Count(), Count(), Count(), Count()
            xhi = Count()

            for s in (sq_done, dec_ready, cst_ready, xb_ready, yT_ready, sto_ready, oT_ready):
                act.sem_inc(s, PRIMED)

            def link(ins):
                ins.then_inc(ach, 1)
                act.wait_ge(ach, chain.up())

            def split(slot, free_at):
                act.wait_ge(raw_ready[slot], split_uses(slot))
                act.wait_ge(lin_out, free_at)
                act.activation(wh[:, slot], raw[:, slot], ACT.Copy).then_inc(hi_ready, 1)

            def split_uses(slot):
                st.uses[slot].up()
                u = st.uses[slot]
                return u.n * 32 if u.i is None or u.per == 0 else u.i * (32 * u.per) + u.n * 32

            def norm(dst):
                with looped(act, KT // 2, [sq], [2]) as i:
                    for b in range(2):
                        act.wait_ge(sq_summed, sq(PRIMED - 1))
                        act.activation(G["full"][:, b, :], G["h"][:, bass.ds(i * 2 + b, 1), :].rearrange("p o t -> p (o t)"),
                                       ACT.Square).then_inc(sq_ready, 1)
                        sq.up()
                act.wait_ge(rinv_ready, rinvs.up())
                act.activation(G["rs"][:, :], G["rs"][:, :], ACT.Sqrt).then_inc(rs_ready, 1)
                if dst is None:
                    return
                with looped(act, KT // 2, [full], [2]) as i:
                    for b in range(2):
                        act.wait_ge(full_ready, full(1))
                        act.activation(dst[:, bass.ds(i * 2 + b, 1), :], G["full"][:, b:b + 1, :], ACT.Copy).then_inc(xhi_ready, 1)
                        full.up()

            def ffn(slots, last=False):
                for t0, nt in THIRDS:
                    with looped(act, nt // 2, st.all() + [full], [2, 1, 1, 4, 0, 0, 2]) as i:
                        for n, s in enumerate(slots):
                            split(1 - s, st.out())
                            st.duo.up()
                            act.wait_ge(lin_out, st.out.up(2))
                            act.wait_ge(full_ready, full())
                            act.activation(in_halves(G["act"][:, :]), halves(4 * n), ACT.Silu).then_inc(gated, 1)
                            act.wait_ge(full_ready, full(1))
                            act.activation(G["xbh"][:, bass.ds(i * 2 + n, 1), :], G["full"][:, n:n + 1, :], ACT.Copy)\
                                .then_inc(xhi_ready, 1)
                            full.up()
                    if last and t0 + nt == FF // P:
                        for s in (slots * 2)[:-1]:
                            split(1 - s, st.out())
                            st.out.up(2)
                        return
                    with looped(act, 2, st.all(), [2, 1, 1, 4, 0, 0]) as i:
                        for s in slots:
                            split(1 - s, st.out())
                            st.duo.up()
                            st.out.up(2)

            G = F1
            act.wait_ge(consts, 1)
            act.wait_ge(raw_ready[0], 32)
            st.uses[0].up()
            act.activation(wh[:, 0], raw[:, 0], ACT.Copy).then_inc(hi_ready, 1)
            act.wait_ge(par_T, 1)
            act.activation(par[:, :], bank(7, PC_END), ACT.Copy).then_inc(par_ready, 1)
            act.wait_ge(par_ready, 1)
            act.mul(parh[:, :], par[:, 0:PC_NORM], 0.5).then_inc(par_ready, 1)
            for f in range(KT):
                act.wait_ge(lin_out, f + 1)
                act.activation(G["h"][:, f, :], bank(2 * (f % 3), TOK), ACT.Copy).then_inc(act_free, 1)
            act.wait_ge(act_free, KT)
            norm(xah)
            ffn((0, 1))

            act.wait_ge(dve_free, PRIMED + 3 * KT)
            act.wait_ge(x_ready, KT + FF // P)
            norm(xah)

            split(1, st.out())
            st.duo.up()
            act.wait_ge(t_pool, 1)
            act.wait_ge(t_in, 64)
            act.wait_ge(lin_out, st.out.up())
            act.activation(in_halves(tx[:, :]), halves(0, 48), ACT.Copy).then_inc(act_free, 1)
            st.act.up()
            act.activation(tcol[0:32, 4:5], tcol[0:32, 1:2], ACT.Exp).then_inc(t_act, 1)
            act.wait_ge(t_dve, 1)
            link(act.activation(tb[:, :], tb[:, :], ACT.Exp))
            act.activation(tb[:, :], tb[:, :], ACT.Ln, bias=ones[0:48, 0:1]).then_inc(t_act, 1)
            act.wait_ge(t_dve, 2)
            act.activation(tdec[:, :], tdec[:, :], ACT.Exp)
            act.activation(tstack[96:128, :], tsum[0:32, :], ACT.Exp).then_inc(t_act, 1)
            act.wait_ge(t_pe, 2)
            tk = bank(6, TILES * P).rearrange("p (t c) -> p t c", t=TILES)
            act.activation(tokt[:, 0:4, :], tk[:, 0:4, :], ACT.Copy)
            act.activation(tokt[0:80, 4, :], tk[0:80, 4, :], ACT.Copy)
            lt = bank(4, TILES * 64).rearrange("p (t c) -> p t c", t=TILES)
            act.activation(lft[:, 0:4, 0:48], lt[:, 0:4, 0:48], ACT.Copy)
            act.activation(lft[0:80, 4, 0:48], lt[0:80, 4, 0:48], ACT.Copy).then_inc(t_act, 1)

            with looped(act, 4, st.all() + [chain], MID_PER + [0]) as i:
                for step in STEPS:
                    kind, g = step[0], step[1] if len(step) > 1 else 0
                    if kind == "split":
                        split(1 - MID_SLOT[g], st.out(-1))
                    elif kind == "lin":
                        k, t, n, g = MID[g], step[2], g, g // 3
                        b, m = 2 * ((OUT_AT[n] + t) % 2), ROWS[t]
                        act.wait_ge(lin_out, st.out.up())
                        if k == "z":
                            zb = (g + t) % 2
                            if n == 0 and t == 0:
                                act.wait_ge(heads_left, i + 1)
                            act.wait_ge(z_used, i * 10 + (PRIMED + 5 * g + t - 1))
                            act.activation(zt[0:m, zb, :], bank(b, 256, m), ACT.Tanh, scale=0.5)
                            act.activation(zr[0:m, zb, :], bank(b, 256, m), ACT.Copy).then_inc(act_free, 1)
                        elif k in ("x", "bc"):
                            j = t + (2 if k == "bc" else 0)
                            if j == 0:
                                act.wait_ge(taps_done, i * 8 + (PRIMED + 4 * g))
                                act.wait_ge(cst_T, i * 2 + (PRIMED + g))
                            act.activation(xp[:, j, CS_:CS_ + SAMPLE], bank(b, SAMPLE), ACT.Copy)
                            act.activation(xp[:, j, CP_:CP_ + HALF - SAMPLE], bank(b, HALF - SAMPLE, at=SAMPLE), ACT.Copy)
                            act.activation(xp[:, j, CP_ + HALF - SAMPLE:CW], bank(b + 1, HALF), ACT.Copy).then_inc(act_free, 1)
                        elif k == "v":
                            act.activation(vt[0:m, t, :], bank(b, 256, m), ACT.Copy).then_inc(act_free, 1)
                        else:
                            act.activation(in_halves((qT if k == "q" else kT)[:, t, :]), halves(b), ACT.Copy).then_inc(act_free, 1)
                        st.act.up()
                        if t == OUTS[k] - 1:
                            st.duo.up()
                    elif kind == "prep":
                        act.wait_ge(sraw_T, i * 2 + (PRIMED + g + 1))
                        act.wait_ge(yo_ready, i * 10 + (PRIMED + 5 * g))
                        act.wait_ge(s_ready, i * 10 + (PRIMED + 5 * g))
                        act.activation(sini[:, :], bank(6, 256), ACT.Copy).then_inc(sini_ready, 1)
                        act.wait_ge(brow_in, i * 32 + 16 * (g + 1))
                        act.activation(dec[:, :, 0], brow[:, :, SAMPLE - 1], ACT.Exp)
                        act.activation(dec[:, :, 1:4], brow[:, :, 255:512:128], ACT.Exp)
                        act.activation(dec[:, :, 4], brow[:, :, TOK - 1], ACT.Exp).then_inc(dec_ready, 1)
                    elif kind == "convA":
                        j = step[2]
                        act.wait_ge(hist_ready, i * 2 + (g + 1))
                        act.wait_ge(act_free, conv_in(i, g, j))
                        act.wait_ge(cv_done, i * 8 + (PRIMED + 4 * g + j - 1))
                        col = conv_tile(i, g, j)
                        act.activation(cvt[:, j % 2, :], xp[:, j, 0:CO], ACT.Identity, scale=parh[:, bass.ds(col, 1)],
                                       bias=parh[:, bass.ds(col + PC_CONVB, 1)]).then_inc(tap0_ready, 1)
                    elif kind == "convB":
                        j = step[2]
                        act.wait_ge(taps_done, i * 8 + (PRIMED + 4 * g + j + 1))
                        act.wait_ge(cv_done, i * 8 + (PRIMED + 4 * g + j))
                        act.activation(th[:, :], cvt[:, j % 2, :], ACT.Tanh).then_inc(tanh_ready, 1)
                    elif kind == "cst":
                        act.wait_ge(cst_T, i * 2 + (PRIMED + g + 1))
                        if g:
                            act.wait_ge(cst_out, i * 192 + 96)
                        act.activation(cst[:, :, :].rearrange("p k c -> p (k c)"), bank(6, 1024, 3), ACT.Copy).then_inc(cst_ready, 1)
                    elif kind == "s1":
                        t = step[2]
                        m, b, tau = ROWS[t], (t + g) % 2, 5 * g + t
                        act.wait_ge(xb_T, i * 10 + (tau + 1))
                        act.wait_ge(st_ready, i * 10 + (PRIMED + tau - 1))
                        act.activation(xbt[0:m, b, :], bank(4, 384, m), ACT.Copy).then_inc(xb_ready, 1)
                        act.wait_ge(seg_ready, i * 10 + (PRIMED + tau + 1))
                        act.activation(eb[0:m, :, 0:m], eb[0:m, :, 0:m], ACT.Exp).then_inc(e_ready, 1)
                    elif kind == "s2":
                        t = step[2]
                        m, tau = ROWS[t], 5 * g + t
                        act.wait_ge(yg_ready, i * 10 + (PRIMED + tau + 1))
                        act.wait_ge(sq_done, i * 10 + (PRIMED + tau))
                        act.activation(junk[0:m, :], yg[0:m, t, :], ACT.Square, accum_out=ssq[0:m, t:t + 1]).then_inc(sq_done, 1)
                    elif kind == "s3":
                        act.wait_ge(rv_ready, i * 2 + (g + 1))
                        act.activation(ssq[:, 0:4], ssq[:, 0:4], ACT.Sqrt)
                        act.activation(ssq[0:80, 4:5], ssq[0:80, 4:5], ACT.Sqrt).then_inc(rt_ready, 1)
                        for j, b in enumerate((6, 4)):
                            act.wait_ge(yT_T, i * 4 + (PRIMED + 2 * g + j + 1))
                            if j == 0 and g:
                                act.wait_ge(yT_out, i * 32 + 16)
                            act.activation(yT[:, j, :], bank(b, TOK), ACT.Copy,
                                           scale=par[:, bass.ds(i * 4 + (PC_SSMN + 2 * g + j), 1)]).then_inc(yT_ready, 1)
                        act.wait_ge(sf_T, i * 2 + (PRIMED + g + 1))
                        if g:
                            act.wait_ge(sto_out, i * 64 + 32)
                        act.activation(sto[:, :, :].rearrange("p a b -> p (a b)"), bank(6, 512), ACT.Copy).then_inc(sto_ready, 1)
                    elif kind == "heads":
                        split(MID_SLOT[0], st.out())
                        act.wait_ge(ssd_left, i + 1)
                        for t in range(TILES):
                            act.wait_ge(ktok_T, i * TILES + (t + 1))
                            act.activation(ktok[0:ROWS[t], t, :], bank(t, 256, ROWS[t]), ACT.Copy).then_inc(ktok_ready, 1)
                        for p in range(2):
                            act.wait_ge(kc_T, i * 2 + (p + 1))
                            act.activation(kcT[:, p, :], bank(6 + p, PAST), ACT.Copy).then_inc(kc_ready, 1)
                        for n in range(JOBS + 3):
                            if n < JOBS:
                                t = n % 5
                                m = ROWS[t]
                                act.wait_ge(mx_ready, i * JOBS + (n + 1))
                                if n >= 4:
                                    act.wait_ge(o_ready, i * JOBS + (n - 3))
                                act.activation(scores(t), scores(t), ACT.Exp, bias=mx[0:m, n % 4:n % 4 + 1],
                                               accum_out=rsum[0:m, n % 4:n % 4 + 1]).then_inc(p_ready, 1)
                            k = n - 2
                            if 0 <= k < JOBS:
                                t = k % 5
                                m, nb = ROWS[t], key_blocks(t)
                                act.wait_ge(p_T, i * JOBS + (k + 1))
                                if k >= 2:
                                    act.wait_ge(pv_ready, i * JOBS + (k - 1))
                                act.activation(pt[:, k % 2, :].rearrange("p (b q) -> p b q", b=TILES)[:, 0:nb, 0:m],
                                               bank(4 + 2 * (k % 2), TILES * P).rearrange("p (b q) -> p b q", b=TILES)[:, 0:nb, 0:m],
                                               ACT.Copy).then_inc(pt_ready, 1)
                        for p in range(2):
                            act.wait_ge(o_T, i * 2 + (p + 1))
                            act.activation(oT[:, p, :], bank(4 + 2 * p, TOK), ACT.Copy).then_inc(oT_ready, 1)

            G = G2
            stage = [Count(), Count()]

            def x_upper(dst, k, b):
                u = stage[b]
                u.up()
                act.wait_ge(stage_in[b], u.n * 16 if u.i is None else u.i * (16 * u.per) + u.n * 16)
                act.activation(dst[:, bass.ds(k, 1), :], G["full"][:, b:b + 1, :], ACT.Copy).then_inc(xhi_ready, 1)

            act.wait_ge(heads_left, 5)
            for part in range(2):
                with looped(act, 2, st.all() + stage, [2, 1, 1, 4, 4, 0, 1, 1]) as i:
                    for n, s in enumerate((1, 0)):
                        split(1 - s, st.out())
                        st.duo.up()
                        for u in range(2):
                            act.wait_ge(lin_out, st.out.up())
                            act.activation(in_halves(gates[:, bass.ds(i * 4 + (8 * part + 2 * n + u), 1), :]
                                                     .rearrange("p o t -> p (o t)")),
                                           halves(2 * (2 * n + u)), ACT.Tanh, scale=0.5).then_inc(act_free, 1)
                            st.act.up()
                        x_upper(G["xbh"], i * 2 + (4 * part + n), n)
            for part, dst in enumerate((xah, G["xbh"], xah, None)):
                if dst is not None:
                    act.wait_ge(lin_out, st.out())
                loads = part < 2
                with looped(act, 2, st.all() + stage, [2, 1, 1, 4, 0, 4] + [2 * loads, 2 * loads]) as i:
                    for n, s in enumerate((1, 0)):
                        split(1 - s, st.out())
                        st.duo.up()
                        for u in range(2):
                            m = i * 4 + (2 * n + u)
                            st.out.up()
                            st.dve.up()
                            if loads:
                                x_upper(dst, m, u)
                            elif dst is not None:
                                act.wait_ge(dve_free, PRIMED + 3 * KT + st.dve())
                                act.activation(dst[:, bass.ds(m, 1), :], G["h"][:, bass.ds(m, 1), :], ACT.Copy).then_inc(xhi_ready, 1)
            act.wait_ge(dve_free, PRIMED + 7 * KT)
            act.wait_ge(x_ready, X_MIX + 4 * KT)
            norm(xah)
            ffn((1, 0), last=True)
            act.wait_ge(dve_free, PRIMED + 7 * KT + 3 * KT)
            norm(None)
            for f in range(KT):
                act.wait_ge(fin_T, PRIMED + f + 1)
                pv = bank(2 * (f % 4), TILES * P).rearrange("p (t c) -> p t c", t=TILES)
                act.activation(ytok[:, 0:4, f * P:(f + 1) * P], pv[:, 0:4, :], ACT.Copy)
                act.activation(ytok[0:80, 4, f * P:(f + 1) * P], pv[0:80, 4, :], ACT.Copy).then_inc(fin_ready, 1)

        @block.vector
        def _(dve):
            st = Stream()
            chain, full, xhi, summed, nsplit = Count(), Count(), Count(), Count(PRIMED), Count()

            for s in (split_done, dve_free, taps_done, cv_done, seg_ready, cbm_ready, m_ready, s_ready, y_used, yg_ready, s_free):
                dve.sem_inc(s, PRIMED)

            def link(ins):
                ins.then_inc(dch, 1)
                dve.wait_ge(dch, chain.up())

            def split(slot):
                dve.wait_ge(hi_ready, nsplit.up())
                dve.tensor_tensor(wl[:, slot], raw[:, slot], wh[:, slot].bitcast(F32), ALU.subtract).then_inc(split_done, 1)

            def x_lower(dst, k, src, hi):
                dve.wait_ge(xhi_ready, xhi.up())
                dve.tensor_tensor(dst[:, bass.ds(k, 1), :], src, hi[:, bass.ds(k, 1), :].bitcast(F32), ALU.subtract)\
                    .then_inc(x_ready, 1)

            def norm(which, split_it=True):
                dve.wait_ge(sq_summed, summed.up(KT))
                link(dve.tensor_scalar(in_halves(G["rs"][:, :]), halves(0), 1.0 / D, EPS, ALU.mult, ALU.add))
                dve.reciprocal(G["rs"][:, :], G["rs"][:, :]).then_inc(rinv_ready, 1)
                dve.wait_ge(rs_ready, roots.up())
                with looped(dve, KT // 2, [full, xhi], [2, 2 * split_it]) as i:
                    for b in range(2):
                        k = i * 2 + b
                        if not split_it:
                            dve.wait_ge(fin_T, i * 2 + (PRIMED + b - 1))
                        dve.scalar_tensor_tensor(out=G["full"][:, b, :], in0=G["h"][:, bass.ds(k, 1), :].rearrange("p o t -> p (o t)"),
                                                 scalar=par[:, bass.ds(i * 2 + (PC_NORM + KT * which + b), 1)],
                                                 in1=G["rs"][:, :], op0=ALU.mult, op1=ALU.mult).then_inc(full_ready, 1)
                        full.up()
                        if split_it:
                            dve.wait_ge(full_ready, full())
                            x_lower(xal, k, G["full"][:, b:b + 1, :], xah)

            def add_to_h(m, b, again):
                dve.wait_ge(lin_out, st.out.up())
                if again:
                    dve.wait_ge(dve_free, st.dve(PRIMED + 1 - KT))
                hm = in_halves(G["h"][:, bass.ds(m, 1), :].rearrange("p o t -> p (o t)"))
                dve.scalar_tensor_tensor(out=hm, in0=halves(b), scalar=0.5, in1=hm, op0=ALU.mult, op1=ALU.add)\
                    .then_inc(dve_free, 1)
                st.dve.up()

            def ffn(slots, last=False):
                for t0, nt in THIRDS:
                    with looped(dve, nt // 2, st.all() + [full, xhi, nsplit, hid], [2, 1, 1, 4, 0, 0, 2, 2, 2, 2]) as i:
                        for n, s in enumerate(slots):
                            split(1 - s)
                            st.duo.up()
                            st.uses[s].up()
                            st.out.up(2)
                            dve.wait_ge(gated, hid.up())
                            dve.tensor_tensor(in_halves(G["full"][:, n, :]), in_halves(G["act"][:, :]), halves(4 * n + 2), ALU.mult)\
                                .then_inc(full_ready, 1)
                            full.up()
                            dve.wait_ge(full_ready, full())
                            x_lower(G["xbl"], i * 2 + n, G["full"][:, n:n + 1, :], G["xbh"])
                    if last and t0 + nt == FF // P:
                        for n, s in enumerate(slots * 2):
                            if n < 3:
                                split(1 - s)
                            for u in range(2):
                                add_to_h(2 * n + u, 2 * ((2 * n + u) % 4), True)
                        return
                    with looped(dve, 2, st.all() + [nsplit], [2, 1, 1, 4, 0, 4, 2]) as i:
                        for n, s in enumerate(slots):
                            split(1 - s)
                            st.duo.up()
                            st.uses[s].up()
                            for u in range(2):
                                add_to_h(i * 4 + (2 * n + u), 2 * (2 * n + u), t0 > 0)

            roots, hid = Count(), Count()
            dve.wait_ge(consts, 2)

            G = F1
            split(0)
            norm(NORM_FFN1)
            ffn((0, 1))
            dve.wait_ge(dve_free, PRIMED + 3 * KT)
            norm(NORM_MIX)

            split(1)
            st.duo.up()
            st.out.up()
            dve.wait_ge(act_free, KT + 1)
            link(dve.tensor_scalar(tx[:, :], tx[:, :], tcol[:, 0:1], tcol[:, 2:3], ALU.add, ALU.mult))
            dve.scalar_tensor_tensor(out=tb[:, :], in0=tx[:, :], scalar=-1.0, in1=tx[:, :], op0=ALU.mult, op1=ALU.min)\
                .then_inc(t_dve, 1)
            dve.wait_ge(t_act, 2)
            dve.tensor_scalar(tcol[0:32, 3:4], tcol[0:32, 4:5], -1.0, None, ALU.mult)
            link(dve.scalar_tensor_tensor(out=tx[:, :], in0=tx[:, :], scalar=0.0, in1=tb[:, :], op0=ALU.max, op1=ALU.add))
            link(dve.tensor_scalar(tsteps[:, :], tx[:, :], tcol[:, 3:4], None, ALU.mult))
            link(dve.tensor_tensor_scan(tsum[:, :], scanm[:, :], tsteps[:, :], 0.0, ALU.mult, ALU.add))
            for n, (c0, c1) in enumerate(CHUNKS):
                last = dve.tensor_scalar(tdec[:, c0:c1], tsum[0:32, c0:c1], -1.0, tsum[0:32, c1 - 1:c1], ALU.mult, ALU.add)
            last.then_inc(t_dve, 1)
            dve.tensor_copy(tstack[0:32, :], tsum[0:32, :])
            dve.tensor_copy(tstack[32:64, :], tx[0:32, :])
            dve.wait_ge(t_act, 3)
            dve.memset(tstack[96:128, SAMPLE:P], 0.0)
            dve.tensor_tensor(tstack[64:96, :], tdec[:, :], tx[0:32, :], ALU.mult).then_inc(t_dve, 1)
            link(dve.tensor_copy(tcm[:, :], tsum[32:48, 0:SAMPLE + META]))
            dve.wait_ge(t_pe, 1)
            link(dve.tensor_tensor_scan(tcs[:, 0:PAST], one16[:, :], bank(5, PAST, 16), tcm[:, SAMPLE + META - 1:SAMPLE + META],
                                        ALU.mult, ALU.add))
            dve.tensor_scalar(tcs[:, PAST:PAST + SAMPLE], tcm[:, 0:SAMPLE], tcs[:, PAST - 1:PAST], None, ALU.add)
            link(dve.tensor_copy(tcs[:, PAST + SAMPLE:], tcm[:, SAMPLE:]))
            dve.tensor_scalar(nb0[:, 0, 0:PAST + SAMPLE + META], tcs[:, :], -1.0, None, ALU.mult)
            dve.tensor_scalar(nb0[:, 1, PAST + SAMPLE:], tsum[32:48, SAMPLE:P], -1.0, None, ALU.mult)
            dve.tensor_scalar(nbp[:, :], tsum[32:48, SAMPLE:], -1.0, None, ALU.mult).then_inc(t_dve, 1)

            def heads4(ap, m):
                return ap.unsqueeze(2).to_broadcast([m, 4, HD])

            def by_head(ap):
                return ap.rearrange("p (h c) -> p h c", h=4)

            with looped(dve, 4, [chain, nsplit], [48, 9]) as i:
                for step in STEPS:
                    kind, g = step[0], step[1] if len(step) > 1 else 0
                    if kind == "split":
                        split(1 - MID_SLOT[g])
                    elif kind == "convA":
                        j = step[2]
                        dve.wait_ge(tap0_ready, i * 8 + (4 * g + j + 1))
                        c = cvt[:, j % 2, :]
                        for tap in range(1, 4):
                            ins = dve.scalar_tensor_tensor(out=c, in0=xp[:, j, tap:tap + CO],
                                                           scalar=parh[:, bass.ds(conv_tile(i, g, j) + 32 * tap, 1)],
                                                           in1=c, op0=ALU.mult, op1=ALU.add)
                            if tap < 3:
                                link(ins)
                        ins.then_inc(taps_done, 1)
                    elif kind == "convB":
                        j = step[2]
                        dve.wait_ge(tanh_ready, i * 8 + (4 * g + j + 1))
                        if j == 0:
                            dve.wait_ge(yd_ready, i * 10 + (PRIMED + 5 * g))
                        for c0, c1, to in ((0, SAMPLE, 0), (CP_ - CS_, CO, SAMPLE)):
                            ins = dve.scalar_tensor_tensor(out=cv[:, j, to:to + c1 - c0], in0=th[:, c0:c1], scalar=1.0,
                                                           in1=cvt[:, j % 2, c0:c1], op0=ALU.add, op1=ALU.mult)
                        ins.then_inc(cv_done, 1)
                    elif kind == "s1":
                        t = step[2]
                        m, tau, c = ROWS[t], 5 * g + t, t * P
                        if t == 0:
                            dve.wait_ge(brow_in, i * 32 + 16 * (g + 1))
                        dve.wait_ge(m_ready, i * 10 + (PRIMED + tau))
                        for r in range(4):
                            ins = dve.tensor_scalar(eb[0:m, r, 0:m], brow[0:m, r, c:c + m],
                                                    tokt[0:m, t, bass.ds(i * 8 + (4 * g + r), 1)], 0.0, ALU.subtract, ALU.min)
                        ins.then_inc(seg_ready, 1)
                        dve.wait_ge(cb_ready, i * 10 + (tau + 1))
                        dve.tensor_tensor(cbm[0:m, 0:m], bank(5, m, m), mask01[0:m, min(t, 1), 0:m], ALU.mult).then_inc(cbm_ready, 1)
                        dve.wait_ge(cbm_ready, i * 10 + (PRIMED + tau + 1))
                        dve.wait_ge(e_ready, i * 10 + (tau + 1))
                        dve.wait_ge(yd_ready, i * 10 + (PRIMED + tau - 1))
                        dve.tensor_tensor(mb[0:m, tau % 2, :, 0:m], eb[0:m, :, 0:m],
                                          cbm[0:m, 0:m].unsqueeze(1).to_broadcast([m, 4, m]), ALU.mult).then_inc(m_ready, 1)
                    elif kind == "s2":
                        t = step[2]
                        m, tau = ROWS[t], 5 * g + t
                        dve.wait_ge(st_ready, i * 10 + (PRIMED + tau + 1))
                        if t == 0:
                            dve.wait_ge(dec_ready, i * 2 + (PRIMED + g + 1))
                            dve.wait_ge(sini_ready, i * 2 + (g + 1))
                            dve.wait_ge(sf_T, i * 2 + (g + PRIMED))
                            for r in range(4):
                                h = slice(HD * r, HD * r + HD)
                                dve.scalar_tensor_tensor(out=sfin[:, h], in0=sini[:, h], scalar=dec[:, r, 0:1],
                                                         in1=bank(7, HD, at=HD * r), op0=ALU.mult, op1=ALU.add)
                            dve.tensor_copy(spr[:, 0, :], bank(7, 256, at=256)).then_inc(s_ready, 1)
                        else:
                            dve.wait_ge(s_ready, i * 10 + (PRIMED + tau))
                            for r in range(4):
                                h = slice(HD * r, HD * r + HD)
                                ins = dve.scalar_tensor_tensor(out=spr[:, t % 2, h], in0=spr[:, (t - 1) % 2, h],
                                                               scalar=dec[:, r, t:t + 1], in1=bank(7, HD, at=HD * r),
                                                               op0=ALU.mult, op1=ALU.add)
                            ins.then_inc(s_ready, 1)
                        dve.wait_ge(yd_ready, i * 10 + (PRIMED + tau + 1))
                        dve.wait_ge(yg_ready, i * 10 + (PRIMED + tau))
                        dve.tensor_tensor(by_head(y1[0:m, :]), by_head(bank(6, 256, m)),
                                          heads4(tokt[0:m, t, bass.ds(i * 8 + (96 + 4 * g), 4)], m), ALU.mult)
                        dve.wait_ge(xd_ready, i * 10 + (tau + 1))
                        dve.tensor_tensor(y2[0:m, :], bank(6, 256, m, at=256), xsk[0:m, tau % 2, :], ALU.add).then_inc(y_used, 1)
                        dve.wait_ge(y_used, i * 10 + (PRIMED + tau + 1))
                        link(dve.tensor_tensor(y1[0:m, :], y1[0:m, :], y2[0:m, :], ALU.add))
                        if t == 0:
                            dve.wait_ge(z_used, i * 10 + (PRIMED + 5 * g + 5))
                            dve.wait_ge(yT_T, i * 4 + (PRIMED + 2 * g))
                        dve.scalar_tensor_tensor(out=yg[0:m, t, :], in0=y1[0:m, :], scalar=0.5, in1=zs[0:m, g, t, :],
                                                 op0=ALU.mult, op1=ALU.mult).then_inc(yg_ready, 1)
                    elif kind == "s3":
                        dve.wait_ge(sq_done, i * 10 + (PRIMED + 5 * g + 5))
                        parts = (ssq[:, 0:4], ssq[0:80, 4:5])
                        for a in parts:
                            ins = dve.tensor_scalar(a, a, 1.0 / 256, EPS, ALU.mult, ALU.add)
                        link(ins)
                        for a in parts:
                            ins = dve.reciprocal(a, a)
                        ins.then_inc(rv_ready, 1)
                        dve.wait_ge(rt_ready, i * 2 + (g + 1))
                        for t in range(TILES):
                            a = yg[0:ROWS[t], t, :]
                            ins = dve.tensor_scalar(a, a, ssq[0:ROWS[t], t:t + 1], None, ALU.mult)
                        ins.then_inc(yn_ready, 1)
                    elif kind == "heads":
                        split(MID_SLOT[0])
                        dve.wait_ge(ssd_left, i + 1)
                        for n in range(JOBS + 3):
                            if n < JOBS:
                                hh, t = n // 5, n % 5
                                m, (before, w) = ROWS[t], score_span(t)
                                dve.wait_ge(bias_in[hh % 2], i * 96 + 48 * (hh // 2 + 1))
                                dve.wait_ge(qk_ready, i * JOBS + (n + 1))
                                if n >= 2:
                                    dve.wait_ge(p_T, i * JOBS + (n - 1))
                                bs = bias[0:m, hh % 2, 0:PAST + P] if t == 0 else bias[0:m, hh % 2, PAST + P:PAST + P + w]
                                sp_ = bank(2 * (n % 2), w, m, at=BANK - before)
                                dve.scalar_tensor_tensor(out=scores(t), in0=sp_, scalar=SCALE, in1=bs, op0=ALU.mult, op1=ALU.add)\
                                    .then_inc(s_free, 1)
                                dve.wait_ge(s_free, i * JOBS + (PRIMED + n + 1))
                                dve.tensor_reduce(mx[0:m, n % 4:n % 4 + 1], scores(t), AX.X, ALU.max, negate=True).then_inc(mx_ready, 1)
                            k = n - 3
                            if k >= 0:
                                hh, t = k // 5, k % 5
                                m = ROWS[t]
                                dve.wait_ge(pv_ready, i * JOBS + (k + 1))
                                link(dve.reciprocal(rinv[0:m, k % 4:k % 4 + 1], rsum[0:m, k % 4:k % 4 + 1]))
                                dve.tensor_scalar(otok[0:m, t, HD * hh:HD * hh + HD], bank(5 + 2 * (k % 2), HD, m, at=256),
                                                  rinv[0:m, k % 4:k % 4 + 1], None, ALU.mult).then_inc(o_ready, 1)
            st.out.up(4 * MID_OUTS)

            G = G2
            for part in range(2):
                with looped(dve, 2, [nsplit, xhi, st.out], [2, 2, 4]) as i:
                    for n, s in enumerate((1, 0)):
                        split(1 - s)
                        st.out.up(2)
                        x_lower(G["xbl"], i * 2 + (4 * part + n), G["full"][:, n:n + 1, :], G["xbh"])
            dve.wait_ge(act_free, KT + 1 + 4 * MID_OUTS + 2 * KT)
            for part, (hi, lo) in enumerate(((xah, xal), (G["xbh"], G["xbl"]), (xah, xal), (None, None))):
                if part == 3:
                    dve.wait_ge(h_back, 16)
                with looped(dve, 2, [nsplit, xhi, st.out, st.dve, chain], [2, 4 * (part < 3), 4, 4, 4 * (part in (1, 2))]) as i:
                    for n, s in enumerate((1, 0)):
                        split(1 - s)
                        for u in range(2):
                            m, b = i * 4 + (2 * n + u), 2 * (2 * n + u)
                            if part == 3:
                                add_to_h(m, b, False)
                                continue
                            dve.wait_ge(lin_out, st.out.up())
                            hm = in_halves(G["h"][:, bass.ds(m, 1), :].rearrange("p o t -> p (o t)"))
                            gt = in_halves(gates[:, bass.ds(m + 8 * (part > 0), 1), :].rearrange("p o t -> p (o t)"))
                            to = hm if part == 0 else in_halves(G["act"][:, :])
                            if part:
                                dve.wait_ge(dve_free, st.dve(PRIMED))
                            ins = dve.scalar_tensor_tensor(out=to, in0=gt, scalar=1.0, in1=halves(b), op0=ALU.add, op1=ALU.mult)
                            if part:
                                link(ins)
                                ins = dve.tensor_tensor(hm, hm, to, ALU.add)
                            ins.then_inc(dve_free, 1)
                            st.dve.up()
                            if part == 2:
                                dve.wait_ge(dve_free, st.dve(PRIMED))
                            src = G["h"][:, bass.ds(m, 1), :] if part == 2 else G["full"][:, u:u + 1, :]
                            x_lower(lo, m, src, hi)

            dve.wait_ge(dve_free, PRIMED + 7 * KT)
            norm(NORM_FFN2)
            ffn((1, 0), last=True)
            dve.wait_ge(dve_free, PRIMED + 7 * KT + 3 * KT)
            norm(NORM_FINAL, split_it=False)

        @block.tensor
        def _(pe):
            st = Stream()
            nsq, xr, full = Count(), Count(), Count()

            for s in (sq_summed, cst_T, sraw_T, st_ready, yo_ready, yd_ready, yT_T, sf_T, fin_T):
                pe.sem_inc(s, PRIMED)

            def duo_split():
                pe.wait_ge(split_done, st.duo(PRIMED + 1))
                st.duo.up()

            def unit(slot, j, xh, xl, nk, b, before_last=None):
                for k in range(nk):
                    if before_last is not None and k == nk - 1:
                        before_last()
                    for w, x in ((wh, xh), (wh, xl), (wl, xh)):
                        for a in range(2):
                            ins = pe.matmul(bank(b + a, HALF), w[:, slot, k, j * P:(j + 1) * P], x[:, k, a * HALF:(a + 1) * HALF],
                                            start=(k == 0 and w is wh and x is xh), stop=(k == nk - 1 and w is wl))
                ins.then_inc(lin_out, 1)
                st.out.up()

            def token_tile(slot, t, b):
                m = ROWS[t]
                for k in range(KT):
                    for w, x in ((wh, xah), (wh, xal), (wl, xah)):
                        ins = pe.matmul(bank(b, 256, m), x[:, k, t * P:t * P + m], w[:, slot, k, :],
                                        start=(k == 0 and w is wh and x is xah), stop=(k == KT - 1 and w is wl))
                ins.then_inc(lin_out, 1)
                st.out.up()

            def norm():
                def square(b, first=False, last=False):
                    pe.wait_ge(sq_ready, nsq.up())
                    for a in range(2):
                        ins = pe.matmul(bank(a, HALF), ones[:, :], G["full"][:, b, a * HALF:(a + 1) * HALF],
                                        start=first, stop=last)
                    ins.then_inc(sq_summed, 1)

                square(0, first=True)
                square(1)
                with looped(pe, KT // 2 - 2, [nsq], [2]) as i:
                    for b in range(2):
                        square(b)
                square(0)
                square(1, last=True)

            def ffn(slots, last=False):
                for t0, nt in THIRDS:
                    with looped(pe, nt // 2, st.all() + [full], [2, 0, 0, 4, 0, 0, 2]) as i:
                        for n, s in enumerate(slots):
                            duo_split()
                            pe.wait_ge(full_ready, full(-1))
                            pe.wait_ge(dve_free, st.dve(PRIMED - 2 * (n == 0)))
                            unit(s, 0, xah, xal, KT, 4 * n)
                            unit(s, 1, xah, xal, KT, 4 * n + 2)
                            full.up()
                    xr.up(nt)
                    with looped(pe, 2, st.all(), [2, 0, 0, 4, 0, 4]) as i:
                        for n, s in enumerate(slots):
                            duo_split()
                            for u in range(2):
                                pe.wait_ge(x_ready, xr() - 1)
                                pe.wait_ge(dve_free, st.dve(PRIMED - 1))
                                unit(s, u, G["xbh"], G["xbl"], nt, 2 * (2 * n + u),
                                     before_last=lambda: pe.wait_ge(x_ready, xr()))
                                st.dve.up()

            def turn(out, in_):
                k = in_.shape[0]
                return pe.transpose(out, in_, ident[0:k, 0:k])

            G = F1
            pe.wait_ge(consts, 2)
            pe.wait_ge(par_in, 16 * 9)
            turn(bank(7, P), prow[:, 0, :])
            turn(bank(7, 80, at=P), prow[0:80, 1, :])
            turn(bank(7, 96, at=208), prow[0:96, 2, :]).then_inc(par_T, 1)
            for f in range(KT):
                if f % 4 == 0:
                    pe.wait_ge(x_in[f // 4], 16 * 5)
                if f >= 3:
                    pe.wait_ge(act_free, f - 2)
                for t in range(TILES):
                    ins = turn(bank(2 * (f % 3), ROWS[t], at=t * P), xin[0:ROWS[t], t, (f % 4) * P:(f % 4 + 1) * P])
                ins.then_inc(lin_out, 1)
            norm()
            full.up(KT)
            xr.up(KT)
            pe.wait_ge(x_ready, xr())
            ffn((0, 1))
            norm()
            full.up(KT)
            xr.up(KT)
            pe.wait_ge(x_ready, xr())

            duo_split()
            unit(0, 0, xah, xal, KT, 0)
            pe.wait_ge(t_in, 16 * 4)
            for a in range(4):
                ins = turn(bank(5, P, 16, at=a * P), clf[:, a, :])
            ins.then_inc(t_pe, 1)
            pe.wait_ge(t_dve, 3)
            pe.wait_ge(t_act, 3)
            for t in range(TILES):
                m = ROWS[t]
                turn(bank(6, P, m, at=t * P), tstack[:, t * P:t * P + m])
                ins = turn(bank(4, 48, m, at=64 * t), tsteps[:, t * P:t * P + m])
            ins.then_inc(t_pe, 1)
            st.act.up()

            with looped(pe, 4, st.all(), [9, 0, 0, MID_OUTS, MID_OUTS, 0]) as i:
                for step in STEPS:
                    kind, g = step[0], step[1] if len(step) > 1 else 0
                    if kind == "lin":
                        n, t = step[1], step[2]
                        k, b = MID[n], 2 * ((OUT_AT[n] + t) % 2)
                        if t == 0:
                            duo_split()
                        if n == 0 and t == 0:
                            pe.wait_ge(s_free, i * JOBS + PRIMED)
                            pe.wait_ge(act_free, st.act())
                            pe.wait_ge(t_act, 4)
                        else:
                            pe.wait_ge(act_free, st.act(-1))
                        st.act.up()
                        if k in ("z", "v"):
                            token_tile(MID_SLOT[n], t, b)
                        else:
                            unit(MID_SLOT[n], t, xah, xal, KT, b)
                    elif kind == "prep":
                        pe.wait_ge(oT_ready, i * 2 + PRIMED)
                        pe.wait_ge(sto_ready, i * 2 + (PRIMED + g))
                        pe.wait_ge(sraw_in, i * 32 + 16 * (g + 1))
                        turn(bank(6, P), sraw[:, 0, :])
                        turn(bank(6, P, at=P), sraw[:, 1, :]).then_inc(sraw_T, 1)
                    elif kind == "cst":
                        pe.wait_ge(act_free, conv_in(i, g, 3))
                        pe.wait_ge(sini_ready, i * 2 + (g + 1))
                        for j in range(4):
                            turn(bank(6, P, 3, at=j * P), xp[:, j, CS_ + SAMPLE - 3:CS_ + SAMPLE])
                            ins = turn(bank(7, P, 3, at=j * P), xp[:, j, CW - 3:CW])
                        ins.then_inc(cst_T, 1)
                    elif kind == "s1":
                        t = step[2]
                        m, tau, c = ROWS[t], 5 * g + t, slice(t * P, t * P + ROWS[t])
                        if t == 0:
                            pe.wait_ge(cv_done, i * 8 + (PRIMED + 4 * g + 4))
                            pe.wait_ge(cst_ready, i * 2 + (PRIMED + g + 1))
                        pe.wait_ge(xb_ready, i * 10 + (PRIMED + tau))
                        for j in range(3):
                            ins = turn(bank(4, P, m, at=j * P), cv[:, j, c])
                        ins.then_inc(xb_T, 1)
                        pe.wait_ge(cbm_ready, i * 10 + (PRIMED + tau))
                        pe.matmul(bank(5, m, m), cv[:, 2, c], cv[:, 3, c], start=True, stop=True).then_inc(cb_ready, 1)
                    elif kind == "s2":
                        t = step[2]
                        m, tau, c = ROWS[t], 5 * g + t, slice(t * P, t * P + ROWS[t])
                        b = tau % 2
                        if t:
                            pe.wait_ge(s_ready, i * 10 + (PRIMED + tau))
                        pe.wait_ge(y_used, i * 10 + (PRIMED + tau))
                        pe.matmul(bank(6, 256, m), cv[:, 3, c], spr[:, (t - 1) % 2, :] if t else sini[:, :],
                                  start=True, stop=True).then_inc(yo_ready, 1)
                        pe.wait_ge(xd_ready, i * 10 + (tau + 1))
                        pe.wait_ge(xb_ready, i * 10 + (PRIMED + tau + 1))
                        pe.wait_ge(s_ready, i * 10 + (PRIMED + tau))
                        if t == 0:
                            pe.matmul(bank(7, 256), xbt[0:64, b, 256:384], xdd[0:64, b, :], start=True, stop=True)\
                                .then_inc(st_sample, 1)
                            pe.wait_ge(st_sample, i * 2 + (g + 1))
                            pe.matmul(bank(7, 256, at=256), xbt[64:128, b, 256:384], xdd[64:128, b, :], start=True, stop=True)\
                                .then_inc(st_ready, 1)
                        else:
                            pe.matmul(bank(7, 256), xbt[0:m, b, 256:384], xdd[0:m, b, :], start=True, stop=True)\
                                .then_inc(st_ready, 1)
                        pe.wait_ge(m_ready, i * 10 + (PRIMED + tau + 1))
                        for r in range(4):
                            ins = pe.matmul(bank(6, HD, m, at=256 + HD * r), mb[0:m, b, r, 0:m], xd[0:m, b, HD * r:HD * r + HD],
                                            start=True, stop=True)
                        ins.then_inc(yd_ready, 1)
                    elif kind == "s3":
                        pe.wait_ge(yn_ready, i * 2 + (g + 1))
                        pe.wait_ge(y_used, i * 10 + (PRIMED + 5 * g + 5))
                        pe.wait_ge(s_ready, i * 10 + (PRIMED + 5 * g + 5))
                        for j, b in enumerate((6, 4)):
                            for t in range(TILES):
                                ins = turn(bank(b, ROWS[t], at=t * P), yg[0:ROWS[t], t, j * P:(j + 1) * P])
                            ins.then_inc(yT_T, 1)
                        pe.wait_ge(yT_ready, i * 4 + (PRIMED + 2 * g + 1))
                        for k, s in enumerate((sfin[:, :], spr[:, 0, :])):
                            for j in range(2):
                                ins = turn(bank(6, P, at=256 * k + j * P), s[:, j * P:(j + 1) * P])
                        ins.then_inc(sf_T, 1)
                    elif kind == "heads":
                        pe.wait_ge(act_free, st.act())
                        pe.wait_ge(sto_ready, i * 2 + (PRIMED + 2))
                        pe.wait_ge(yT_ready, i * 4 + (PRIMED + 4))
                        for t in range(TILES):
                            m = ROWS[t]
                            for p in range(2):
                                ins = turn(bank(t, P, m, at=p * P), kT[:, p, t * P:t * P + m])
                            ins.then_inc(ktok_T, 1)
                        pe.wait_ge(kc_in, i * 16 + 16)
                        for p in range(2):
                            for a in range(4):
                                ins = turn(bank(6 + p, P, at=a * P), kcr[:, a, p * P:(p + 1) * P])
                            ins.then_inc(kc_T, 1)
                        for n in range(JOBS + 3):
                            if n < JOBS:
                                hh, t = n // 5, n % 5
                                p, r = hh // 2, slice(HD * (hh % 2), HD * (hh % 2) + HD)
                                m, (before, w) = ROWS[t], score_span(t)
                                if n == 0:
                                    pe.wait_ge(ktok_ready, i * TILES + TILES)
                                    pe.wait_ge(kc_ready, i * 2 + 2)
                                if n >= 2:
                                    pe.wait_ge(s_free, i * JOBS + (PRIMED + n - 1))
                                q = qT[r, p, t * P:t * P + m]
                                b = 2 * (n % 2)
                                pe.matmul(bank(b, before, m, at=BANK - before), q, kcT[r, p, :] if t == 0 else kT[r, p, SAMPLE:t * P],
                                          start=True, stop=True)
                                pe.matmul(bank(b + 1, m, m), q, kT[r, p, t * P:t * P + m], start=True, stop=False)
                                pe.matmul(bank(b + 1, m, m), identb[0:m, 0:m], negmask[0:m, min(t, 1), 0:m],
                                          start=False, stop=True).then_inc(qk_ready, 1)
                            k = n - 2
                            if 0 <= k < JOBS:
                                t = k % 5
                                m = ROWS[t]
                                pe.wait_ge(p_ready, i * JOBS + (k + 1))
                                if k == 1:
                                    pe.wait_ge(pz_ready, i + 1)
                                if k >= 2:
                                    pe.wait_ge(pt_ready, i * JOBS + (k - 1))
                                    pe.wait_ge(o_ready, i * JOBS + (k - 1))
                                for b in range(key_blocks(t)):
                                    kw = P if b < 4 or t == 0 else ROWS[4]
                                    src = p0[:, b * P:b * P + P] if t == 0 else pp[0:m, t % 2, b * P:b * P + kw]
                                    ins = turn(bank(4 + 2 * (k % 2), m, kw, at=b * P), src)
                                ins.then_inc(p_T, 1)
                            k = n - 3
                            if k >= 0:
                                hh, t = k // 5, k % 5
                                m, nb = ROWS[t], key_blocks(t)
                                pe.wait_ge(pt_ready, i * JOBS + (k + 1))
                                if k == 0:
                                    pe.wait_ge(vc_in, i * 16 + 16)
                                for b in range(nb):
                                    c = slice(HD * hh, HD * hh + HD)
                                    if t == 0:
                                        kw, v = P, vc[:, b, c] if b < 4 else vt[:, 0, c]
                                    else:
                                        kw = P if b < 4 else ROWS[4]
                                        v = vt[0:kw, b, c]
                                    ins = pe.matmul(bank(5 + 2 * (k % 2), HD, m, at=256), pt[0:kw, k % 2, b * P:b * P + m], v,
                                                    start=(b == 0), stop=(b == nb - 1))
                                ins.then_inc(pv_ready, 1)
                        pe.wait_ge(o_ready, i * JOBS + JOBS)
                        for p in range(2):
                            for t in range(TILES):
                                ins = turn(bank(4 + 2 * p, ROWS[t], at=t * P), otok[0:ROWS[t], t, p * P:(p + 1) * P])
                            ins.then_inc(o_T, 1)

            G = G2
            pe.wait_ge(oT_ready, PRIMED + 8)
            pe.wait_ge(s_free, PRIMED + 4 * JOBS)
            for part in range(2):
                with looped(pe, 2, st.all(), [2, 0, 0, 4, 4, 0]) as i:
                    for n, s in enumerate((1, 0)):
                        duo_split()
                        for u in range(2):
                            pe.wait_ge(act_free, st.act(-1))
                            unit(s, u, xah, xal, KT, 2 * (2 * n + u))
                            st.act.up()
            pe.wait_ge(act_free, st.act())
            for xh, xl in ((G["xbh"], G["xbl"]), (xah, xal), (G["xbh"], G["xbl"]), (xah, xal)):
                xr.up(KT)
                pe.wait_ge(x_ready, xr())
                with looped(pe, 2, st.all(), [2, 0, 0, 4, 0, 4]) as i:
                    for n, s in enumerate((1, 0)):
                        duo_split()
                        for u in range(2):
                            pe.wait_ge(dve_free, st.dve(PRIMED - 1))
                            unit(s, u, xh, xl, KT, 2 * (2 * n + u))
                            st.dve.up()
            norm()
            full.up(KT)
            xr.up(KT)
            pe.wait_ge(x_ready, xr())
            ffn((1, 0))
            norm()
            for f in range(KT):
                pe.wait_ge(full_ready, full.up())
                if f >= 4:
                    pe.wait_ge(fin_ready, f - 3)
                for t in range(TILES):
                    ins = turn(bank(2 * (f % 4), P, ROWS[t], at=t * P), G["full"][:, f % 2, t * P:t * P + ROWS[t]])
                ins.then_inc(fin_T, 1)


_INS = ["x_prompt", "x_sample", "cache_k", "cache_v", "cache_logf", "state_ssm", "state_conv", "meta_tokens",
        "norm_ffn1", "ffn1_w_in", "ffn1_w_out", "norm_mix", "w_in", "conv_w", "conv_b", "dt_bias", "a_log", "d_skip",
        "f_bias", "ssm_norm", "w_br_ssm", "w_br_attn", "w_out", "norm_ffn2", "ffn2_w_in", "ffn2_w_out", "norm_final"]
_OUTS = [(1, SEQ, D), (1, SAMPLE, D), (1, 1, PROMPT, HEADS, HD), (1, 1, PROMPT, HEADS, HD), (1, 1, PROMPT, HEADS),
         (1, 1, SSM_HEADS, HD, NSTATE), (1, 1, 3, D_CONV), (1, 1, SAMPLE, HEADS, HD), (1, 1, SAMPLE, HEADS, HD),
         (1, 1, SAMPLE, HEADS), (1, 1, SSM_HEADS, HD, NSTATE), (1, 1, 3, D_CONV)]


def kernel(**inputs):
    import numpy as _np
    import concourse.bacc as _bacc
    from concourse import mybir as _mybir
    from concourse.bass_utils import run_bass_kernel_spmd as _run

    nc = _bacc.Bacc("TRN2", target_bir_lowering=False, num_devices=1)
    arrays, args = {}, []
    for name in _INS:
        a = _np.ascontiguousarray(inputs[name])
        arrays[f"in_{name}_dram"] = a
        args.append(nc.dram_tensor(f"in_{name}_dram", a.shape, _mybir.dt.from_np(a.dtype), kind="ExternalInput").ap())
    for i, shape in enumerate(_OUTS):
        args.append(nc.dram_tensor(f"out_{i}_dram", shape, _mybir.dt.float32, kind="ExternalOutput").ap())
    fox_ssd_hybrid_kernel(nc, *args)
    r = _run(nc, [arrays], core_ids=[0])
    return tuple(r.results[0][f"out_{i}_dram"] for i in range(len(_OUTS)))
```

```python
from contextlib import ExitStack, contextmanager

import concourse.bass as bass
from concourse import mybir

F32 = mybir.dt.float32
F32R = mybir.dt.float32r
BF16 = mybir.dt.bfloat16
ALU = mybir.AluOpType
ACT = mybir.ActivationFunctionType
AX = mybir.AxisListType

P = 128
D = 1024
SAMPLE = 64
META = 16
SEQ = 512
PROMPT = META + SEQ
TOK = SAMPLE + PROMPT
PAST = 512
KT = D // P
FF = 2816
HEADS = 16
HD = 64
SSM_HEADS = 32
GROUPS = 8
NSTATE = 128
D_SSM = 2048
D_CONV = 4096
OFF_XBC = D_SSM
OFF_DT = OFF_XBC + D_CONV
OFF_Q = OFF_DT + SSM_HEADS
OFF_K = OFF_Q + D
OFF_V = OFF_K + D
OFF_F = OFF_V + D
OFF_GS = OFF_F + HEADS
OFF_GA = OFF_GS + D
EPS = 1e-6
NEG = -1e30
SCALE = float(HD) ** -0.5

TILES = 5
ROWS = [128, 128, 128, 128, TOK - 512]
HALF = TOK // 2
BANK = 512
PC_CONVW, PC_CONVB, PC_NORM, PC_SSMN, PC_STATE, PC_END = 0, 128, 160, 192, 208, 304
NORM_FFN1, NORM_MIX, NORM_FFN2, NORM_FINAL = range(4)
CS_ = 3
CP_ = CS_ + SAMPLE + 3
CW = CP_ + PROMPT
CO = CW - 3
CHUNKS = [(0, 64), (64, 128), (128, 256), (256, 384), (384, 512), (512, TOK)]
THIRDS = [(0, 8), (8, 8), (16, 6)]


class Count:

    def __init__(self, start=0):
        self.n, self.i, self.per = start, None, 0

    def __call__(self, more=0):
        v = self.n + more
        return v if self.i is None or self.per == 0 else self.i * self.per + v

    def up(self, k=1):
        self.n += k
        return self()


@contextmanager
def looped(eng, iters, counts, pers):
    base = [c.n for c in counts]
    with eng.Fori(0, iters) as i:
        for c, p in zip(counts, pers):
            c.i, c.per = i, p
        yield i
        moved = [c.n - b for c, b in zip(counts, base)]
        assert moved == list(pers), (moved, list(pers))
    for c, b, p in zip(counts, base, pers):
        c.i, c.per, c.n = None, 0, b + p * iters


class Stream:

    def __init__(self):
        self.duo = Count()
        self.uses = [Count(), Count()]
        self.out = Count(KT)
        self.act = Count(KT)
        self.dve = Count()

    def all(self):
        return [self.duo, *self.uses, self.out, self.act, self.dve]


PRIMED = 2

MID = ["z", "x", "bc", "z", "x", "bc", "q", "k", "v"]
MID_SLOT = [1, 0, 1, 0, 1, 0, 1, 0, 1]
OUTS = {"z": TILES, "v": TILES, "x": 2, "bc": 2, "q": 2, "k": 2}
MID_OUTS = sum(OUTS[k] for k in MID)
OUT_AT = [sum(OUTS[k] for k in MID[:n]) for n in range(9)]
MID_PER = [9, 4, 5, MID_OUTS, MID_OUTS, 0]
JOBS = 4 * TILES


STAGES = JOBS + 2


def pieces(duos, ahead=0):
    return [("lin", n, t, ahead, 0, 0) for n in duos for t in range(OUTS[MID[n]])]


def with_splits(steps):
    out = []
    for step in steps:
        if step[0] == "lin" and step[2] == 1 and step[1] < 8:
            out.append(("split", step[1]))
        out.append(step)
    return out


def ssd_window(duos, g):
    ssd = {
        0: [("prep", g), ("convA", g, 0), ("convA", g, 1)],
        1: [("convB", g, 0), ("cst", g)],
        2: [("convA", g, 2), ("convB", g, 1)],
        3: [("convA", g, 3), ("convB", g, 2)],
        4: [("convB", g, 3)],
        5: [("s1", g, 0)],
        6: [("s1", g, 1), ("s2", g, 0)],
        7: [("s1", g, 2), ("s2", g, 1)],
        8: [("s1", g, 3), ("s2", g, 2)],
        9: [("s1", g, 4)] + [("rows", 1, 0)] * (g == 0) + [("s2", g, 3), ("s2", g, 4), ("s3", g)],
    }
    order = []
    for at, piece in enumerate(pieces(duos)):
        order += ssd.get(at, []) + [piece]
    return with_splits(order + ssd[9])


def heads_window():
    order = [("enter",), ("rows", 0, 1), ("split", 8)]
    stage = 0
    for _, n, t, ahead, _, _ in pieces([0, 1, 2], 1):
        if (n, t) == (0, 2):
            order.append(("cache",))
        more = 4 if n else 2 * (t >= 2)
        order.append(("lin", n, t, ahead, stage, stage + more))
        stage += more
    assert stage == STAGES
    return with_splits(order) + [("leave",)]


FIRST_STEPS = [("rows", 0, 0)] + with_splits(pieces([0, 1, 2]))
SSD_STEPS = ssd_window([3, 4, 5], 0) + ssd_window([6, 7, 8], 1)
LOOP_STEPS = SSD_STEPS + heads_window()
LAST_STEPS = SSD_STEPS + [("enter",), ("split", 8), ("cache",), ("stages", 0, STAGES), ("leave",)]


def freed(i, n, t):
    return i * MID_OUTS + (KT + 1 + OUT_AT[n] + t + 1)


def conv_in(i, g, j):
    return freed(i, 3 * g + 1 + j // 2, j % 2)


def conv_tile(i, g, j):
    return i * 4 + (2 * g + j) if j < 2 else i * 2 + (2 * KT + (j - 2) * GROUPS + g)


def score_span(t):
    before = PAST if t == 0 else t * P - SAMPLE
    return before, before + ROWS[t]


def key_blocks(t):
    return TILES if t == 0 else t + 1


def fox_ssd_hybrid_kernel(nc, x_prompt, x_sample, cache_k, cache_v, cache_logf, state_ssm, state_conv,
                          meta_tokens, norm_ffn1, ffn1_w_in, ffn1_w_out, norm_mix, w_in, conv_w, conv_b,
                          dt_bias, a_log, d_skip, f_bias, ssm_norm, w_br_ssm, w_br_attn, w_out, norm_ffn2,
                          ffn2_w_in, ffn2_w_out, norm_final,
                          y_prompt, y_sample, k_prompt, v_prompt, logf_prompt, ssm_prompt, conv_prompt,
                          k_sample, v_sample, logf_sample, ssm_sample, conv_sample):
    ctx = ExitStack()
    with ctx:
        def sb(name, shape, dt=F32, scope=ctx):
            return scope.enter_context(nc.sbuf_tensor(name, shape, dt))

        def sem(name):
            return ctx.enter_context(nc.semaphore(name))

        h_spill = nc.dram_tensor("h_spill", [P, KT * TOK], F32).ap()
        oa_spill = nc.dram_tensor("oa_spill", [KT, P, TOK], F32).ap()
        os_spill = nc.dram_tensor("os_spill", [2 * KT, P, TOK], F32).ap()
        acs_rows = nc.dram_tensor("acs_rows", [SSM_HEADS, TOK], F32).ap()
        bias0_rows = nc.dram_tensor("bias0_rows", [HEADS, 2, PAST + P], F32).ap()
        biasp_rows = nc.dram_tensor("biasp_rows", [HEADS, PROMPT], F32).ap()

        raw = sb("raw", [P, 2, KT, 256])
        wh = sb("wh", [P, 2, KT, 256], F32R)
        wl = sb("wl", [P, 2, KT, 256], F32R)
        xah = sb("xah", [P, KT, TOK], F32R)
        xal = sb("xal", [P, KT, TOK], F32R)
        ident = sb("ident", [P, P])
        ones = sb("ones", [P, P])
        identb = sb("identb", [P, P], BF16)
        negmask = sb("negmask", [P, 2, P], BF16)
        mask01 = sb("mask01", [P, 2, P])
        par = sb("par", [P, PC_END])
        parh = sb("parh", [P, PC_NORM])
        dsk = sb("dsk", [P, SSM_HEADS])
        tokt = sb("tokt", [P, TILES, P])
        scanm = sb("scanm", [48, TOK])

        ps = ctx.enter_context(nc.psum_tensor("ps", [P, 8 * BANK], F32))

        passed = sem("passed")

        def bank(b, n, rows=P, at=0):
            return ps[0:rows, b * BANK + at:b * BANK + at + n]

        def halves(b, rows=P):
            return ps[0:rows, b * BANK:(b + 2) * BANK].rearrange("p (a n) -> p a n", a=2)[:, :, 0:HALF]

        def in_halves(ap):
            return ap.rearrange("p (a n) -> p a n", a=2)

        def ffn_buffers(scope, tag):
            return {"h": sb("h" + tag, [P, KT, TOK], F32, scope),
                    "xbh": sb("xbh" + tag, [P, KT, TOK], F32R, scope),
                    "xbl": sb("xbl" + tag, [P, KT, TOK], F32R, scope),
                    "act": sb("act" + tag, [P, TOK], F32, scope),
                    "full": sb("full" + tag, [P, 2, TOK], F32, scope),
                    "rs": sb("rs" + tag, [P, TOK], F32, scope)}

        with ExitStack() as s:
            F1 = ffn_buffers(s, "1")
            xin = sb("xin", [P, TILES, 512], F32, s)
            prow = sb("prow", [P, 3, P], F32, s)
        with ExitStack() as s:
            tcol = sb("tcol", [48, 8], F32, s)
            tx = sb("tx", [48, TOK], F32, s)
            tb = sb("tb", [48, TOK], F32, s)
            tsteps = sb("tsteps", [48, TOK], F32, s)
            tsum = sb("tsum", [48, TOK], F32, s)
            tdec = sb("tdec", [32, TOK], F32, s)
            tstack = sb("tstack", [P, TOK], F32, s)
            tcm = sb("tcm", [16, SAMPLE + META], F32, s)
            tcs = sb("tcs", [16, PAST + SAMPLE + META], F32, s)
            nb0 = sb("nb0", [16, 2, PAST + P], F32, s)
            nbp = sb("nbp", [16, PROMPT], F32, s)
            clf = sb("clf", [P, 4, 16], F32, s)
            lft = sb("lft", [P, TILES, 64], F32, s)
            one16 = sb("one16", [16, PAST], F32, s)
        with ExitStack() as s:
            qz = sb("qz", [P, 4, TOK], F32, s)
            kT = sb("kT", [P, 2, TOK], F32, s)
            vt = sb("vt", [P, TILES, 256], F32, s)
            kcT = sb("kcT", [P, 2, PAST], F32, s)
            vc = sb("vc", [P, 4, 256], F32, s)
            xp = sb("xp", [P, 4, CW], F32, s)
            cvt = sb("cvt", [P, 2, CO], F32, s)
            th = sb("th", [P, CO], F32, s)
            brow = sb("brow", [P, 4, TOK], F32, s)
            zs = sb("zs", [P, 2, TILES, 256], F32, s)
            zt = sb("zt", [P, 2, 256], F32, s)
            zr = sb("zr", [P, 2, 256], F32, s)
            sini = sb("sini", [P, 256], F32, s)
            sraw = sb("sraw", [P, 2, P], F32, s)
            dec = sb("dec", [P, 4, TILES], F32, s)
            with ExitStack() as g:
                cv = sb("cv", [P, 4, TOK], F32, g)
                xbt = sb("xbt", [P, 2, 384], F32, g)
                xd = sb("xd", [P, 2, 256], F32, g)
                xdd = sb("xdd", [P, 2, 256], F32, g)
                xsk = sb("xsk", [P, 2, 256], F32, g)
                eb = sb("eb", [P, 4, P], F32, g)
                mb = sb("mb", [P, 2, 4, P], F32, g)
                cbm = sb("cbm", [P, P], F32, g)
                y1 = sb("y1", [P, 256], F32, g)
                y2 = sb("y2", [P, 256], F32, g)
                yg = sb("yg", [P, TILES, 256], F32, g)
                junk = sb("junk", [P, 256], F32, g)
                ssq = sb("ssq", [P, 8], F32, g)
                sfin = sb("sfin", [P, 256], F32, g)
                spr = sb("spr", [P, 2, 256], F32, g)
                sto = sb("sto", [P, 4, P], F32, g)
                yT = sb("yT", [P, 2, TOK], F32, g)
                cst = yT[0:3, :, 0:512]
            with ExitStack() as g:
                bias = sb("bias", [P, 2, PAST + P + PROMPT], F32, g)
                kcr = sb("kcr", [P, 4, 256], F32, g)
                p0 = sb("p0", [P, PAST + P], F32, g)
                pp = sb("pp", [P, 2, TOK], F32, g)
                pt = sb("pt", [P, 2, TILES * P], F32, g)
                otok = sb("otok", [P, TILES, 256], F32, g)
                ktok = sb("ktok", [P, TILES, 256], F32, g)
                oT = sb("oT", [P, 2, TOK], F32, g)
                mx = sb("mx", [P, 4], F32, g)
                rsum = sb("rsum", [P, 4], F32, g)
                rinv = sb("rinv", [P, 4], F32, g)
        with ExitStack() as s:
            G2 = ffn_buffers(s, "2")
            gates = sb("gates", [P, 2 * KT, TOK], F32, s)
            ytok = gates[:, 0:9, :].rearrange("p a b -> p (a b)")[:, 0:TILES * D].rearrange(
                "p (t c) -> p t c", t=TILES)

        x_in = [sem("x_in0"), sem("x_in1")]
        par_in, consts, par_T, par_ready = sem("par_in"), sem("consts"), sem("par_T"), sem("par_ready")
        raw_ready = [sem("raw_ready0"), sem("raw_ready1")]
        hi_ready, split_done = sem("hi_ready"), sem("split_done")
        lin_out, act_free, dve_free = sem("lin_out"), sem("act_free"), sem("dve_free")
        gated, full_ready, xhi_ready, x_ready = sem("gated"), sem("full_ready"), sem("xhi_ready"), sem("x_ready")
        sq_ready, sq_summed, rinv_ready, rs_ready = sem("sq_ready"), sem("sq_summed"), sem("rinv_ready"), sem("rs_ready")
        h_out, h_back = sem("h_out"), sem("h_back")
        dch, ach, gch = sem("dch"), sem("ach"), sem("gch")
        t_pool, t_dve, t_act, t_pe, t_in, t_out = (sem("t_" + n) for n in ("pool", "dve", "act", "pe", "in", "out"))
        heads_left, ssd_left = sem("heads_left"), sem("ssd_left")
        z_used, hist_ready = sem("z_used"), sem("hist_ready")
        tap0_ready, taps_done, tanh_ready, cv_done = sem("tap0_ready"), sem("taps_done"), sem("tanh_ready"), sem("cv_done")
        brow_in, sraw_in, sraw_T, sini_ready = sem("brow_in"), sem("sraw_in"), sem("sraw_T"), sem("sini_ready")
        dec_ready, cst_T, cst_ready, cst_out = sem("dec_ready"), sem("cst_T"), sem("cst_ready"), sem("cst_out")
        xb_T, xb_ready, cb_ready, cbm_ready = sem("xb_T"), sem("xb_ready"), sem("cb_ready"), sem("cbm_ready")
        seg_ready, e_ready, m_ready, xd_ready = sem("seg_ready"), sem("e_ready"), sem("m_ready"), sem("xd_ready")
        st_ready, s_ready, yo_ready, yd_ready = sem("st_ready"), sem("s_ready"), sem("yo_ready"), sem("yd_ready")
        y_used, yg_ready, sq_done, rv_ready = sem("y_used"), sem("yg_ready"), sem("sq_done"), sem("rv_ready")
        rt_ready, yn_ready, yT_T, yT_ready, yT_out = (sem(n) for n in ("rt_ready", "yn_ready", "yT_T", "yT_ready", "yT_out"))
        st_sample = sem("st_sample")
        sf_T, sto_ready, sto_out = sem("sf_T"), sem("sto_ready"), sem("sto_out")
        kc_in, vc_in, kc_T, kc_ready = sem("kc_in"), sem("vc_in"), sem("kc_T"), sem("kc_ready")
        ktok_T, ktok_ready, k_out, v_out = sem("ktok_T"), sem("ktok_ready"), sem("k_out"), sem("v_out")
        bias_in = [sem("bias_in0"), sem("bias_in1")]
        qk_ready, s_free, mx_ready, p_ready, p_T = (sem(n) for n in ("qk_ready", "s_free", "mx_ready", "p_ready", "p_T"))
        pt_ready, pv_ready, o_ready, pz_ready = sem("pt_ready"), sem("pv_ready"), sem("o_ready"), sem("pz_ready")
        o_T, oT_ready, oT_out = sem("o_T"), sem("oT_ready"), sem("oT_out")
        stage_in = [sem("stage_in0"), sem("stage_in1")]
        fin_T, fin_ready, y_out = sem("fin_T"), sem("fin_ready"), sem("y_out")

        def rows_of(w):
            return w[0].rearrange("(k p) n -> p k n", p=P)

        win1, wout1, winp = rows_of(ffn1_w_in), rows_of(ffn1_w_out), rows_of(w_in)
        win2, wout2 = rows_of(ffn2_w_in), rows_of(ffn2_w_out)
        wbs, wba, wo = rows_of(w_br_ssm), rows_of(w_br_attn), rows_of(w_out)

        def state_rows(s, g):
            return s[0, 0].rearrange("(g h) p n -> g (h p) n", h=4)[bass.ds(g, 1)].rearrange(
                "g (j q) n -> q (g j) n", q=P)

        def scores(t):
            before, n = score_span(t)
            return p0[:, 0:n] if t == 0 else pp[0:ROWS[t], t % 2, SAMPLE:SAMPLE + n]

        X_MIX = KT + FF // P + KT

        block = ctx.enter_context(nc.Block())

        @block.sync
        def _(sp):
            st = Stream()

            def load(slot, parts, back=1):
                sp.wait_ge(split_done, st.duo(back))
                for dst, src in parts:
                    sp.dma_start(dst, src).then_inc(raw_ready[slot], 16)
                st.duo.up()
                st.uses[slot].up()

            def r(slot, k0, k1, c0, c1):
                return raw[:, slot, k0:k1, c0:c1]

            def wide(s, w, c, back=1):
                load(s, [(r(s, 0, 4, 0, 256), w[:, 0:4, bass.ds(c, 256)]),
                         (r(s, 4, KT, 0, 256), w[:, 4:KT, bass.ds(c, 256)])], back)

            def pair(s, w, c, apart, back=1):
                load(s, [(r(s, 0, KT, 0, P), w[:, :, bass.ds(c, P)]),
                         (r(s, 0, KT, P, 256), w[:, :, bass.ds(c + apart, P)])], back)

            def ffn(win, wout, slots):
                for t0, nt in THIRDS:
                    with looped(sp, nt // 2, st.all(), [2, 1, 1, 0, 0, 0]) as i:
                        for n, s in enumerate(slots):
                            pair(s, win, i * 256 + (t0 + n) * P, FF)
                    with looped(sp, 2, st.all(), [2, 1, 1, 0, 0, 0]) as i:
                        for n, s in enumerate(slots):
                            c, m = i * 512 + n * 256, nt // 2
                            load(s, [(r(s, 0, m, 0, 256), wout[:, t0:t0 + m, bass.ds(c, 256)]),
                                     (r(s, m, nt, 0, 256), wout[:, t0 + m:t0 + nt, bass.ds(c, 256)])])

            ffn(win1, wout1, (0, 1))
            load(0, [(r(0, 0, KT, 0, SSM_HEADS), winp[:, :, OFF_DT:OFF_DT + SSM_HEADS]),
                     (r(0, 0, KT, SSM_HEADS, 48), winp[:, :, OFF_F:OFF_F + HEADS])])

            def mid(i, duos):
                for n in duos:
                    kind, s, g, back = MID[n], MID_SLOT[n], n // 3, 2 if n == 0 else 1
                    if kind == "z":
                        wide(s, winp, i * 512 + g * 256, back)
                    elif kind == "x":
                        wide(s, winp, i * 512 + (OFF_XBC + g * 256))
                    elif kind == "bc":
                        pair(s, winp, i * 256 + (OFF_XBC + D_SSM + g * P), GROUPS * NSTATE)
                    else:
                        wide(s, winp, i * 256 + {"q": OFF_Q, "k": OFF_K, "v": OFF_V}[kind])

            mid(0, range(3))
            with looped(sp, 3, st.all(), MID_PER[:3] + [0, 0, 0]) as i:
                mid(i, range(3, 9))
                mid(i + 1, range(3))
            mid(3, range(3, 9))
            first = 2
            for w, off in ((winp, OFF_GA), (winp, OFF_GS), (wba, 0), (wbs[:, 0:KT], 0), (wbs[:, KT:2 * KT], 0), (wo, 0)):
                with looped(sp, 2, st.all(), [2, 1, 1, 0, 0, 0]) as i:
                    for n, s in enumerate((1, 0)):
                        wide(s, w, i * 512 + (off + n * 256), first if n == 0 else 1)
                first = 1
            ffn(win2, wout2, (1, 0))

        @block.gpsimd
        def _(pool):
            chain = Count()

            def link(ins):
                ins.then_inc(gch, 1)
                pool.wait_ge(gch, chain.up())

            def settle():
                pool.sem_inc(passed, 1)

            pool.sem_inc(z_used, PRIMED)

            for half in range(2):
                c = slice(512 * half, 512 * half + 512)
                if half:
                    pool.wait_ge(lin_out, 4)
                for dst, src in ((xin[0:64, 0, :], x_sample[0, :, c]), (xin[64:80, 0, :], meta_tokens[:, c]),
                                 (xin[80:128, 0, :], x_prompt[0, 0:48, c]),
                                 (xin[:, 1:4, :], x_prompt[0, 48:432, c].rearrange("(t p) c -> p t c", p=P)),
                                 (xin[0:80, 4, :], x_prompt[0, 432:512, c])):
                    pool.dma_start(dst, src).then_inc(x_in[half], 16)
                if half:
                    continue
                for dst, src in (
                        (prow[:, 0, :], conv_w[0].rearrange("j (t c) -> (j t) c", c=P)),
                        (prow[0:32, 1, :], conv_b[0].rearrange("(t c) -> t c", c=P)),
                        (prow[32:40, 1, :], norm_ffn1[0].rearrange("(t c) -> t c", c=P)),
                        (prow[40:48, 1, :], norm_mix[0].rearrange("(t c) -> t c", c=P)),
                        (prow[48:56, 1, :], norm_ffn2[0].rearrange("(t c) -> t c", c=P)),
                        (prow[56:64, 1, :], norm_final.rearrange("(t c) -> t c", c=P)),
                        (prow[64:80, 1, :], ssm_norm[0].rearrange("(t c) -> t c", c=P)),
                        (prow[0:96, 2, :], state_conv[0, 0].rearrange("r (t c) -> (r t) c", c=P)),
                        (dsk[:, :], d_skip[0:1, :].to_broadcast([P, SSM_HEADS]))):
                    pool.dma_start(dst, src).then_inc(par_in, 16)
                link(pool.memset(ident[:, :], 0.0))
                link(pool.affine_select(out=ident[:, :], in_=ident[:, :], compare_op=ALU.not_equal, fill=1.0,
                                        base=0, pattern=[[-1, P]], channel_multiplier=1))
                pool.tensor_copy(identb[:, :], ident[:, :])
                pool.memset(ones[:, :], 1.0).then_inc(consts, 1)
                link(pool.memset(negmask[:, :, :], 0.0))
                link(pool.affine_select(out=negmask[:, :, :], in_=negmask[:, :, :], compare_op=ALU.is_ge,
                                        fill=NEG, base=0, pattern=[[0, 2], [-1, P]], channel_multiplier=1))
                link(pool.memset(negmask[0:64, 0, 64:80], 0.0))
                link(pool.memset(mask01[:, :, :], 1.0))
                link(pool.affine_select(out=mask01[:, :, :], in_=mask01[:, :, :], compare_op=ALU.is_ge,
                                        fill=0.0, base=0, pattern=[[0, 2], [1, P]], channel_multiplier=-1))
                link(pool.memset(mask01[0:64, 0, 64:128], 0.0))
                link(pool.memset(scanm[:, :], 1.0))
                for c0, _ in CHUNKS:
                    pool.memset(scanm[0:32, c0:c0 + 1], 0.0)
                pool.memset(scanm[32:48, 64:65], 0.0).then_inc(consts, 1)

            pool.wait_ge(x_ready, X_MIX)
            pool.dma_start(h_spill, F1["h"][:, :, :].rearrange("p k t -> p (k t)")).then_inc(h_out, 16)
            pool.wait_ge(h_out, 16)
            for dst, src in ((clf[:, :, :], cache_logf[0, 0].rearrange("(a p) h -> p a h", p=P)),
                             (tcol[0:32, 0:1], dt_bias.rearrange("o h -> h o")),
                             (tcol[32:48, 0:1], f_bias.rearrange("o h -> h o")),
                             (tcol[0:32, 1:2], a_log.rearrange("o h -> h o"))):
                pool.dma_start(dst, src).then_inc(t_in, 16)
            pool.memset(one16[:, :], 1.0)
            pool.memset(tcol[0:32, 2:3], 1.0)
            link(pool.memset(tcol[32:48, 2:3], -1.0))
            pool.memset(tcol[:, 3:4], -1.0)
            pool.memset(nb0[:, 1, 0:PAST + SAMPLE], NEG)
            pool.memset(nb0[:, 0, PAST + SAMPLE + META:], NEG).then_inc(t_pool, 1)
            pool.wait_ge(t_dve, 4)
            pool.dma_start(acs_rows, tsum[0:32, :]).then_inc(t_out, 16)
            pool.dma_start(bias0_rows, nb0[:, :, :]).then_inc(t_out, 16)
            pool.dma_start(biasp_rows, nbp[:, :]).then_inc(t_out, 16)
            pool.wait_ge(t_act, 4)
            pool.dma_start(logf_sample[0, 0], lft[0:64, 0, 32:48]).then_inc(t_out, 16)
            pool.dma_start(logf_prompt[0, 0, 0:64], lft[64:128, 0, 32:48]).then_inc(t_out, 16)
            pool.dma_start(logf_prompt[0, 0, 64:448].rearrange("(t p) h -> p t h", p=P), lft[:, 1:4, 32:48]).then_inc(t_out, 16)
            pool.dma_start(logf_prompt[0, 0, 448:528], lft[0:80, 4, 32:48]).then_inc(t_out, 16)
            pool.wait_ge(t_out, 16 * 7)
            for hh in range(4):
                r = HD * (1 - hh % 2)
                link(pool.memset(qz[r:r + HD, hh, :], 0.0))
            pool.sem_inc(heads_left, 1)

            def mid(now, steps):
                for step in steps:
                    i, kind, g = now, step[0], step[1] if len(step) > 1 else 0
                    if kind == "lin" and MID[g] == "z":
                        i, t, g = now + step[3], step[2], g // 3
                        if t == 0 and step[3]:
                            pool.wait_ge(yg_ready, now * 10 + (PRIMED + 5))
                        m, b = ROWS[t], (g + t) % 2
                        pool.wait_ge(act_free, freed(i, step[1], t))
                        settle()
                        link(pool.tensor_scalar(zt[0:m, b, :], zt[0:m, b, :], 1.0, None, ALU.add))
                        pool.tensor_tensor(zs[0:m, g, t, :], zt[0:m, b, :], zr[0:m, b, :], ALU.mult).then_inc(z_used, 1)
                    elif kind == "lin" and MID[g] == "x" and step[2] == 0:
                        i, g = now + step[3], g // 3
                        pool.wait_ge(taps_done, i * 8 + (PRIMED + 4 * g))
                        pool.wait_ge(cst_T, i * 2 + (PRIMED + g))
                        settle()
                        hist = par[:, PC_STATE:PC_STATE + 96].rearrange("p (r t) -> p t r", r=3)
                        pool.memset(xp[:, :, CS_ + SAMPLE:CP_], 0.0)
                        pool.tensor_copy(xp[:, 0:2, 0:3], hist[:, bass.ds(i * 4 + 2 * g, 2), :])
                        pool.tensor_copy(xp[:, 2:3, 0:3], hist[:, bass.ds(i * 2 + (16 + g), 1), :])
                        pool.tensor_copy(xp[:, 3:4, 0:3], hist[:, bass.ds(i * 2 + (24 + g), 1), :]).then_inc(hist_ready, 1)
                    elif kind == "rows":
                        i = now + step[2]
                        pool.wait_ge(seg_ready, i * 10 + (PRIMED + 5 * g))
                        pool.wait_ge(dec_ready, i * 2 + (PRIMED + g))
                        pool.wait_ge(sraw_T, i * 2 + (PRIMED + g))
                        settle()
                        pool.dma_start(brow[:, :, :], acs_rows[bass.ds(i * 8 + 4 * g, 4), :].partition_broadcast(P))\
                            .then_inc(brow_in, 16)
                        pool.dma_start(sraw[:, :, :], state_rows(state_ssm, i * 2 + g)).then_inc(sraw_in, 16)
                    elif kind == "cst":
                        pool.wait_ge(cst_ready, i * 2 + (PRIMED + g + 1))
                        settle()
                        for k, dst in enumerate((conv_sample[0, 0], conv_prompt[0, 0])):
                            for c0, n, off in ((0, 256, i * 512 + 256 * g), (256, P, i * 256 + (D_SSM + P * g)),
                                               (384, P, i * 256 + (D_SSM + D + P * g))):
                                pool.dma_start(dst[:, bass.ds(off, n)], cst[:, k, c0:c0 + n]).then_inc(cst_out, 16)
                    elif kind == "s1":
                        t = step[2]
                        m, b, hs, tau = ROWS[t], (t + g) % 2, i * 8 + 4 * g, PRIMED + 5 * g + t
                        xv = xbt[0:m, b, 0:256].rearrange("p (h c) -> p h c", h=4)
                        pool.wait_ge(xb_ready, i * 10 + (tau + 1))
                        pool.wait_ge(yd_ready, i * 10 + (tau - 1))
                        pool.wait_ge(y_used, i * 10 + (tau - 1))
                        for dst, src in ((xd, tokt[0:m, t, bass.ds(hs + 32, 4)]), (xdd, tokt[0:m, t, bass.ds(hs + 64, 4)]),
                                         (xsk, dsk[0:m, bass.ds(hs, 4)])):
                            last = pool.tensor_tensor(dst[0:m, b, :].rearrange("p (h c) -> p h c", h=4), xv,
                                                      src.unsqueeze(2).to_broadcast([m, 4, HD]), ALU.mult)
                        last.then_inc(xd_ready, 1)
                    elif kind == "s3":
                        pool.wait_ge(yT_ready, i * 4 + (PRIMED + 2 * g + 2))
                        settle()
                        pool.dma_start(os_spill[bass.ds(i * 4 + 2 * g, 2)].rearrange("j p t -> p j t"), yT[:, :, :])\
                            .then_inc(yT_out, 16)
                        pool.wait_ge(sto_ready, i * 2 + (PRIMED + g + 1))
                        settle()
                        for k, dst in enumerate((ssm_sample, ssm_prompt)):
                            pool.dma_start(state_rows(dst, i * 2 + g), sto[:, 2 * k:2 * k + 2, :]).then_inc(sto_out, 16)
                    if kind == "enter":
                        pool.wait_ge(yT_out, i * 32 + 32)
                        pool.wait_ge(sto_out, i * 64 + 64)
                        pool.wait_ge(cst_out, i * 192 + 192)
                        pool.sem_inc(ssd_left, 1)
                        pool.dma_start(kcr[:, :, :], cached(cache_k, i * 256)).then_inc(kc_in, 16)
                        load_bias(i, 0)
                        load_bias(i, 1)
                        pool.memset(pp[:, :, 0:SAMPLE], 0.0).then_inc(pz_ready, 1)
                        pool.dma_start(vc[:, :, :], cached(cache_v, i * 256)).then_inc(vc_in, 16)
                    elif kind == "cache":
                        pool.wait_ge(act_free, i * MID_OUTS + (KT + 1 + MID_OUTS))
                        settle()
                        store_rows(v_sample, v_prompt, i * 256, vt, v_out)
                        pool.wait_ge(ktok_ready, i * 3 + 3)
                        settle()
                        store_rows(k_sample, k_prompt, i * 256, ktok, k_out)
                    elif kind in ("lin", "stages"):
                        s0, s1 = step[-2:]
                        for hh in (2, 3):
                            if s0 <= 5 * hh - 5 < s1:
                                pool.wait_ge(s_free, now * JOBS + (PRIMED + 5 * (hh - 1)))
                                settle()
                                load_bias(now, hh)
                    elif kind == "leave":
                        pool.wait_ge(oT_ready, i * 2 + (PRIMED + 2))
                        settle()
                        pool.dma_start(oa_spill[bass.ds(i * 2, 2)].rearrange("j p t -> p j t"), oT[:, :, :]).then_inc(oT_out, 16)
                        pool.wait_ge(k_out, i * 64 + 64)
                        pool.wait_ge(v_out, i * 64 + 64)
                        pool.wait_ge(oT_out, i * 16 + 16)
                        pool.sem_inc(heads_left, 1)

            def cached(cache, c):
                return cache[0, 0].rearrange("(a p) h d -> p a (h d)", p=P)[:, :, bass.ds(c, 256)]

            def load_bias(i, hh):
                b, hd = hh % 2, i * 4 + hh
                for q in range(2):
                    pool.dma_start(bias[64 * q:64 * q + 64, b, 0:PAST + P],
                                   bias0_rows[bass.ds(hd, 1), q, :].to_broadcast([64, PAST + P])).then_inc(bias_in[b], 16)
                pool.dma_start(bias[:, b, PAST + P:], biasp_rows[bass.ds(hd, 1), :].to_broadcast([P, PROMPT]))\
                    .then_inc(bias_in[b], 16)

            def store_rows(to_sample, to_prompt, c, src, s):
                to_s = to_sample[0, 0].rearrange("t h d -> t (h d)")[:, bass.ds(c, 256)]
                to_p = to_prompt[0, 0].rearrange("t h d -> t (h d)")[:, bass.ds(c, 256)]
                pool.dma_start(to_s, src[0:64, 0, :]).then_inc(s, 16)
                pool.dma_start(to_p[0:64], src[64:128, 0, :]).then_inc(s, 16)
                pool.dma_start(to_p[64:448].rearrange("(t p) c -> p t c", p=P), src[:, 1:4, :]).then_inc(s, 16)
                pool.dma_start(to_p[448:528], src[0:80, 4, :]).then_inc(s, 16)

            mid(0, FIRST_STEPS)
            with looped(pool, 3, [chain], [2 * TILES]) as i:
                mid(i, LOOP_STEPS)
            mid(3, LAST_STEPS)

            n = X_MIX
            for src, t0 in ((oa_spill, 0), (os_spill, 0), (os_spill, KT)):
                with looped(pool, 4, [], []) as i:
                    for b in range(2):
                        pool.wait_ge(x_ready, i * 2 + (n + b - 1))
                        settle()
                        pool.dma_start(G2["full"][:, b, :], src[bass.ds(i * 2 + (t0 + b), 1)].rearrange("o p t -> p (o t)"))\
                            .then_inc(stage_in[b], 16)
                n += KT
            pool.wait_ge(x_ready, n + KT)
            pool.dma_start(G2["h"][:, :, :].rearrange("p k t -> p (k t)"), h_spill).then_inc(h_back, 16)

            pool.wait_ge(fin_ready, KT)
            pool.dma_start(y_sample[0], ytok[0:64, 0, :]).then_inc(y_out, 16)
            pool.dma_start(y_prompt[0, 0:48], ytok[80:128, 0, :]).then_inc(y_out, 16)
            pool.dma_start(y_prompt[0, 48:432].rearrange("(t p) c -> p t c", p=P), ytok[:, 1:4, :]).then_inc(y_out, 16)
            pool.dma_start(y_prompt[0, 432:512], ytok[0:80, 4, :]).then_inc(y_out, 16)
            pool.wait_ge(y_out, 64)

        @block.scalar
        def _(act):
            st = Stream()
            chain, full, sq, rinvs, summed = Count(), Count(), Count(), Count(), Count()
            xhi = Count()

            for s in (sq_done, dec_ready, cst_ready, xb_ready, yT_ready, sto_ready, oT_ready):
                act.sem_inc(s, PRIMED)

            def link(ins):
                ins.then_inc(ach, 1)
                act.wait_ge(ach, chain.up())

            def split(slot, free_at):
                act.wait_ge(raw_ready[slot], split_uses(slot))
                act.wait_ge(lin_out, free_at)
                act.activation(wh[:, slot], raw[:, slot], ACT.Copy).then_inc(hi_ready, 1)

            def split_uses(slot):
                st.uses[slot].up()
                u = st.uses[slot]
                return u.n * 32 if u.i is None or u.per == 0 else u.i * (32 * u.per) + u.n * 32

            def norm(dst):
                with looped(act, KT // 2, [sq], [2]) as i:
                    for b in range(2):
                        act.wait_ge(sq_summed, sq(PRIMED - 1))
                        act.activation(G["full"][:, b, :], G["h"][:, bass.ds(i * 2 + b, 1), :].rearrange("p o t -> p (o t)"),
                                       ACT.Square).then_inc(sq_ready, 1)
                        sq.up()
                act.wait_ge(rinv_ready, rinvs.up())
                act.activation(G["rs"][:, :], G["rs"][:, :], ACT.Sqrt).then_inc(rs_ready, 1)
                if dst is None:
                    return
                with looped(act, KT // 2, [full], [2]) as i:
                    for b in range(2):
                        act.wait_ge(full_ready, full(1))
                        act.activation(dst[:, bass.ds(i * 2 + b, 1), :], G["full"][:, b:b + 1, :], ACT.Copy).then_inc(xhi_ready, 1)
                        full.up()

            def ffn(slots, last=False):
                for t0, nt in THIRDS:
                    with looped(act, nt // 2, st.all() + [full], [2, 1, 1, 4, 0, 0, 2]) as i:
                        for n, s in enumerate(slots):
                            split(1 - s, st.out())
                            st.duo.up()
                            act.wait_ge(lin_out, st.out.up(2))
                            act.wait_ge(full_ready, full())
                            act.activation(in_halves(G["act"][:, :]), halves(4 * n), ACT.Silu).then_inc(gated, 1)
                            act.wait_ge(full_ready, full(1))
                            act.activation(G["xbh"][:, bass.ds(i * 2 + n, 1), :], G["full"][:, n:n + 1, :], ACT.Copy)\
                                .then_inc(xhi_ready, 1)
                            full.up()
                    if last and t0 + nt == FF // P:
                        for s in (slots * 2)[:-1]:
                            split(1 - s, st.out())
                            st.out.up(2)
                        return
                    with looped(act, 2, st.all(), [2, 1, 1, 4, 0, 0]) as i:
                        for s in slots:
                            split(1 - s, st.out())
                            st.duo.up()
                            st.out.up(2)

            G = F1
            act.wait_ge(consts, 1)
            act.wait_ge(raw_ready[0], 32)
            st.uses[0].up()
            act.activation(wh[:, 0], raw[:, 0], ACT.Copy).then_inc(hi_ready, 1)
            act.wait_ge(par_T, 1)
            act.activation(par[:, :], bank(7, PC_END), ACT.Copy).then_inc(par_ready, 1)
            act.wait_ge(par_ready, 1)
            act.mul(parh[:, :], par[:, 0:PC_NORM], 0.5).then_inc(par_ready, 1)
            for f in range(KT):
                act.wait_ge(lin_out, f + 1)
                act.activation(G["h"][:, f, :], bank(2 * (f % 3), TOK), ACT.Copy).then_inc(act_free, 1)
            act.wait_ge(act_free, KT)
            norm(xah)
            ffn((0, 1))

            act.wait_ge(dve_free, PRIMED + 3 * KT)
            act.wait_ge(x_ready, KT + FF // P)
            norm(xah)

            split(1, st.out())
            st.duo.up()
            act.wait_ge(t_pool, 1)
            act.wait_ge(t_in, 64)
            act.wait_ge(lin_out, st.out.up())
            act.activation(in_halves(tx[:, :]), halves(0, 48), ACT.Copy).then_inc(act_free, 1)
            st.act.up()
            act.activation(tcol[0:32, 4:5], tcol[0:32, 1:2], ACT.Exp).then_inc(t_act, 1)
            act.wait_ge(t_dve, 1)
            link(act.activation(tb[:, :], tb[:, :], ACT.Exp))
            act.activation(tb[:, :], tb[:, :], ACT.Ln, bias=ones[0:48, 0:1]).then_inc(t_act, 1)
            act.wait_ge(t_dve, 2)
            act.activation(tdec[:, :], tdec[:, :], ACT.Exp)
            act.activation(tstack[96:128, :], tsum[0:32, :], ACT.Exp).then_inc(t_act, 1)
            act.wait_ge(t_pe, 2)
            tk = bank(6, TILES * P).rearrange("p (t c) -> p t c", t=TILES)
            act.activation(tokt[:, 0:4, :], tk[:, 0:4, :], ACT.Copy)
            act.activation(tokt[0:80, 4, :], tk[0:80, 4, :], ACT.Copy)
            lt = bank(4, TILES * 64).rearrange("p (t c) -> p t c", t=TILES)
            act.activation(lft[:, 0:4, 0:48], lt[:, 0:4, 0:48], ACT.Copy)
            act.activation(lft[0:80, 4, 0:48], lt[0:80, 4, 0:48], ACT.Copy).then_inc(t_act, 1)

            def stage(i, n):
                k = n - 1
                if 0 <= k < JOBS:
                    t = k % 5
                    m, nb = ROWS[t], key_blocks(t)
                    act.wait_ge(p_T, i * JOBS + (k + 1))
                    if k >= 2:
                        act.wait_ge(pv_ready, i * JOBS + (k - 1))
                    act.activation(pt[:, k % 2, :].rearrange("p (b q) -> p b q", b=TILES)[:, 0:nb, 0:m],
                                   bank(6, TILES * P).rearrange("p (b q) -> p b q", b=TILES)[:, 0:nb, 0:m],
                                   ACT.Copy).then_inc(pt_ready, 1)
                if n < JOBS:
                    t = n % 5
                    m = ROWS[t]
                    act.wait_ge(mx_ready, i * JOBS + (n + 1))
                    if n >= 4:
                        act.wait_ge(o_ready, i * JOBS + (n - 3))
                    act.activation(scores(t), scores(t), ACT.Exp, bias=mx[0:m, n % 4:n % 4 + 1],
                                   accum_out=rsum[0:m, n % 4:n % 4 + 1]).then_inc(p_ready, 1)

            def mid(now, steps):
                for step in steps:
                    i, kind, g = now, step[0], step[1] if len(step) > 1 else 0
                    if kind in ("lin", "stages"):
                        for n in range(*step[-2:]):
                            stage(now, n)
                    if kind == "split" and g == 8:
                        split(MID_SLOT[0], st.out())
                    elif kind == "split":
                        split(1 - MID_SLOT[g], st.out(-1))
                    elif kind == "lin":
                        i = now + step[3]
                        k, t, n, g = MID[g], step[2], g, g // 3
                        b, m = 2 * ((OUT_AT[n] + t) % 2), ROWS[t]
                        act.wait_ge(lin_out, st.out.up())
                        if k == "z":
                            zb = (g + t) % 2
                            if steps is FIRST_STEPS and t == 0:
                                act.wait_ge(heads_left, 1)
                            act.wait_ge(z_used, i * 10 + (PRIMED + 5 * g + t - 1))
                            act.activation(zt[0:m, zb, :], bank(b, 256, m), ACT.Tanh, scale=0.5)
                            act.activation(zr[0:m, zb, :], bank(b, 256, m), ACT.Copy).then_inc(act_free, 1)
                        elif k in ("x", "bc"):
                            j = t + (2 if k == "bc" else 0)
                            if j == 0:
                                act.wait_ge(taps_done, i * 8 + (PRIMED + 4 * g))
                                act.wait_ge(cst_T, i * 2 + (PRIMED + g))
                            act.activation(xp[:, j, CS_:CS_ + SAMPLE], bank(b, SAMPLE), ACT.Copy)
                            act.activation(xp[:, j, CP_:CP_ + HALF - SAMPLE], bank(b, HALF - SAMPLE, at=SAMPLE), ACT.Copy)
                            act.activation(xp[:, j, CP_ + HALF - SAMPLE:CW], bank(b + 1, HALF), ACT.Copy).then_inc(act_free, 1)
                        elif k == "v":
                            act.activation(vt[0:m, t, :], bank(b, 256, m), ACT.Copy).then_inc(act_free, 1)
                        elif k == "q":
                            act.activation(in_halves(qz[0:HD, 2 * t, :]), halves(b)[0:HD], ACT.Copy)
                            act.activation(in_halves(qz[HD:P, 2 * t + 1, :]), halves(b)[HD:P], ACT.Copy).then_inc(act_free, 1)
                        else:
                            act.activation(in_halves(kT[:, t, :]), halves(b), ACT.Copy).then_inc(act_free, 1)
                        st.act.up()
                        if t == OUTS[k] - 1:
                            st.duo.up()
                    elif kind == "prep":
                        act.wait_ge(sraw_T, i * 2 + (PRIMED + g + 1))
                        act.wait_ge(yo_ready, i * 10 + (PRIMED + 5 * g))
                        act.wait_ge(s_ready, i * 10 + (PRIMED + 5 * g))
                        act.activation(sini[:, :], bank(6, 256), ACT.Copy).then_inc(sini_ready, 1)
                        act.wait_ge(brow_in, i * 32 + 16 * (g + 1))
                        act.activation(dec[:, :, 0], brow[:, :, SAMPLE - 1], ACT.Exp)
                        act.activation(dec[:, :, 1:4], brow[:, :, 255:512:128], ACT.Exp)
                        act.activation(dec[:, :, 4], brow[:, :, TOK - 1], ACT.Exp).then_inc(dec_ready, 1)
                    elif kind == "convA":
                        j = step[2]
                        act.wait_ge(hist_ready, i * 2 + (g + 1))
                        act.wait_ge(act_free, conv_in(i, g, j))
                        act.wait_ge(cv_done, i * 8 + (PRIMED + 4 * g + j - 1))
                        col = conv_tile(i, g, j)
                        act.activation(cvt[:, j % 2, :], xp[:, j, 0:CO], ACT.Identity, scale=parh[:, bass.ds(col, 1)],
                                       bias=parh[:, bass.ds(col + PC_CONVB, 1)]).then_inc(tap0_ready, 1)
                    elif kind == "convB":
                        j = step[2]
                        act.wait_ge(taps_done, i * 8 + (PRIMED + 4 * g + j + 1))
                        act.wait_ge(cv_done, i * 8 + (PRIMED + 4 * g + j))
                        act.activation(th[:, :], cvt[:, j % 2, :], ACT.Tanh).then_inc(tanh_ready, 1)
                    elif kind == "cst":
                        act.wait_ge(cst_T, i * 2 + (PRIMED + g + 1))
                        if g == 0:
                            act.wait_ge(heads_left, i + 1)
                        else:
                            act.wait_ge(yT_out, i * 32 + 16)
                        act.activation(cst[:, :, :], bank(6, 1024, 3).rearrange("p (k c) -> p k c", k=2), ACT.Copy).then_inc(cst_ready, 1)
                    elif kind == "s1":
                        t = step[2]
                        m, b, tau = ROWS[t], (t + g) % 2, 5 * g + t
                        act.wait_ge(xb_T, i * 10 + (tau + 1))
                        act.wait_ge(st_ready, i * 10 + (PRIMED + tau - 1))
                        act.activation(xbt[0:m, b, :], bank(4, 384, m), ACT.Copy).then_inc(xb_ready, 1)
                        act.wait_ge(seg_ready, i * 10 + (PRIMED + tau + 1))
                        act.activation(eb[0:m, :, 0:m], eb[0:m, :, 0:m], ACT.Exp).then_inc(e_ready, 1)
                    elif kind == "s2":
                        t = step[2]
                        m, tau = ROWS[t], 5 * g + t
                        act.wait_ge(yg_ready, i * 10 + (PRIMED + tau + 1))
                        act.wait_ge(sq_done, i * 10 + (PRIMED + tau))
                        act.activation(junk[0:m, :], yg[0:m, t, :], ACT.Square, accum_out=ssq[0:m, t:t + 1]).then_inc(sq_done, 1)
                    elif kind == "s3":
                        act.wait_ge(rv_ready, i * 2 + (g + 1))
                        act.activation(ssq[:, 0:4], ssq[:, 0:4], ACT.Sqrt)
                        act.activation(ssq[0:80, 4:5], ssq[0:80, 4:5], ACT.Sqrt).then_inc(rt_ready, 1)
                        for j, b in enumerate((6, 4)):
                            act.wait_ge(yT_T, i * 4 + (PRIMED + 2 * g + j + 1))
                            if j == 0:
                                act.wait_ge(cst_out, i * 192 + 96 * (g + 1))
                            act.activation(yT[:, j, :], bank(b, TOK), ACT.Copy,
                                           scale=par[:, bass.ds(i * 4 + (PC_SSMN + 2 * g + j), 1)]).then_inc(yT_ready, 1)
                        act.wait_ge(sf_T, i * 2 + (PRIMED + g + 1))
                        if g:
                            act.wait_ge(sto_out, i * 64 + 32)
                        act.activation(sto[:, :, :].rearrange("p a b -> p (a b)"), bank(6, 512), ACT.Copy).then_inc(sto_ready, 1)
                    elif kind == "enter":
                        act.wait_ge(ssd_left, i + 1)
                        for n in range(3):
                            act.wait_ge(ktok_T, i * 3 + (n + 1))
                            m, t1 = ROWS[2 * n], min(2 * n + 2, TILES)
                            act.activation(ktok[0:m, 2 * n:t1, :].rearrange("p t c -> p (t c)"), bank(4 + n, 256 * (t1 - 2 * n), m),
                                           ACT.Copy).then_inc(ktok_ready, 1)
                    elif kind == "cache":
                        for p in range(2):
                            act.wait_ge(kc_T, i * 2 + (p + 1))
                            act.activation(kcT[:, p, :], bank(7 - 3 * p, PAST), ACT.Copy).then_inc(kc_ready, 1)
                    elif kind == "leave":
                        for p in range(2):
                            act.wait_ge(o_T, i * 2 + (p + 1))
                            act.activation(oT[:, p, :], bank(4 + 2 * p, TOK), ACT.Copy).then_inc(oT_ready, 1)

            mid(0, FIRST_STEPS)
            with looped(act, 3, st.all() + [chain], MID_PER + [0]) as i:
                mid(i, LOOP_STEPS)
            mid(3, LAST_STEPS)

            G = G2
            stage = [Count(), Count()]

            def x_upper(dst, k, b):
                u = stage[b]
                u.up()
                act.wait_ge(stage_in[b], u.n * 16 if u.i is None else u.i * (16 * u.per) + u.n * 16)
                act.activation(dst[:, bass.ds(k, 1), :], G["full"][:, b:b + 1, :], ACT.Copy).then_inc(xhi_ready, 1)

            act.wait_ge(heads_left, 5)
            for part in range(2):
                with looped(act, 2, st.all() + stage, [2, 1, 1, 4, 4, 0, 1, 1]) as i:
                    for n, s in enumerate((1, 0)):
                        split(1 - s, st.out())
                        st.duo.up()
                        for u in range(2):
                            act.wait_ge(lin_out, st.out.up())
                            act.activation(in_halves(gates[:, bass.ds(i * 4 + (8 * part + 2 * n + u), 1), :]
                                                     .rearrange("p o t -> p (o t)")),
                                           halves(2 * (2 * n + u)), ACT.Tanh, scale=0.5).then_inc(act_free, 1)
                            st.act.up()
                        x_upper(G["xbh"], i * 2 + (4 * part + n), n)
            for part, dst in enumerate((xah, G["xbh"], xah, None)):
                if dst is not None:
                    act.wait_ge(lin_out, st.out())
                loads = part < 2
                with looped(act, 2, st.all() + stage, [2, 1, 1, 4, 0, 4] + [2 * loads, 2 * loads]) as i:
                    for n, s in enumerate((1, 0)):
                        split(1 - s, st.out())
                        st.duo.up()
                        for u in range(2):
                            m = i * 4 + (2 * n + u)
                            st.out.up()
                            st.dve.up()
                            if loads:
                                x_upper(dst, m, u)
                            elif dst is not None:
                                act.wait_ge(dve_free, PRIMED + 3 * KT + st.dve())
                                act.activation(dst[:, bass.ds(m, 1), :], G["h"][:, bass.ds(m, 1), :], ACT.Copy).then_inc(xhi_ready, 1)
            act.wait_ge(dve_free, PRIMED + 7 * KT)
            act.wait_ge(x_ready, X_MIX + 4 * KT)
            norm(xah)
            ffn((1, 0), last=True)
            act.wait_ge(dve_free, PRIMED + 7 * KT + 3 * KT)
            norm(None)
            for f in range(KT):
                act.wait_ge(fin_T, PRIMED + f + 1)
                pv = bank(2 * (f % 4), TILES * P).rearrange("p (t c) -> p t c", t=TILES)
                act.activation(ytok[:, 0:4, f * P:(f + 1) * P], pv[:, 0:4, :], ACT.Copy)
                act.activation(ytok[0:80, 4, f * P:(f + 1) * P], pv[0:80, 4, :], ACT.Copy).then_inc(fin_ready, 1)

        @block.vector
        def _(dve):
            st = Stream()
            chain, full, xhi, summed, nsplit = Count(), Count(), Count(), Count(PRIMED), Count()

            for s in (split_done, dve_free, taps_done, cv_done, seg_ready, cbm_ready, m_ready, s_ready, y_used, yg_ready, s_free):
                dve.sem_inc(s, PRIMED)

            def link(ins):
                ins.then_inc(dch, 1)
                dve.wait_ge(dch, chain.up())

            def split(slot):
                dve.wait_ge(hi_ready, nsplit.up())
                dve.tensor_tensor(wl[:, slot], raw[:, slot], wh[:, slot].bitcast(F32), ALU.subtract).then_inc(split_done, 1)

            def x_lower(dst, k, src, hi):
                dve.wait_ge(xhi_ready, xhi.up())
                dve.tensor_tensor(dst[:, bass.ds(k, 1), :], src, hi[:, bass.ds(k, 1), :].bitcast(F32), ALU.subtract)\
                    .then_inc(x_ready, 1)

            def norm(which, split_it=True):
                dve.wait_ge(sq_summed, summed.up(KT))
                link(dve.tensor_scalar(in_halves(G["rs"][:, :]), halves(0), 1.0 / D, EPS, ALU.mult, ALU.add))
                dve.reciprocal(G["rs"][:, :], G["rs"][:, :]).then_inc(rinv_ready, 1)
                dve.wait_ge(rs_ready, roots.up())
                with looped(dve, KT // 2, [full, xhi], [2, 2 * split_it]) as i:
                    for b in range(2):
                        k = i * 2 + b
                        if not split_it:
                            dve.wait_ge(fin_T, i * 2 + (PRIMED + b - 1))
                        dve.scalar_tensor_tensor(out=G["full"][:, b, :], in0=G["h"][:, bass.ds(k, 1), :].rearrange("p o t -> p (o t)"),
                                                 scalar=par[:, bass.ds(i * 2 + (PC_NORM + KT * which + b), 1)],
                                                 in1=G["rs"][:, :], op0=ALU.mult, op1=ALU.mult).then_inc(full_ready, 1)
                        full.up()
                        if split_it:
                            dve.wait_ge(full_ready, full())
                            x_lower(xal, k, G["full"][:, b:b + 1, :], xah)

            def add_to_h(m, b, again):
                dve.wait_ge(lin_out, st.out.up())
                if again:
                    dve.wait_ge(dve_free, st.dve(PRIMED + 1 - KT))
                hm = in_halves(G["h"][:, bass.ds(m, 1), :].rearrange("p o t -> p (o t)"))
                dve.scalar_tensor_tensor(out=hm, in0=halves(b), scalar=0.5, in1=hm, op0=ALU.mult, op1=ALU.add)\
                    .then_inc(dve_free, 1)
                st.dve.up()

            def ffn(slots, last=False):
                for t0, nt in THIRDS:
                    with looped(dve, nt // 2, st.all() + [full, xhi, nsplit, hid], [2, 1, 1, 4, 0, 0, 2, 2, 2, 2]) as i:
                        for n, s in enumerate(slots):
                            split(1 - s)
                            st.duo.up()
                            st.uses[s].up()
                            st.out.up(2)
                            dve.wait_ge(gated, hid.up())
                            dve.tensor_tensor(in_halves(G["full"][:, n, :]), in_halves(G["act"][:, :]), halves(4 * n + 2), ALU.mult)\
                                .then_inc(full_ready, 1)
                            full.up()
                            dve.wait_ge(full_ready, full())
                            x_lower(G["xbl"], i * 2 + n, G["full"][:, n:n + 1, :], G["xbh"])
                    if last and t0 + nt == FF // P:
                        for n, s in enumerate(slots * 2):
                            if n < 3:
                                split(1 - s)
                            for u in range(2):
                                add_to_h(2 * n + u, 2 * ((2 * n + u) % 4), True)
                        return
                    with looped(dve, 2, st.all() + [nsplit], [2, 1, 1, 4, 0, 4, 2]) as i:
                        for n, s in enumerate(slots):
                            split(1 - s)
                            st.duo.up()
                            st.uses[s].up()
                            for u in range(2):
                                add_to_h(i * 4 + (2 * n + u), 2 * (2 * n + u), t0 > 0)

            roots, hid = Count(), Count()
            dve.wait_ge(consts, 2)

            G = F1
            split(0)
            norm(NORM_FFN1)
            ffn((0, 1))
            dve.wait_ge(dve_free, PRIMED + 3 * KT)
            norm(NORM_MIX)

            split(1)
            st.duo.up()
            st.out.up()
            dve.wait_ge(act_free, KT + 1)
            link(dve.tensor_scalar(tx[:, :], tx[:, :], tcol[:, 0:1], tcol[:, 2:3], ALU.add, ALU.mult))
            dve.scalar_tensor_tensor(out=tb[:, :], in0=tx[:, :], scalar=-1.0, in1=tx[:, :], op0=ALU.mult, op1=ALU.min)\
                .then_inc(t_dve, 1)
            dve.wait_ge(t_act, 2)
            dve.tensor_scalar(tcol[0:32, 3:4], tcol[0:32, 4:5], -1.0, None, ALU.mult)
            link(dve.scalar_tensor_tensor(out=tx[:, :], in0=tx[:, :], scalar=0.0, in1=tb[:, :], op0=ALU.max, op1=ALU.add))
            link(dve.tensor_scalar(tsteps[:, :], tx[:, :], tcol[:, 3:4], None, ALU.mult))
            link(dve.tensor_tensor_scan(tsum[:, :], scanm[:, :], tsteps[:, :], 0.0, ALU.mult, ALU.add))
            for n, (c0, c1) in enumerate(CHUNKS):
                last = dve.tensor_scalar(tdec[:, c0:c1], tsum[0:32, c0:c1], -1.0, tsum[0:32, c1 - 1:c1], ALU.mult, ALU.add)
            last.then_inc(t_dve, 1)
            dve.tensor_copy(tstack[0:32, :], tsum[0:32, :])
            dve.tensor_copy(tstack[32:64, :], tx[0:32, :])
            dve.wait_ge(t_act, 3)
            dve.memset(tstack[96:128, SAMPLE:P], 0.0)
            dve.tensor_tensor(tstack[64:96, :], tdec[:, :], tx[0:32, :], ALU.mult).then_inc(t_dve, 1)
            link(dve.tensor_copy(tcm[:, :], tsum[32:48, 0:SAMPLE + META]))
            dve.wait_ge(t_pe, 1)
            link(dve.tensor_tensor_scan(tcs[:, 0:PAST], one16[:, :], bank(5, PAST, 16), tcm[:, SAMPLE + META - 1:SAMPLE + META],
                                        ALU.mult, ALU.add))
            dve.tensor_scalar(tcs[:, PAST:PAST + SAMPLE], tcm[:, 0:SAMPLE], tcs[:, PAST - 1:PAST], None, ALU.add)
            link(dve.tensor_copy(tcs[:, PAST + SAMPLE:], tcm[:, SAMPLE:]))
            dve.tensor_scalar(nb0[:, 0, 0:PAST + SAMPLE + META], tcs[:, :], -1.0, None, ALU.mult)
            dve.tensor_scalar(nb0[:, 1, PAST + SAMPLE:], tsum[32:48, SAMPLE:P], -1.0, None, ALU.mult)
            dve.tensor_scalar(nbp[:, :], tsum[32:48, SAMPLE:], -1.0, None, ALU.mult).then_inc(t_dve, 1)

            def heads4(ap, m):
                return ap.unsqueeze(2).to_broadcast([m, 4, HD])

            def by_head(ap):
                return ap.rearrange("p (h c) -> p h c", h=4)

            def stage(i, n):
                k = n - 2
                if k >= 0:
                    hh, t = k // 5, k % 5
                    m = ROWS[t]
                    dve.wait_ge(pv_ready, i * JOBS + (k + 1))
                    link(dve.reciprocal(rinv[0:m, k % 4:k % 4 + 1], rsum[0:m, k % 4:k % 4 + 1]))
                    dve.tensor_scalar(otok[0:m, t, HD * hh:HD * hh + HD], bank(7, HD, m, at=256),
                                      rinv[0:m, k % 4:k % 4 + 1], None, ALU.mult).then_inc(o_ready, 1)
                if n < JOBS:
                    hh, t = n // 5, n % 5
                    m, (before, w) = ROWS[t], score_span(t)
                    dve.wait_ge(bias_in[hh % 2], i * 96 + 48 * (hh // 2 + 1))
                    dve.wait_ge(qk_ready, i * JOBS + (n + 1))
                    if n >= 2:
                        dve.wait_ge(p_T, i * JOBS + (n - 1))
                    bs = bias[0:m, hh % 2, 0:PAST + P] if t == 0 else bias[0:m, hh % 2, PAST + P:PAST + P + w]
                    dve.scalar_tensor_tensor(out=scores(t), in0=bank(4, w, m, at=BANK - before), scalar=SCALE, in1=bs,
                                             op0=ALU.mult, op1=ALU.add).then_inc(s_free, 1)
                    dve.wait_ge(s_free, i * JOBS + (PRIMED + n + 1))
                    dve.tensor_reduce(mx[0:m, n % 4:n % 4 + 1], scores(t), AX.X, ALU.max, negate=True).then_inc(mx_ready, 1)

            def mid(i, steps):
                for step in steps:
                    kind, g = step[0], step[1] if len(step) > 1 else 0
                    if kind in ("lin", "stages"):
                        for n in range(*step[-2:]):
                            stage(i, n)
                    elif kind == "split":
                        split(MID_SLOT[0] if g == 8 else 1 - MID_SLOT[g])
                    elif kind == "convA":
                        j = step[2]
                        dve.wait_ge(tap0_ready, i * 8 + (4 * g + j + 1))
                        c = cvt[:, j % 2, :]
                        for tap in range(1, 4):
                            ins = dve.scalar_tensor_tensor(out=c, in0=xp[:, j, tap:tap + CO],
                                                           scalar=parh[:, bass.ds(conv_tile(i, g, j) + 32 * tap, 1)],
                                                           in1=c, op0=ALU.mult, op1=ALU.add)
                            if tap < 3:
                                link(ins)
                        ins.then_inc(taps_done, 1)
                    elif kind == "convB":
                        j = step[2]
                        dve.wait_ge(tanh_ready, i * 8 + (4 * g + j + 1))
                        if j == 0:
                            dve.wait_ge(yd_ready, i * 10 + (PRIMED + 5 * g))
                            dve.wait_ge(heads_left, i + 1)
                        for c0, c1, to in ((0, SAMPLE, 0), (CP_ - CS_, CO, SAMPLE)):
                            ins = dve.scalar_tensor_tensor(out=cv[:, j, to:to + c1 - c0], in0=th[:, c0:c1], scalar=1.0,
                                                           in1=cvt[:, j % 2, c0:c1], op0=ALU.add, op1=ALU.mult)
                        ins.then_inc(cv_done, 1)
                    elif kind == "s1":
                        t = step[2]
                        m, tau, c = ROWS[t], 5 * g + t, t * P
                        if t == 0:
                            dve.wait_ge(brow_in, i * 32 + 16 * (g + 1))
                        dve.wait_ge(m_ready, i * 10 + (PRIMED + tau))
                        for r in range(4):
                            ins = dve.tensor_scalar(eb[0:m, r, 0:m], brow[0:m, r, c:c + m],
                                                    tokt[0:m, t, bass.ds(i * 8 + (4 * g + r), 1)], 0.0, ALU.subtract, ALU.min)
                        ins.then_inc(seg_ready, 1)
                        dve.wait_ge(cb_ready, i * 10 + (tau + 1))
                        dve.tensor_tensor(cbm[0:m, 0:m], bank(5, m, m), mask01[0:m, min(t, 1), 0:m], ALU.mult).then_inc(cbm_ready, 1)
                        dve.wait_ge(cbm_ready, i * 10 + (PRIMED + tau + 1))
                        dve.wait_ge(e_ready, i * 10 + (tau + 1))
                        dve.wait_ge(yd_ready, i * 10 + (PRIMED + tau - 1))
                        dve.tensor_tensor(mb[0:m, tau % 2, :, 0:m], eb[0:m, :, 0:m],
                                          cbm[0:m, 0:m].unsqueeze(1).to_broadcast([m, 4, m]), ALU.mult).then_inc(m_ready, 1)
                    elif kind == "s2":
                        t = step[2]
                        m, tau = ROWS[t], 5 * g + t
                        dve.wait_ge(st_ready, i * 10 + (PRIMED + tau + 1))
                        if t == 0:
                            dve.wait_ge(dec_ready, i * 2 + (PRIMED + g + 1))
                            dve.wait_ge(sini_ready, i * 2 + (g + 1))
                            dve.wait_ge(sf_T, i * 2 + (g + PRIMED))
                            for r in range(4):
                                h = slice(HD * r, HD * r + HD)
                                dve.scalar_tensor_tensor(out=sfin[:, h], in0=sini[:, h], scalar=dec[:, r, 0:1],
                                                         in1=bank(7, HD, at=HD * r), op0=ALU.mult, op1=ALU.add)
                            dve.tensor_copy(spr[:, 0, :], bank(7, 256, at=256)).then_inc(s_ready, 1)
                        else:
                            dve.wait_ge(s_ready, i * 10 + (PRIMED + tau))
                            for r in range(4):
                                h = slice(HD * r, HD * r + HD)
                                ins = dve.scalar_tensor_tensor(out=spr[:, t % 2, h], in0=spr[:, (t - 1) % 2, h],
                                                               scalar=dec[:, r, t:t + 1], in1=bank(7, HD, at=HD * r),
                                                               op0=ALU.mult, op1=ALU.add)
                            ins.then_inc(s_ready, 1)
                        dve.wait_ge(yd_ready, i * 10 + (PRIMED + tau + 1))
                        dve.wait_ge(yg_ready, i * 10 + (PRIMED + tau))
                        dve.tensor_tensor(by_head(y1[0:m, :]), by_head(bank(6, 256, m)),
                                          heads4(tokt[0:m, t, bass.ds(i * 8 + (96 + 4 * g), 4)], m), ALU.mult)
                        dve.wait_ge(xd_ready, i * 10 + (tau + 1))
                        dve.tensor_tensor(y2[0:m, :], bank(6, 256, m, at=256), xsk[0:m, tau % 2, :], ALU.add).then_inc(y_used, 1)
                        dve.wait_ge(y_used, i * 10 + (PRIMED + tau + 1))
                        link(dve.tensor_tensor(y1[0:m, :], y1[0:m, :], y2[0:m, :], ALU.add))
                        if t == 0:
                            dve.wait_ge(z_used, i * 10 + (PRIMED + 5 * g + 5))
                            dve.wait_ge(yT_T, i * 4 + (PRIMED + 2 * g))
                        dve.scalar_tensor_tensor(out=yg[0:m, t, :], in0=y1[0:m, :], scalar=0.5, in1=zs[0:m, g, t, :],
                                                 op0=ALU.mult, op1=ALU.mult).then_inc(yg_ready, 1)
                    elif kind == "s3":
                        dve.wait_ge(sq_done, i * 10 + (PRIMED + 5 * g + 5))
                        parts = (ssq[:, 0:4], ssq[0:80, 4:5])
                        for a in parts:
                            ins = dve.tensor_scalar(a, a, 1.0 / 256, EPS, ALU.mult, ALU.add)
                        link(ins)
                        for a in parts:
                            ins = dve.reciprocal(a, a)
                        ins.then_inc(rv_ready, 1)
                        dve.wait_ge(rt_ready, i * 2 + (g + 1))
                        for t in range(TILES):
                            a = yg[0:ROWS[t], t, :]
                            ins = dve.tensor_scalar(a, a, ssq[0:ROWS[t], t:t + 1], None, ALU.mult)
                        ins.then_inc(yn_ready, 1)
                    elif kind == "enter":
                        dve.wait_ge(ssd_left, i + 1)

            mid(0, FIRST_STEPS)
            with looped(dve, 3, [chain, nsplit], [48, 9]) as i:
                mid(i, LOOP_STEPS)
            mid(3, LAST_STEPS)
            st.out.up(4 * MID_OUTS)

            G = G2
            for part in range(2):
                with looped(dve, 2, [nsplit, xhi, st.out], [2, 2, 4]) as i:
                    for n, s in enumerate((1, 0)):
                        split(1 - s)
                        st.out.up(2)
                        x_lower(G["xbl"], i * 2 + (4 * part + n), G["full"][:, n:n + 1, :], G["xbh"])
            dve.wait_ge(act_free, KT + 1 + 4 * MID_OUTS + 2 * KT)
            for part, (hi, lo) in enumerate(((xah, xal), (G["xbh"], G["xbl"]), (xah, xal), (None, None))):
                if part == 3:
                    dve.wait_ge(h_back, 16)
                with looped(dve, 2, [nsplit, xhi, st.out, st.dve, chain], [2, 4 * (part < 3), 4, 4, 4 * (part in (1, 2))]) as i:
                    for n, s in enumerate((1, 0)):
                        split(1 - s)
                        for u in range(2):
                            m, b = i * 4 + (2 * n + u), 2 * (2 * n + u)
                            if part == 3:
                                add_to_h(m, b, False)
                                continue
                            dve.wait_ge(lin_out, st.out.up())
                            hm = in_halves(G["h"][:, bass.ds(m, 1), :].rearrange("p o t -> p (o t)"))
                            gt = in_halves(gates[:, bass.ds(m + 8 * (part > 0), 1), :].rearrange("p o t -> p (o t)"))
                            to = hm if part == 0 else in_halves(G["act"][:, :])
                            if part:
                                dve.wait_ge(dve_free, st.dve(PRIMED))
                            ins = dve.scalar_tensor_tensor(out=to, in0=gt, scalar=1.0, in1=halves(b), op0=ALU.add, op1=ALU.mult)
                            if part:
                                link(ins)
                                ins = dve.tensor_tensor(hm, hm, to, ALU.add)
                            ins.then_inc(dve_free, 1)
                            st.dve.up()
                            if part == 2:
                                dve.wait_ge(dve_free, st.dve(PRIMED))
                            src = G["h"][:, bass.ds(m, 1), :] if part == 2 else G["full"][:, u:u + 1, :]
                            x_lower(lo, m, src, hi)

            dve.wait_ge(dve_free, PRIMED + 7 * KT)
            norm(NORM_FFN2)
            ffn((1, 0), last=True)
            dve.wait_ge(dve_free, PRIMED + 7 * KT + 3 * KT)
            norm(NORM_FINAL, split_it=False)

        @block.tensor
        def _(pe):
            st = Stream()
            nsq, xr, full = Count(), Count(), Count()

            for s in (sq_summed, cst_T, sraw_T, st_ready, yo_ready, yd_ready, yT_T, sf_T, fin_T):
                pe.sem_inc(s, PRIMED)

            def duo_split():
                pe.wait_ge(split_done, st.duo(PRIMED + 1))
                st.duo.up()

            def unit(slot, j, xh, xl, nk, b, before_last=None, between=lambda k: None):
                for k in range(nk):
                    if before_last is not None and k == nk - 1:
                        before_last()
                    for w, x in ((wh, xh), (wh, xl), (wl, xh)):
                        for a in range(2):
                            ins = pe.matmul(bank(b + a, HALF), w[:, slot, k, j * P:(j + 1) * P], x[:, k, a * HALF:(a + 1) * HALF],
                                            start=(k == 0 and w is wh and x is xh), stop=(k == nk - 1 and w is wl))
                    if k == nk - 1:
                        ins.then_inc(lin_out, 1)
                    between(k)
                st.out.up()

            def token_tile(slot, t, b, between):
                m = ROWS[t]
                for k in range(KT):
                    for w, x in ((wh, xah), (wh, xal), (wl, xah)):
                        ins = pe.matmul(bank(b, 256, m), x[:, k, t * P:t * P + m], w[:, slot, k, :],
                                        start=(k == 0 and w is wh and x is xah), stop=(k == KT - 1 and w is wl))
                    if k == KT - 1:
                        ins.then_inc(lin_out, 1)
                    between(k)
                st.out.up()

            def norm():
                def square(b, first=False, last=False):
                    pe.wait_ge(sq_ready, nsq.up())
                    for a in range(2):
                        ins = pe.matmul(bank(a, HALF), ones[:, :], G["full"][:, b, a * HALF:(a + 1) * HALF],
                                        start=first, stop=last)
                    ins.then_inc(sq_summed, 1)

                square(0, first=True)
                square(1)
                with looped(pe, KT // 2 - 2, [nsq], [2]) as i:
                    for b in range(2):
                        square(b)
                square(0)
                square(1, last=True)

            def ffn(slots, last=False):
                for t0, nt in THIRDS:
                    with looped(pe, nt // 2, st.all() + [full], [2, 0, 0, 4, 0, 0, 2]) as i:
                        for n, s in enumerate(slots):
                            duo_split()
                            pe.wait_ge(full_ready, full(-1))
                            pe.wait_ge(dve_free, st.dve(PRIMED - 2 * (n == 0)))
                            unit(s, 0, xah, xal, KT, 4 * n)
                            unit(s, 1, xah, xal, KT, 4 * n + 2)
                            full.up()
                    xr.up(nt)
                    with looped(pe, 2, st.all(), [2, 0, 0, 4, 0, 4]) as i:
                        for n, s in enumerate(slots):
                            duo_split()
                            for u in range(2):
                                pe.wait_ge(x_ready, xr() - 1)
                                pe.wait_ge(dve_free, st.dve(PRIMED - 1))
                                unit(s, u, G["xbh"], G["xbl"], nt, 2 * (2 * n + u),
                                     before_last=lambda: pe.wait_ge(x_ready, xr()))
                                st.dve.up()

            def turn(out, in_):
                k = in_.shape[0]
                return pe.transpose(out, in_, ident[0:k, 0:k])

            G = F1
            pe.wait_ge(consts, 2)
            pe.wait_ge(par_in, 16 * 9)
            turn(bank(7, P), prow[:, 0, :])
            turn(bank(7, 80, at=P), prow[0:80, 1, :])
            turn(bank(7, 96, at=208), prow[0:96, 2, :]).then_inc(par_T, 1)
            for f in range(KT):
                if f % 4 == 0:
                    pe.wait_ge(x_in[f // 4], 16 * 5)
                if f >= 3:
                    pe.wait_ge(act_free, f - 2)
                for t in range(TILES):
                    ins = turn(bank(2 * (f % 3), ROWS[t], at=t * P), xin[0:ROWS[t], t, (f % 4) * P:(f % 4 + 1) * P])
                ins.then_inc(lin_out, 1)
            norm()
            full.up(KT)
            xr.up(KT)
            pe.wait_ge(x_ready, xr())
            ffn((0, 1))
            norm()
            full.up(KT)
            xr.up(KT)
            pe.wait_ge(x_ready, xr())

            duo_split()
            unit(0, 0, xah, xal, KT, 0)
            pe.wait_ge(t_in, 16 * 4)
            for a in range(4):
                ins = turn(bank(5, P, 16, at=a * P), clf[:, a, :])
            ins.then_inc(t_pe, 1)
            pe.wait_ge(t_dve, 3)
            pe.wait_ge(t_act, 3)
            for t in range(TILES):
                m = ROWS[t]
                turn(bank(6, P, m, at=t * P), tstack[:, t * P:t * P + m])
                ins = turn(bank(4, 48, m, at=64 * t), tsteps[:, t * P:t * P + m])
            ins.then_inc(t_pe, 1)
            st.act.up()

            def give(i, k):
                hh, t = k // 5, k % 5
                m, nb = ROWS[t], key_blocks(t)
                pe.wait_ge(pt_ready, i * JOBS + (k + 1))
                if k == 0:
                    pe.wait_ge(vc_in, i * 16 + 16)
                for b in range(nb):
                    c = slice(HD * hh, HD * hh + HD)
                    if t == 0:
                        kw, v = P, vc[:, b, c] if b < 4 else vt[:, 0, c]
                    else:
                        kw = P if b < 4 else ROWS[4]
                        v = vt[0:kw, b, c]
                    ins = pe.matmul(bank(7, HD, m, at=256), pt[0:kw, k % 2, b * P:b * P + m], v, start=(b == 0), stop=(b == nb - 1))
                ins.then_inc(pv_ready, 1)

            def score(i, n):
                hh, t = n // 5, n % 5
                p = hh // 2
                m, (before, w) = ROWS[t], score_span(t)
                if n == 0:
                    pe.wait_ge(ktok_ready, i * 3 + 3)
                    pe.wait_ge(kc_ready, i * 2 + 2)
                else:
                    pe.wait_ge(s_free, i * JOBS + (PRIMED + n))
                q = qz[:, hh, t * P:t * P + m]
                pe.matmul(bank(4, before, m, at=BANK - before), q, kcT[:, p, :] if t == 0 else kT[:, p, SAMPLE:t * P],
                          start=True, stop=True)
                pe.matmul(bank(5, m, m), q, kT[:, p, t * P:t * P + m], start=True, stop=False)
                pe.matmul(bank(5, m, m), identb[0:m, 0:m], negmask[0:m, min(t, 1), 0:m], start=False, stop=True).then_inc(qk_ready, 1)

            def turn_probs(i, k):
                t = k % 5
                m = ROWS[t]
                pe.wait_ge(p_ready, i * JOBS + (k + 1))
                if k == 1:
                    pe.wait_ge(pz_ready, i + 1)
                if k >= 1:
                    pe.wait_ge(pt_ready, i * JOBS + k)
                    pe.wait_ge(o_ready, i * JOBS + k)
                for b in range(key_blocks(t)):
                    kw = P if b < 4 or t == 0 else ROWS[4]
                    src = p0[:, b * P:b * P + P] if t == 0 else pp[0:m, t % 2, b * P:b * P + kw]
                    ins = turn(bank(6, m, kw, at=b * P), src)
                ins.then_inc(p_T, 1)

            def half_stage(i, h):
                n = h // 2
                if h % 2:
                    if 0 <= n - 1 < JOBS:
                        turn_probs(i, n - 1)
                    return
                if n >= 2:
                    give(i, n - 2)
                if n < JOBS:
                    score(i, n)

            def mid(i, steps):
                for step in steps:
                    kind, g = step[0], step[1] if len(step) > 1 else 0
                    if kind == "stages":
                        for h in range(2 * step[1], 2 * step[2]):
                            half_stage(i, h)
                    elif kind == "lin":
                        n, t = step[1], step[2]
                        halves_in = range(2 * step[4], 2 * step[5])
                        every = KT // max(len(halves_in), 1)

                        def between(k, halves_in=halves_in, every=every):
                            if len(halves_in) and k % every == every - 1:
                                half_stage(i, halves_in[k // every])
                        k, b = MID[n], 2 * ((OUT_AT[n] + t) % 2)
                        if t == 0:
                            duo_split()
                        if n == 0 and t == 0:
                            pe.wait_ge(act_free, st.act())
                            pe.wait_ge(t_act, 4)
                        else:
                            pe.wait_ge(act_free, st.act(-1))
                        st.act.up()
                        if k in ("z", "v"):
                            token_tile(MID_SLOT[n], t, b, between)
                        else:
                            unit(MID_SLOT[n], t, xah, xal, KT, b, between=between)
                    elif kind == "prep":
                        pe.wait_ge(oT_ready, i * 2 + PRIMED)
                        pe.wait_ge(sto_ready, i * 2 + (PRIMED + g))
                        pe.wait_ge(sraw_in, i * 32 + 16 * (g + 1))
                        turn(bank(6, P), sraw[:, 0, :])
                        turn(bank(6, P, at=P), sraw[:, 1, :]).then_inc(sraw_T, 1)
                    elif kind == "cst":
                        pe.wait_ge(act_free, conv_in(i, g, 3))
                        pe.wait_ge(sini_ready, i * 2 + (g + 1))
                        for j in range(4):
                            turn(bank(6, P, 3, at=j * P), xp[:, j, CS_ + SAMPLE - 3:CS_ + SAMPLE])
                            ins = turn(bank(7, P, 3, at=j * P), xp[:, j, CW - 3:CW])
                        ins.then_inc(cst_T, 1)
                    elif kind == "s1":
                        t = step[2]
                        m, tau, c = ROWS[t], 5 * g + t, slice(t * P, t * P + ROWS[t])
                        if t == 0:
                            pe.wait_ge(cv_done, i * 8 + (PRIMED + 4 * g + 4))
                            pe.wait_ge(cst_ready, i * 2 + (PRIMED + g + 1))
                        pe.wait_ge(xb_ready, i * 10 + (PRIMED + tau))
                        for j in range(3):
                            ins = turn(bank(4, P, m, at=j * P), cv[:, j, c])
                        ins.then_inc(xb_T, 1)
                        pe.wait_ge(cbm_ready, i * 10 + (PRIMED + tau))
                        pe.matmul(bank(5, m, m), cv[:, 2, c], cv[:, 3, c], start=True, stop=True).then_inc(cb_ready, 1)
                    elif kind == "s2":
                        t = step[2]
                        m, tau, c = ROWS[t], 5 * g + t, slice(t * P, t * P + ROWS[t])
                        b = tau % 2
                        if t:
                            pe.wait_ge(s_ready, i * 10 + (PRIMED + tau))
                        pe.wait_ge(y_used, i * 10 + (PRIMED + tau))
                        pe.matmul(bank(6, 256, m), cv[:, 3, c], spr[:, (t - 1) % 2, :] if t else sini[:, :],
                                  start=True, stop=True).then_inc(yo_ready, 1)
                        pe.wait_ge(xd_ready, i * 10 + (tau + 1))
                        pe.wait_ge(xb_ready, i * 10 + (PRIMED + tau + 1))
                        pe.wait_ge(s_ready, i * 10 + (PRIMED + tau))
                        if t == 0:
                            pe.matmul(bank(7, 256), xbt[0:64, b, 256:384], xdd[0:64, b, :], start=True, stop=True)\
                                .then_inc(st_sample, 1)
                            pe.wait_ge(st_sample, i * 2 + (g + 1))
                            pe.matmul(bank(7, 256, at=256), xbt[64:128, b, 256:384], xdd[64:128, b, :], start=True, stop=True)\
                                .then_inc(st_ready, 1)
                        else:
                            pe.matmul(bank(7, 256), xbt[0:m, b, 256:384], xdd[0:m, b, :], start=True, stop=True)\
                                .then_inc(st_ready, 1)
                        pe.wait_ge(m_ready, i * 10 + (PRIMED + tau + 1))
                        for r in range(4):
                            ins = pe.matmul(bank(6, HD, m, at=256 + HD * r), mb[0:m, b, r, 0:m], xd[0:m, b, HD * r:HD * r + HD],
                                            start=True, stop=True)
                        ins.then_inc(yd_ready, 1)
                    elif kind == "s3":
                        pe.wait_ge(yn_ready, i * 2 + (g + 1))
                        pe.wait_ge(y_used, i * 10 + (PRIMED + 5 * g + 5))
                        pe.wait_ge(s_ready, i * 10 + (PRIMED + 5 * g + 5))
                        for j, b in enumerate((6, 4)):
                            for t in range(TILES):
                                ins = turn(bank(b, ROWS[t], at=t * P), yg[0:ROWS[t], t, j * P:(j + 1) * P])
                            ins.then_inc(yT_T, 1)
                        pe.wait_ge(yT_ready, i * 4 + (PRIMED + 2 * g + 1))
                        for k, s in enumerate((sfin[:, :], spr[:, 0, :])):
                            for j in range(2):
                                ins = turn(bank(6, P, at=256 * k + j * P), s[:, j * P:(j + 1) * P])
                        ins.then_inc(sf_T, 1)
                    elif kind == "enter":
                        pe.wait_ge(act_free, i * MID_OUTS + (KT + 1 + OUT_AT[8]))
                        pe.wait_ge(sto_ready, i * 2 + (PRIMED + 2))
                        pe.wait_ge(yT_ready, i * 4 + (PRIMED + 4))
                        for n in range(3):
                            for t in range(2 * n, min(2 * n + 2, TILES)):
                                for p in range(2):
                                    ins = turn(bank(4 + n, P, ROWS[t], at=t % 2 * 256 + p * P), kT[:, p, t * P:t * P + ROWS[t]])
                            ins.then_inc(ktok_T, 1)
                    elif kind == "cache":
                        pe.wait_ge(kc_in, i * 16 + 16)
                        pe.wait_ge(ktok_ready, i * 3 + 1)
                        for p in range(2):
                            for a in range(4):
                                ins = turn(bank(7 - 3 * p, P, at=a * P), kcr[:, a, p * P:(p + 1) * P])
                            ins.then_inc(kc_T, 1)
                    elif kind == "leave":
                        pe.wait_ge(o_ready, i * JOBS + JOBS)
                        for p in range(2):
                            for t in range(TILES):
                                ins = turn(bank(4 + 2 * p, ROWS[t], at=t * P), otok[0:ROWS[t], t, p * P:(p + 1) * P])
                            ins.then_inc(o_T, 1)

            mid(0, FIRST_STEPS)
            with looped(pe, 3, st.all(), [9, 0, 0, MID_OUTS, MID_OUTS, 0]) as i:
                mid(i, LOOP_STEPS)
            mid(3, LAST_STEPS)

            G = G2
            pe.wait_ge(oT_ready, PRIMED + 8)
            pe.wait_ge(s_free, PRIMED + 4 * JOBS)
            for part in range(2):
                with looped(pe, 2, st.all(), [2, 0, 0, 4, 4, 0]) as i:
                    for n, s in enumerate((1, 0)):
                        duo_split()
                        for u in range(2):
                            pe.wait_ge(act_free, st.act(-1))
                            unit(s, u, xah, xal, KT, 2 * (2 * n + u))
                            st.act.up()
            pe.wait_ge(act_free, st.act())
            for xh, xl in ((G["xbh"], G["xbl"]), (xah, xal), (G["xbh"], G["xbl"]), (xah, xal)):
                xr.up(KT)
                pe.wait_ge(x_ready, xr())
                with looped(pe, 2, st.all(), [2, 0, 0, 4, 0, 4]) as i:
                    for n, s in enumerate((1, 0)):
                        duo_split()
                        for u in range(2):
                            pe.wait_ge(dve_free, st.dve(PRIMED - 1))
                            unit(s, u, xh, xl, KT, 2 * (2 * n + u))
                            st.dve.up()
            norm()
            full.up(KT)
            xr.up(KT)
            pe.wait_ge(x_ready, xr())
            ffn((1, 0))
            norm()
            for f in range(KT):
                pe.wait_ge(full_ready, full.up())
                if f >= 4:
                    pe.wait_ge(fin_ready, f - 3)
                for t in range(TILES):
                    ins = turn(bank(2 * (f % 4), P, ROWS[t], at=t * P), G["full"][:, f % 2, t * P:t * P + ROWS[t]])
                ins.then_inc(fin_T, 1)


_INS = ["x_prompt", "x_sample", "cache_k", "cache_v", "cache_logf", "state_ssm", "state_conv", "meta_tokens",
        "norm_ffn1", "ffn1_w_in", "ffn1_w_out", "norm_mix", "w_in", "conv_w", "conv_b", "dt_bias", "a_log", "d_skip",
        "f_bias", "ssm_norm", "w_br_ssm", "w_br_attn", "w_out", "norm_ffn2", "ffn2_w_in", "ffn2_w_out", "norm_final"]
_OUTS = [(1, SEQ, D), (1, SAMPLE, D), (1, 1, PROMPT, HEADS, HD), (1, 1, PROMPT, HEADS, HD), (1, 1, PROMPT, HEADS),
         (1, 1, SSM_HEADS, HD, NSTATE), (1, 1, 3, D_CONV), (1, 1, SAMPLE, HEADS, HD), (1, 1, SAMPLE, HEADS, HD),
         (1, 1, SAMPLE, HEADS), (1, 1, SSM_HEADS, HD, NSTATE), (1, 1, 3, D_CONV)]


def kernel(**inputs):
    import numpy as _np
    import concourse.bacc as _bacc
    from concourse import mybir as _mybir
    from concourse.bass_utils import run_bass_kernel_spmd as _run

    nc = _bacc.Bacc("TRN2", target_bir_lowering=False, num_devices=1)
    arrays, args = {}, []
    for name in _INS:
        a = _np.ascontiguousarray(inputs[name])
        arrays[f"in_{name}_dram"] = a
        args.append(nc.dram_tensor(f"in_{name}_dram", a.shape, _mybir.dt.from_np(a.dtype), kind="ExternalInput").ap())
    for i, shape in enumerate(_OUTS):
        args.append(nc.dram_tensor(f"out_{i}_dram", shape, _mybir.dt.float32, kind="ExternalOutput").ap())
    fox_ssd_hybrid_kernel(nc, *args)
    r = _run(nc, [arrays], core_ids=[0])
    return tuple(r.results[0][f"out_{i}_dram"] for i in range(len(_OUTS)))
```

```python
from contextlib import ExitStack, contextmanager

import concourse.bass as bass
from concourse import mybir

F32 = mybir.dt.float32
F32R = mybir.dt.float32r
BF16 = mybir.dt.bfloat16
ALU = mybir.AluOpType
ACT = mybir.ActivationFunctionType
AX = mybir.AxisListType

P = 128
D = 1024
SAMPLE = 64
META = 16
SEQ = 512
PROMPT = META + SEQ
TOK = SAMPLE + PROMPT
PAST = 512
KT = D // P
FF = 2816
HEADS = 16
HD = 64
SSM_HEADS = 32
GROUPS = 8
NSTATE = 128
D_SSM = 2048
D_CONV = 4096
OFF_XBC = D_SSM
OFF_DT = OFF_XBC + D_CONV
OFF_Q = OFF_DT + SSM_HEADS
OFF_K = OFF_Q + D
OFF_V = OFF_K + D
OFF_F = OFF_V + D
OFF_GS = OFF_F + HEADS
OFF_GA = OFF_GS + D
EPS = 1e-6
NEG = -1e30
SCALE = float(HD) ** -0.5

TILES = 5
ROWS = [128, 128, 128, 128, TOK - 512]
HALF = TOK // 2
BANK = 512
PC_CONVW, PC_CONVB, PC_NORM, PC_SSMN, PC_STATE, PC_END = 0, 128, 160, 192, 208, 304
NORM_FFN1, NORM_MIX, NORM_FFN2, NORM_FINAL = range(4)
CS_ = 3
CP_ = CS_ + SAMPLE + 3
CW = CP_ + PROMPT
CO = CW - 3
CHUNKS = [(0, 64), (64, 128), (128, 256), (256, 384), (384, 512), (512, TOK)]
THIRDS = [(0, 8), (8, 8), (16, 6)]


class Count:

    def __init__(self, start=0):
        self.n, self.i, self.per = start, None, 0

    def __call__(self, more=0):
        v = self.n + more
        return v if self.i is None or self.per == 0 else self.i * self.per + v

    def up(self, k=1):
        self.n += k
        return self()


@contextmanager
def looped(eng, iters, counts, pers):
    base = [c.n for c in counts]
    with eng.Fori(0, iters) as i:
        for c, p in zip(counts, pers):
            c.i, c.per = i, p
        yield i
        moved = [c.n - b for c, b in zip(counts, base)]
        assert moved == list(pers), (moved, list(pers))
    for c, b, p in zip(counts, base, pers):
        c.i, c.per, c.n = None, 0, b + p * iters


class Stream:

    def __init__(self):
        self.duo = Count()
        self.uses = [Count(), Count()]
        self.out = Count(KT)
        self.act = Count(KT)
        self.dve = Count()

    def all(self):
        return [self.duo, *self.uses, self.out, self.act, self.dve]


PRIMED = 2

MID = ["z", "x", "bc", "z", "x", "bc", "v", "q0", "q1", "k"]
MID_SLOT = [1, 0] * 5
OUTS = {"z": TILES, "v": TILES, "x": 2, "bc": 2, "q0": 1, "q1": 1, "k": 2}
MID_OUTS = sum(OUTS[k] for k in MID)
OUT_AT = [sum(OUTS[k] for k in MID[:n]) for n in range(len(MID))]
MID_PER = [10, 5, 5, MID_OUTS, MID_OUTS, 0]
JOBS = 4 * TILES


STAGES = JOBS + 2


def pieces(duos, ahead=0):
    return [("lin", n, t, ahead, ()) for n in duos for t in range(OUTS[MID[n]])]


def flat(steps):
    for step in steps:
        if step[0] == "lin":
            yield from (inner for _, inner in step[4])
        yield step


QUARTERS = {1: [(0, 0), (0, 2), (0, 3), (0, 5)], 2: [(0, 3), (0, 6), (1, 1), (1, 3)], TILES: [(0, 2), (1, 2), (2, 2), (3, 2)]}


def with_splits(steps):
    out = []
    for step in steps:
        if step[0] == "lin":
            n, t = step[1:3]
            quarters = tuple((3 * k + 2, ("split", n, c, t)) for c, (at, k) in enumerate(QUARTERS[OUTS[MID[n]]]) if at == t)
            step = step[:4] + (tuple(sorted(quarters + step[4], key=lambda inner: inner[0])), )
        out.append(step)
    return out


def first_pieces(ahead, within=lambda n, t: ()):
    order = []
    for piece in pieces([0, 1, 2], ahead):
        n, t = piece[1:3]
        if (n, t) == (2, 0):
            order += [("convA", 0, 0, ahead), ("convA", 0, 1, ahead)]
        if (n, t) == (2, 1):
            order += [("convB", 0, 0, ahead), ("convA", 0, 2, ahead), ("convB", 0, 1, ahead)]
        order.append(piece[:4] + (within(n, t),))
    return with_splits(order)


def ssd_window(duos, g):
    before = {
        0: [("prep", g), ("convA", g, 3, 0), ("convB", g, 2, 0), ("cst", g), ("convB", g, 3, 0)],
        6: [("rows", 1, 0)] * (g == 0),
        7: [("convA", 1, 0, 0), ("convA", 1, 1, 0)] * (g == 0),
        8: [("convB", 1, 0, 0), ("convA", 1, 2, 0), ("convB", 1, 1, 0)] * (g == 0) + [("fetch",)] * (g == 1),
    }
    within = {
        1: ((5, ("s1", g, 0)), ),
        2: ((0, ("s1", g, 1)), (4, ("s2", g, 0))),
        3: ((0, ("s1", g, 2)), (4, ("s2", g, 1))),
        4: ((0, ("s1", g, 3)), (4, ("s2", g, 2))),
        5: ((0, ("s1", g, 4)), (2, ("s2", g, 3)), (6, ("s2", g, 4))),
        6: ((7, ("s3", g)), ),
        7: ((3, ("s4", g)), ),
    }
    order = []
    for at, piece in enumerate(pieces(duos)):
        order += before.get(at, []) + [piece[:4] + (tuple((3 * k + 2, inner) for k, inner in within.get(at, ())),)]
    return with_splits(order)


def heads_window():
    half = 0
    taken = {}
    for (n, t), more in zip([(0, 2), (0, 3), (0, 4), (1, 0), (1, 1), (2, 0), (2, 1)], (4, 6, 6, 8, 8, 8, 4)):
        room = 3 * KT // (1 if (n, t) != (2, 1) else 2)
        taken[n, t] = tuple(((m // 2 * 2 + 2) * room // more - (1 if m % 2 else 2), ("half", half + m)) for m in range(more))
        half += more
    assert half == 2 * STAGES
    taken[0, 0] = ((11, ("enter",)), )
    taken[2, 1] += ((20, ("leave",)), )
    order = first_pieces(1, lambda n, t: taken.get((n, t), ()))
    at = [step[1:3] for step in order].index((0, 2))
    return [("rows", 0, 1)] + order[:at] + [("cache",)] + order[at:]


FIRST_STEPS = [("rows", 0, 0)] + first_pieces(0)
SSD_STEPS = ssd_window([3, 4, 5], 0) + ssd_window([6, 7, 8, 9], 1)
LOOP_STEPS = SSD_STEPS + heads_window()
LAST_STEPS = SSD_STEPS + [("enter",), ("cache",)] + [("half", h) for h in range(2 * STAGES)] + [("leave",)]


def split_cols(n):
    return P if MID[(n + 1) % len(MID)] in ("q0", "q1") else 256


def lin_bank(n, t):
    return 3 if n == t == 0 else 2 * ((OUT_AT[n] + t) % 2)


def freed(i, n, t):
    return i * MID_OUTS + (KT + 1 + OUT_AT[n] + t + 1)


def conv_in(i, g, j):
    return freed(i, 3 * g + 1 + j // 2, j % 2)


def conv_tile(i, g, j):
    return i * 4 + (2 * g + j) if j < 2 else i * 2 + (2 * KT + (j - 2) * GROUPS + g)


def score_span(t):
    before = PAST if t == 0 else t * P - SAMPLE
    return before, before + ROWS[t]


def key_blocks(t):
    return TILES if t == 0 else t + 1


def fox_ssd_hybrid_kernel(nc, x_prompt, x_sample, cache_k, cache_v, cache_logf, state_ssm, state_conv,
                          meta_tokens, norm_ffn1, ffn1_w_in, ffn1_w_out, norm_mix, w_in, conv_w, conv_b,
                          dt_bias, a_log, d_skip, f_bias, ssm_norm, w_br_ssm, w_br_attn, w_out, norm_ffn2,
                          ffn2_w_in, ffn2_w_out, norm_final,
                          y_prompt, y_sample, k_prompt, v_prompt, logf_prompt, ssm_prompt, conv_prompt,
                          k_sample, v_sample, logf_sample, ssm_sample, conv_sample):
    ctx = ExitStack()
    with ctx:
        def sb(name, shape, dt=F32, scope=ctx):
            return scope.enter_context(nc.sbuf_tensor(name, shape, dt))

        def sem(name):
            return ctx.enter_context(nc.semaphore(name))

        h_spill = nc.dram_tensor("h_spill", [P, KT * TOK], F32).ap()
        oa_spill = nc.dram_tensor("oa_spill", [KT, P, TOK], F32).ap()
        os_spill = nc.dram_tensor("os_spill", [2 * KT, P, TOK], F32).ap()
        acs_rows = nc.dram_tensor("acs_rows", [SSM_HEADS, TOK], F32).ap()
        bias0_rows = nc.dram_tensor("bias0_rows", [HEADS, 2, PAST + P], F32).ap()
        biasp_rows = nc.dram_tensor("biasp_rows", [HEADS, PROMPT], F32).ap()

        raw = sb("raw", [P, 2, KT, 256])
        wh = sb("wh", [P, 2, KT, 256], F32R)
        wl = sb("wl", [P, 2, KT, 256], F32R)
        xah = sb("xah", [P, KT, TOK], F32R)
        xal = sb("xal", [P, KT, TOK], F32R)
        ident = sb("ident", [P, P])
        ones = sb("ones", [P, P])
        identb = sb("identb", [P, P], BF16)
        negmask = sb("negmask", [P, 2, P], BF16)
        mask01 = sb("mask01", [P, 2, P])
        par = sb("par", [P, PC_END])
        parh = sb("parh", [P, PC_NORM])
        dsk = sb("dsk", [P, SSM_HEADS])
        tokt = sb("tokt", [P, TILES, P])
        scanm = sb("scanm", [48, TOK])

        ps = ctx.enter_context(nc.psum_tensor("ps", [P, 8 * BANK], F32))

        passed = sem("passed")

        def bank(b, n, rows=P, at=0):
            return ps[0:rows, b * BANK + at:b * BANK + at + n]

        def halves(b, rows=P):
            return ps[0:rows, b * BANK:(b + 2) * BANK].rearrange("p (a n) -> p a n", a=2)[:, :, 0:HALF]

        def in_halves(ap):
            return ap.rearrange("p (a n) -> p a n", a=2)

        def ffn_buffers(scope, tag):
            return {"h": sb("h" + tag, [P, KT, TOK], F32, scope),
                    "xbh": sb("xbh" + tag, [P, KT, TOK], F32R, scope),
                    "xbl": sb("xbl" + tag, [P, KT, TOK], F32R, scope),
                    "act": sb("act" + tag, [P, TOK], F32, scope),
                    "full": sb("full" + tag, [P, 2, TOK], F32, scope),
                    "rs": sb("rs" + tag, [P, TOK], F32, scope)}

        with ExitStack() as s:
            F1 = ffn_buffers(s, "1")
            xin = sb("xin", [P, TILES, 512], F32, s)
            prow = sb("prow", [P, 3, P], F32, s)
        with ExitStack() as s:
            tcol = sb("tcol", [48, 8], F32, s)
            tx = sb("tx", [48, TOK], F32, s)
            tb = sb("tb", [48, TOK], F32, s)
            tsteps = sb("tsteps", [48, TOK], F32, s)
            tsum = sb("tsum", [48, TOK], F32, s)
            tdec = sb("tdec", [32, TOK], F32, s)
            tstack = sb("tstack", [P, TOK], F32, s)
            tcm = sb("tcm", [16, SAMPLE + META], F32, s)
            tcs = sb("tcs", [16, PAST + SAMPLE + META], F32, s)
            nb0 = sb("nb0", [16, 2, PAST + P], F32, s)
            nbp = sb("nbp", [16, PROMPT], F32, s)
            clf = sb("clf", [P, 4, 16], F32, s)
            lft = sb("lft", [P, TILES, 64], F32, s)
            one16 = sb("one16", [16, PAST], F32, s)
        with ExitStack() as s:
            qz = sb("qz", [P, 4, TOK], F32, s)
            kT = sb("kT", [P, 2, TOK], F32, s)
            vt = sb("vt", [P, TILES, 256], F32, s)
            kcT = sb("kcT", [P, 2, PAST], F32, s)
            vc = sb("vc", [P, 4, 256], F32, s)
            xp = sb("xp", [P, 4, CW], F32, s)
            cvt = sb("cvt", [P, 2, CO], F32, s)
            th = sb("th", [P, CO], F32, s)
            brow = sb("brow", [P, 4, TOK], F32, s)
            zs = sb("zs", [P, 2, TILES, 256], F32, s)
            zt = sb("zt", [P, 2, 256], F32, s)
            zr = sb("zr", [P, 2, 256], F32, s)
            sini = sb("sini", [P, 256], F32, s)
            sraw = sb("sraw", [P, 2, P], F32, s)
            dec = sb("dec", [P, 4, TILES], F32, s)
            cv = sb("cv", [P, 4, TOK], F32, s)
            with ExitStack() as g:
                xbt = sb("xbt", [P, 2, 384], F32, g)
                xd = sb("xd", [P, 2, 256], F32, g)
                xdd = sb("xdd", [P, 2, 256], F32, g)
                xsk = sb("xsk", [P, 2, 256], F32, g)
                eb = sb("eb", [P, 4, P], F32, g)
                mb = sb("mb", [P, 2, 4, P], F32, g)
                cbm = sb("cbm", [P, P], F32, g)
                y1 = sb("y1", [P, 256], F32, g)
                y2 = sb("y2", [P, 256], F32, g)
                yg = sb("yg", [P, TILES, 256], F32, g)
                junk = sb("junk", [P, 256], F32, g)
                ssq = sb("ssq", [P, 8], F32, g)
                sfin = sb("sfin", [P, 256], F32, g)
                spr = sb("spr", [P, 2, 256], F32, g)
                sto = sb("sto", [P, 4, P], F32, g)
                yT = sb("yT", [P, 2, TOK], F32, g)
                cst = yT[0:3, :, 0:512]
            with ExitStack() as g:
                bias = sb("bias", [P, 2, PAST + P + PROMPT], F32, g)
                p0 = sb("p0", [P, PAST + P], F32, g)
                pp = sb("pp", [P, 2, TOK], F32, g)
                pt = sb("pt", [P, 2, TILES * P], F32, g)
                kcr = pt[:, :, :].rearrange("p a b -> p (a b)")[:, 0:PAST * 2].rearrange("p (a c) -> p a c", a=4)
                otok = sb("otok", [P, TILES, 256], F32, g)
                ktok = sb("ktok", [P, TILES, 256], F32, g)
                oT = pp
                mx = sb("mx", [P, 4], F32, g)
                rsum = sb("rsum", [P, 4], F32, g)
                rinv = sb("rinv", [P, 4], F32, g)
        with ExitStack() as s:
            G2 = ffn_buffers(s, "2")
            gates = sb("gates", [P, 2 * KT, TOK], F32, s)
            ytok = gates[:, 0:9, :].rearrange("p a b -> p (a b)")[:, 0:TILES * D].rearrange(
                "p (t c) -> p t c", t=TILES)

        x_in = [sem("x_in0"), sem("x_in1")]
        par_in, consts, par_T, par_ready = sem("par_in"), sem("consts"), sem("par_T"), sem("par_ready")
        raw_ready = [sem("raw_ready0"), sem("raw_ready1")]
        hi_ready, split_done = sem("hi_ready"), sem("split_done")
        lin_out, act_free, dve_free = sem("lin_out"), sem("act_free"), sem("dve_free")
        gated, full_ready, xhi_ready, x_ready = sem("gated"), sem("full_ready"), sem("xhi_ready"), sem("x_ready")
        sq_ready, sq_summed, rinv_ready, rs_ready = sem("sq_ready"), sem("sq_summed"), sem("rinv_ready"), sem("rs_ready")
        hi_part = sem("hi_part")
        h_out, h_back = sem("h_out"), sem("h_back")
        dch, ach, gch = sem("dch"), sem("ach"), sem("gch")
        t_pool, t_dve, t_act, t_pe, t_in, t_out = (sem("t_" + n) for n in ("pool", "dve", "act", "pe", "in", "out"))
        heads_left, ssd_left = sem("heads_left"), sem("ssd_left")
        z_used, hist_ready = sem("z_used"), sem("hist_ready")
        tap0_ready, taps_done, tanh_ready, cv_done = sem("tap0_ready"), sem("taps_done"), sem("tanh_ready"), sem("cv_done")
        brow_in, sraw_in, sraw_T, sini_ready = sem("brow_in"), sem("sraw_in"), sem("sraw_T"), sem("sini_ready")
        dec_ready, cst_T, cst_ready, cst_out = sem("dec_ready"), sem("cst_T"), sem("cst_ready"), sem("cst_out")
        xb_T, xb_ready, cb_ready, cbm_ready = sem("xb_T"), sem("xb_ready"), sem("cb_ready"), sem("cbm_ready")
        seg_ready, e_ready, m_ready, xd_ready = sem("seg_ready"), sem("e_ready"), sem("m_ready"), sem("xd_ready")
        st_ready, s_ready, yo_ready, yd_ready = sem("st_ready"), sem("s_ready"), sem("yo_ready"), sem("yd_ready")
        y_used, yg_ready, sq_done, rv_ready = sem("y_used"), sem("yg_ready"), sem("sq_done"), sem("rv_ready")
        rt_ready, yn_ready, yT_T, yT_ready, yT_out = (sem(n) for n in ("rt_ready", "yn_ready", "yT_T", "yT_ready", "yT_out"))
        st_sample = sem("st_sample")
        sf_T, sto_ready, sto_out = sem("sf_T"), sem("sto_ready"), sem("sto_out")
        kc_in, vc_in, kc_T, kc_ready = sem("kc_in"), sem("vc_in"), sem("kc_T"), sem("kc_ready")
        ktok_T, ktok_ready, k_out, v_out = sem("ktok_T"), sem("ktok_ready"), sem("k_out"), sem("v_out")
        bias_in = [sem("bias_in0"), sem("bias_in1")]
        qk_ready, s_free, mx_ready, p_ready, p_T = (sem(n) for n in ("qk_ready", "s_free", "mx_ready", "p_ready", "p_T"))
        pt_ready, pv_ready, o_ready, pz_ready = sem("pt_ready"), sem("pv_ready"), sem("o_ready"), sem("pz_ready")
        o_T, oT_ready, oT_out = sem("o_T"), sem("oT_ready"), sem("oT_out")
        stage_in = [sem("stage_in0"), sem("stage_in1")]
        fin_T, fin_ready, y_out = sem("fin_T"), sem("fin_ready"), sem("y_out")

        def rows_of(w):
            return w[0].rearrange("(k p) n -> p k n", p=P)

        win1, wout1, winp = rows_of(ffn1_w_in), rows_of(ffn1_w_out), rows_of(w_in)
        win2, wout2 = rows_of(ffn2_w_in), rows_of(ffn2_w_out)
        wbs, wba, wo = rows_of(w_br_ssm), rows_of(w_br_attn), rows_of(w_out)

        def state_rows(s, g):
            return s[0, 0].rearrange("(g h) p n -> g (h p) n", h=4)[bass.ds(g, 1)].rearrange(
                "g (j q) n -> q (g j) n", q=P)

        def scores(t):
            before, n = score_span(t)
            return p0[:, 0:n] if t == 0 else pp[0:ROWS[t], t % 2, SAMPLE:SAMPLE + n]

        X_MIX = KT + FF // P + KT

        SPLITS_MIX = FF // P + 3 * 4 + 2

        block = ctx.enter_context(nc.Block())

        @block.sync
        def _(sp):
            st = Stream()

            def load(slot, parts):
                sp.wait_ge(split_done, st.duo(PRIMED - 1))
                for dst, src in parts:
                    sp.dma_start(dst, src).then_inc(raw_ready[slot], 16)
                st.duo.up()
                st.uses[slot].up()

            def r(slot, k0, k1, c0, c1):
                return raw[:, slot, k0:k1, c0:c1]

            def wide(s, w, c):
                load(s, [(r(s, 0, 4, 0, 256), w[:, 0:4, bass.ds(c, 256)]),
                         (r(s, 4, KT, 0, 256), w[:, 4:KT, bass.ds(c, 256)])])

            def pair(s, w, c, apart):
                load(s, [(r(s, 0, KT, 0, P), w[:, :, bass.ds(c, P)]),
                         (r(s, 0, KT, P, 256), w[:, :, bass.ds(c + apart, P)])])

            def ffn(win, wout, slots):
                for t0, nt in THIRDS:
                    with looped(sp, nt // 2, st.all(), [2, 1, 1, 0, 0, 0]) as i:
                        for n, s in enumerate(slots):
                            pair(s, win, i * 256 + (t0 + n) * P, FF)
                    with looped(sp, 2, st.all(), [2, 1, 1, 0, 0, 0]) as i:
                        for n, s in enumerate(slots):
                            c, m = i * 512 + n * 256, nt // 2
                            load(s, [(r(s, 0, m, 0, 256), wout[:, t0:t0 + m, bass.ds(c, 256)]),
                                     (r(s, m, nt, 0, 256), wout[:, t0 + m:t0 + nt, bass.ds(c, 256)])])

            ffn(win1, wout1, (0, 1))
            load(0, [(r(0, 0, KT, 0, SSM_HEADS), winp[:, :, OFF_DT:OFF_DT + SSM_HEADS]),
                     (r(0, 0, KT, SSM_HEADS, 48), winp[:, :, OFF_F:OFF_F + HEADS])])

            def load_mid(i, n):
                if n >= len(MID):
                    i, n = i + 1, n - len(MID)
                kind, s, g = MID[n], MID_SLOT[n], n // 3
                if kind == "z":
                    wide(s, winp, i * 512 + g * 256)
                elif kind == "x":
                    wide(s, winp, i * 512 + (OFF_XBC + g * 256))
                elif kind == "bc":
                    pair(s, winp, i * 256 + (OFF_XBC + D_SSM + g * P), GROUPS * NSTATE)
                elif kind in ("q0", "q1"):
                    c = bass.ds(i * 256 + (OFF_Q + P * (kind == "q1")), P)
                    load(s, [(r(s, 0, 4, 0, P), winp[:, 0:4, c]), (r(s, 4, KT, 0, P), winp[:, 4:KT, c])])
                else:
                    wide(s, winp, i * 256 + {"k": OFF_K, "v": OFF_V}[kind])

            def load_gate(n):
                wide((1, 0)[n % 2], winp, OFF_GA + n * 256)

            def cached(cache, c):
                return cache[0, 0].rearrange("(a p) h d -> p a (h d)", p=P)[:, :, bass.ds(c, 256)]

            def load_bias(i, hh):
                b, hd = hh % 2, i * 4 + hh
                for q in range(2):
                    sp.dma_start(bias[64 * q:64 * q + 64, b, 0:PAST + P],
                                 bias0_rows[bass.ds(hd, 1), q, :].to_broadcast([64, PAST + P])).then_inc(bias_in[b], 16)
                sp.dma_start(bias[:, b, PAST + P:], biasp_rows[bass.ds(hd, 1), :].to_broadcast([P, PROMPT]))\
                    .then_inc(bias_in[b], 16)

            def store_rows(to_sample, to_prompt, c, src, s):
                to_s = to_sample[0, 0].rearrange("t h d -> t (h d)")[:, bass.ds(c, 256)]
                to_p = to_prompt[0, 0].rearrange("t h d -> t (h d)")[:, bass.ds(c, 256)]
                sp.dma_start(to_s, src[0:64, 0, :]).then_inc(s, 16)
                sp.dma_start(to_p[0:64], src[64:128, 0, :]).then_inc(s, 16)
                sp.dma_start(to_p[64:448].rearrange("(t p) c -> p t c", p=P), src[:, 1:4, :]).then_inc(s, 16)
                sp.dma_start(to_p[448:528], src[0:80, 4, :]).then_inc(s, 16)

            def mid(now, steps):
                for step in flat(steps):
                    i, kind, g = now, step[0], step[1] if len(step) > 1 else 0
                    if kind == "split" and step[2] == 3:
                        if steps is LAST_STEPS and g + 3 >= len(MID):
                            load_gate(g + 3 - len(MID))
                        else:
                            load_mid(now + (steps is LOOP_STEPS and g < 3), g + 3)
                    elif kind == "rows":
                        i = now + step[2]
                        sp.wait_ge(seg_ready, i * 10 + (PRIMED + 5 * g))
                        sp.wait_ge(dec_ready, i * 2 + (PRIMED + g))
                        sp.wait_ge(sraw_T, i * 2 + (PRIMED + g))
                        sp.dma_start(brow[:, :, :], acs_rows[bass.ds(i * 8 + 4 * g, 4), :].partition_broadcast(P))\
                            .then_inc(brow_in, 16)
                        sp.dma_start(sraw[:, :, :], state_rows(state_ssm, i * 2 + g)).then_inc(sraw_in, 16)
                    elif kind == "cst":
                        sp.wait_ge(cst_ready, i * 2 + (PRIMED + g + 1))
                        for k, dst in enumerate((conv_sample[0, 0], conv_prompt[0, 0])):
                            for c0, n, off in ((0, 256, i * 512 + 256 * g), (256, P, i * 256 + (D_SSM + P * g)),
                                               (384, P, i * 256 + (D_SSM + D + P * g))):
                                sp.dma_start(dst[:, bass.ds(off, n)], cst[:, k, c0:c0 + n]).then_inc(cst_out, 16)
                    elif kind == "s4":
                        sp.wait_ge(yT_ready, i * 4 + (PRIMED + 2 * g + 2))
                        sp.dma_start(os_spill[bass.ds(i * 4 + 2 * g, 2)].rearrange("j p t -> p j t"), yT[:, :, :])\
                            .then_inc(yT_out, 16)
                        sp.wait_ge(sto_ready, i * 2 + (PRIMED + g + 1))
                        for k, dst in enumerate((ssm_sample, ssm_prompt)):
                            sp.dma_start(state_rows(dst, i * 2 + g), sto[:, 2 * k:2 * k + 2, :]).then_inc(sto_out, 16)
                    elif kind == "fetch":
                        sp.wait_ge(yT_out, i * 32 + 32)
                        sp.wait_ge(sto_out, i * 64 + 64)
                        sp.wait_ge(cst_out, i * 192 + 192)
                        sp.sem_inc(ssd_left, 1)
                        sp.dma_start(kcr[:, :, :], cached(cache_k, i * 256)).then_inc(kc_in, 16)
                        load_bias(i, 0)
                        load_bias(i, 1)
                        sp.dma_start(vc[:, :, :], cached(cache_v, i * 256)).then_inc(vc_in, 16)
                    elif kind == "cache":
                        sp.wait_ge(act_free, i * MID_OUTS + (KT + 1 + OUT_AT[7]))
                        store_rows(v_sample, v_prompt, i * 256, vt, v_out)
                        sp.wait_ge(ktok_ready, i * 3 + 3)
                        store_rows(k_sample, k_prompt, i * 256, ktok, k_out)
                    elif kind == "half" and g in (10, 20):
                        hh = g // 10 + 1
                        sp.wait_ge(s_free, i * JOBS + (PRIMED + 5 * (hh - 1)))
                        load_bias(i, hh)
                    elif kind == "leave":
                        sp.wait_ge(oT_ready, i * 2 + (PRIMED + 2))
                        sp.dma_start(oa_spill[bass.ds(i * 2, 2)].rearrange("j p t -> p j t"), oT[:, :, :]).then_inc(oT_out, 16)
                        sp.wait_ge(k_out, i * 64 + 64)
                        sp.wait_ge(v_out, i * 64 + 64)
                        sp.wait_ge(oT_out, i * 16 + 16)
                        sp.sem_inc(heads_left, 1)

            for n in range(3):
                load_mid(0, n)
            sp.wait_ge(heads_left, 1)
            mid(0, FIRST_STEPS)
            with looped(sp, 3, st.all(), MID_PER[:3] + [0, 0, 0]) as i:
                mid(i, LOOP_STEPS)
            mid(3, LAST_STEPS)
            load_gate(3)
            for w, off in ((winp, OFF_GS), (wba, 0), (wbs[:, 0:KT], 0), (wbs[:, KT:2 * KT], 0), (wo, 0)):
                with looped(sp, 2, st.all(), [2, 1, 1, 0, 0, 0]) as i:
                    for n, s in enumerate((1, 0)):
                        wide(s, w, i * 512 + (off + n * 256))
            ffn(win2, wout2, (1, 0))

            for f in (KT // 2, KT):
                c = slice((f - KT // 2) * P, f * P)
                sp.wait_ge(fin_ready, f)
                sp.dma_start(y_prompt[0, 48:432, c].rearrange("(t p) c -> p t c", p=P), ytok[:, 1:4, c]).then_inc(y_out, 16)
                sp.dma_start(y_sample[0, :, c], ytok[0:64, 0, c]).then_inc(y_out, 16)
                sp.dma_start(y_prompt[0, 0:48, c], ytok[80:128, 0, c]).then_inc(y_out, 16)
                sp.dma_start(y_prompt[0, 432:512, c], ytok[0:80, 4, c]).then_inc(y_out, 16)
            sp.wait_ge(y_out, 128)

        @block.gpsimd
        def _(pool):
            chain = Count()

            def link(ins):
                ins.then_inc(gch, 1)
                pool.wait_ge(gch, chain.up())

            def settle():
                pool.sem_inc(passed, 1)

            pool.sem_inc(z_used, PRIMED)

            for half in range(2):
                c = slice(512 * half, 512 * half + 512)
                if half:
                    pool.wait_ge(lin_out, 4)
                for dst, src in ((xin[0:64, 0, :], x_sample[0, :, c]), (xin[64:80, 0, :], meta_tokens[:, c]),
                                 (xin[80:128, 0, :], x_prompt[0, 0:48, c]),
                                 (xin[:, 1:4, :], x_prompt[0, 48:432, c].rearrange("(t p) c -> p t c", p=P)),
                                 (xin[0:80, 4, :], x_prompt[0, 432:512, c])):
                    pool.dma_start(dst, src).then_inc(x_in[half], 16)
                if half:
                    continue
                link(pool.memset(ident[:, :], 0.0))
                link(pool.affine_select(out=ident[:, :], in_=ident[:, :], compare_op=ALU.not_equal, fill=1.0,
                                        base=0, pattern=[[-1, P]], channel_multiplier=1))
                pool.tensor_copy(identb[:, :], ident[:, :])
                pool.memset(ones[:, :], 1.0).then_inc(consts, 1)
                link(pool.memset(negmask[:, :, :], 0.0))
                link(pool.affine_select(out=negmask[:, :, :], in_=negmask[:, :, :], compare_op=ALU.is_ge,
                                        fill=NEG, base=0, pattern=[[0, 2], [-1, P]], channel_multiplier=1))
                link(pool.memset(negmask[0:64, 0, 64:80], 0.0))
                link(pool.memset(mask01[:, :, :], 1.0))
                link(pool.affine_select(out=mask01[:, :, :], in_=mask01[:, :, :], compare_op=ALU.is_ge,
                                        fill=0.0, base=0, pattern=[[0, 2], [1, P]], channel_multiplier=-1))
                link(pool.memset(mask01[0:64, 0, 64:128], 0.0))
                link(pool.memset(scanm[:, :], 1.0))
                for c0, _ in CHUNKS:
                    pool.memset(scanm[0:32, c0:c0 + 1], 0.0)
                pool.memset(scanm[32:48, 64:65], 0.0).then_inc(consts, 1)

            pool.wait_ge(dve_free, PRIMED + 3 * KT)
            pool.dma_start(h_spill, F1["h"][:, :, :].rearrange("p k t -> p (k t)")).then_inc(h_out, 16)
            pool.wait_ge(h_out, 16)
            pool.wait_ge(x_ready, X_MIX)
            for dst, src in ((clf[:, :, :], cache_logf[0, 0].rearrange("(a p) h -> p a h", p=P)),
                             (tcol[0:32, 0:1], dt_bias.rearrange("o h -> h o")),
                             (tcol[32:48, 0:1], f_bias.rearrange("o h -> h o")),
                             (tcol[0:32, 1:2], a_log.rearrange("o h -> h o"))):
                pool.dma_start(dst, src).then_inc(t_in, 16)
            pool.memset(one16[:, :], 1.0)
            pool.memset(tcol[0:32, 2:3], 1.0)
            link(pool.memset(tcol[32:48, 2:3], -1.0))
            pool.memset(tcol[:, 3:4], -1.0)
            pool.memset(nb0[:, 1, 0:PAST + SAMPLE], NEG)
            pool.memset(nb0[:, 0, PAST + SAMPLE + META:], NEG).then_inc(t_pool, 1)
            pool.wait_ge(t_dve, 4)
            pool.dma_start(acs_rows, tsum[0:32, :]).then_inc(t_out, 16)
            pool.dma_start(bias0_rows, nb0[:, :, :]).then_inc(t_out, 16)
            pool.dma_start(biasp_rows, nbp[:, :]).then_inc(t_out, 16)
            pool.wait_ge(t_act, 4)
            pool.dma_start(logf_sample[0, 0], lft[0:64, 0, 32:48]).then_inc(t_out, 16)
            pool.dma_start(logf_prompt[0, 0, 0:64], lft[64:128, 0, 32:48]).then_inc(t_out, 16)
            pool.dma_start(logf_prompt[0, 0, 64:448].rearrange("(t p) h -> p t h", p=P), lft[:, 1:4, 32:48]).then_inc(t_out, 16)
            pool.dma_start(logf_prompt[0, 0, 448:528], lft[0:80, 4, 32:48]).then_inc(t_out, 16)
            pool.wait_ge(t_out, 16 * 7)
            for hh in range(4):
                r = HD * (1 - hh % 2)
                link(pool.memset(qz[r:r + HD, hh, :], 0.0))
            pool.sem_inc(heads_left, 1)

            nsplit, hparts = Count(SPLITS_MIX), Count()

            def split_quarter(slot, c, cols):
                if c < 3:
                    pool.wait_ge(hi_part, hparts.up())
                else:
                    pool.wait_ge(hi_ready, nsplit.up())
                k = slice(2 * c, 2 * c + 2)
                ins = pool.tensor_tensor(wl[:, slot, k, 0:cols], raw[:, slot, k, 0:cols], wh[:, slot, k, 0:cols].bitcast(F32),
                                         ALU.subtract)
                if c == 3:
                    ins.then_inc(split_done, 1)

            def mid(now, steps):
                for step in flat(steps):
                    i, kind, g = now, step[0], step[1] if len(step) > 1 else 0
                    if kind == "split":
                        split_quarter(1 - MID_SLOT[g], step[2], split_cols(g))
                    if kind == "lin" and MID[g] == "z":
                        i, t, g = now + step[3], step[2], g // 3
                        if t == 0 and step[3]:
                            pool.wait_ge(yg_ready, now * 10 + (PRIMED + 5))
                        m, b = ROWS[t], (g + t) % 2
                        pool.wait_ge(act_free, freed(i, step[1], t))
                        settle()
                        link(pool.tensor_scalar(zt[0:m, b, :], zt[0:m, b, :], 1.0, None, ALU.add))
                        pool.tensor_tensor(zs[0:m, g, t, :], zt[0:m, b, :], zr[0:m, b, :], ALU.mult).then_inc(z_used, 1)
                    elif kind == "lin" and MID[g] == "x" and step[2] == 0:
                        i, g = now + step[3], g // 3
                        pool.wait_ge(taps_done, i * 8 + (PRIMED + 4 * g))
                        pool.wait_ge(cst_T, i * 2 + (PRIMED + g))
                        settle()
                        hist = par[:, PC_STATE:PC_STATE + 96].rearrange("p (r t) -> p t r", r=3)
                        pool.memset(xp[:, :, CS_ + SAMPLE:CP_], 0.0)
                        pool.tensor_copy(xp[:, 0:2, 0:3], hist[:, bass.ds(i * 4 + 2 * g, 2), :])
                        pool.tensor_copy(xp[:, 2:3, 0:3], hist[:, bass.ds(i * 2 + (16 + g), 1), :])
                        pool.tensor_copy(xp[:, 3:4, 0:3], hist[:, bass.ds(i * 2 + (24 + g), 1), :]).then_inc(hist_ready, 1)
                    elif kind == "s1":
                        t = step[2]
                        m, b, hs, tau = ROWS[t], (t + g) % 2, i * 8 + 4 * g, PRIMED + 5 * g + t
                        xv = xbt[0:m, b, 0:256].rearrange("p (h c) -> p h c", h=4)
                        pool.wait_ge(xb_ready, i * 10 + (tau + 1))
                        pool.wait_ge(yd_ready, i * 10 + (tau - 1))
                        pool.wait_ge(y_used, i * 10 + (tau - 1))
                        for dst, src in ((xd, tokt[0:m, t, bass.ds(hs + 32, 4)]), (xdd, tokt[0:m, t, bass.ds(hs + 64, 4)]),
                                         (xsk, dsk[0:m, bass.ds(hs, 4)])):
                            last = pool.tensor_tensor(dst[0:m, b, :].rearrange("p (h c) -> p h c", h=4), xv,
                                                      src.unsqueeze(2).to_broadcast([m, 4, HD]), ALU.mult)
                        last.then_inc(xd_ready, 1)
                    elif kind == "fetch":
                        pool.wait_ge(ssd_left, i + 1)
                        settle()
                        pool.memset(pp[:, :, 0:SAMPLE], 0.0).then_inc(pz_ready, 1)

            mid(0, FIRST_STEPS)
            with looped(pool, 3, [chain, nsplit, hparts], [2 * TILES, 10, 30]) as i:
                mid(i, LOOP_STEPS)
            mid(3, LAST_STEPS)

            pool.wait_ge(heads_left, 5)
            n = X_MIX
            for src, t0 in ((oa_spill, 0), (os_spill, 0), (os_spill, KT)):
                with looped(pool, 4, [], []) as i:
                    for b in range(2):
                        pool.wait_ge(x_ready, i * 2 + (n + b - 1))
                        settle()
                        pool.dma_start(G2["full"][:, b, :], src[bass.ds(i * 2 + (t0 + b), 1)].rearrange("o p t -> p (o t)"))\
                            .then_inc(stage_in[b], 16)
                n += KT
            pool.wait_ge(x_ready, n + KT)
            pool.dma_start(G2["h"][:, :, :].rearrange("p k t -> p (k t)"), h_spill).then_inc(h_back, 16)

        @block.scalar
        def _(act):
            st = Stream()
            chain, full, sq, rinvs, summed = Count(), Count(), Count(), Count(), Count()
            xhi = Count()

            for s in (gated, sq_done, dec_ready, cst_ready, xb_ready, yT_ready, sto_ready, oT_ready):
                act.sem_inc(s, PRIMED)

            def link(ins):
                ins.then_inc(ach, 1)
                act.wait_ge(ach, chain.up())

            def split(slot, free_at, cols=256):
                act.wait_ge(raw_ready[slot], split_uses(slot))
                act.wait_ge(lin_out, free_at)
                act.activation(wh[:, slot, :, 0:cols], raw[:, slot, :, 0:cols], ACT.Copy).then_inc(hi_ready, 1)

            def split_quarter(slot, c, free_at, cols):
                if c == 0:
                    act.wait_ge(raw_ready[slot], split_uses(slot))
                    act.wait_ge(lin_out, free_at)
                k = slice(2 * c, 2 * c + 2)
                act.activation(wh[:, slot, k, 0:cols], raw[:, slot, k, 0:cols], ACT.Copy).then_inc(hi_ready if c == 3 else hi_part, 1)

            def split_uses(slot):
                st.uses[slot].up()
                u = st.uses[slot]
                return u.n * 32 if u.i is None or u.per == 0 else u.i * (32 * u.per) + u.n * 32

            def norm(dst):
                with looped(act, KT // 2, [sq], [2]) as i:
                    for b in range(2):
                        act.wait_ge(sq_summed, sq(PRIMED - 1))
                        act.activation(G["full"][:, b, :], G["h"][:, bass.ds(i * 2 + b, 1), :].rearrange("p o t -> p (o t)"),
                                       ACT.Square).then_inc(sq_ready, 1)
                        sq.up()
                act.wait_ge(rinv_ready, rinvs.up())
                act.activation(G["rs"][:, :], G["rs"][:, :], ACT.Sqrt).then_inc(rs_ready, 1)
                if dst is None:
                    return
                with looped(act, KT // 2, [full], [2]) as i:
                    for b in range(2):
                        act.wait_ge(full_ready, full(1))
                        act.activation(dst[:, bass.ds(i * 2 + b, 1), :], G["full"][:, b:b + 1, :], ACT.Copy).then_inc(xhi_ready, 1)
                        full.up()

            def ffn(slots, last=False):
                for t0, nt in THIRDS:
                    with looped(act, nt // 2, st.all() + [full], [2, 1, 1, 4, 0, 0, 2]) as i:
                        for n, s in enumerate(slots):
                            split(1 - s, st.out())
                            st.duo.up()
                            act.wait_ge(lin_out, st.out.up(2))
                            act.wait_ge(full_ready, full())
                            act.activation(in_halves(G["act"][:, :]), halves(4 * n), ACT.Silu).then_inc(gated, 1)
                            act.wait_ge(full_ready, full(1))
                            act.activation(G["xbh"][:, bass.ds(i * 2 + n, 1), :], G["full"][:, n:n + 1, :], ACT.Copy)\
                                .then_inc(xhi_ready, 1)
                            full.up()
                    if last and t0 + nt == FF // P:
                        for s in (slots * 2)[:-1]:
                            split(1 - s, st.out())
                            st.out.up(2)
                        return
                    with looped(act, 2, st.all(), [2, 1, 1, 4, 0, 0]) as i:
                        for s in slots:
                            split(1 - s, st.out())
                            st.duo.up()
                            st.out.up(2)

            G = F1
            for dst, src in (
                    (prow[:, 0, :], conv_w[0].rearrange("j (t c) -> (j t) c", c=P)),
                    (prow[0:32, 1, :], conv_b[0].rearrange("(t c) -> t c", c=P)),
                    (prow[32:40, 1, :], norm_ffn1[0].rearrange("(t c) -> t c", c=P)),
                    (prow[40:48, 1, :], norm_mix[0].rearrange("(t c) -> t c", c=P)),
                    (prow[48:56, 1, :], norm_ffn2[0].rearrange("(t c) -> t c", c=P)),
                    (prow[56:64, 1, :], norm_final.rearrange("(t c) -> t c", c=P)),
                    (prow[64:80, 1, :], ssm_norm[0].rearrange("(t c) -> t c", c=P)),
                    (prow[0:96, 2, :], state_conv[0, 0].rearrange("r (t c) -> (r t) c", c=P)),
                    (dsk[:, :], d_skip[0:1, :].to_broadcast([P, SSM_HEADS]))):
                act.dma_start(dst, src).then_inc(par_in, 16)
            act.wait_ge(consts, 1)
            act.wait_ge(raw_ready[0], 32)
            st.uses[0].up()
            act.activation(wh[:, 0], raw[:, 0], ACT.Copy).then_inc(hi_ready, 1)
            act.wait_ge(par_T, 1)
            act.activation(par[:, :], bank(7, PC_END), ACT.Copy).then_inc(par_ready, 1)
            act.wait_ge(par_ready, 1)
            act.mul(parh[:, :], par[:, 0:PC_NORM], 0.5).then_inc(par_ready, 1)
            for f in range(KT):
                act.wait_ge(lin_out, f + 1)
                act.activation(G["h"][:, f, :], bank(2 * (f % 3), TOK), ACT.Copy).then_inc(act_free, 1)
            act.wait_ge(act_free, KT)
            norm(xah)
            ffn((0, 1))

            act.wait_ge(dve_free, PRIMED + 3 * KT)
            act.wait_ge(x_ready, KT + FF // P)
            norm(xah)

            split(1, st.out())
            st.duo.up()
            act.wait_ge(t_pool, 1)
            act.wait_ge(t_in, 64)
            act.wait_ge(lin_out, st.out.up())
            act.activation(in_halves(tx[:, :]), halves(0, 48), ACT.Copy).then_inc(act_free, 1)
            st.act.up()
            act.activation(tcol[0:32, 4:5], tcol[0:32, 1:2], ACT.Exp).then_inc(t_act, 1)
            act.wait_ge(t_dve, 1)
            link(act.activation(tb[:, :], tb[:, :], ACT.Exp))
            act.activation(tb[:, :], tb[:, :], ACT.Ln, bias=ones[0:48, 0:1]).then_inc(t_act, 1)
            act.wait_ge(t_dve, 2)
            act.activation(tdec[:, :], tdec[:, :], ACT.Exp)
            act.activation(tstack[96:128, :], tsum[0:32, :], ACT.Exp).then_inc(t_act, 1)
            act.wait_ge(t_pe, 2)
            tk = bank(6, TILES * P).rearrange("p (t c) -> p t c", t=TILES)
            act.activation(tokt[:, 0:4, :], tk[:, 0:4, :], ACT.Copy)
            act.activation(tokt[0:80, 4, :], tk[0:80, 4, :], ACT.Copy)
            lt = bank(4, TILES * 64).rearrange("p (t c) -> p t c", t=TILES)
            act.activation(lft[:, 0:4, 0:48], lt[:, 0:4, 0:48], ACT.Copy)
            act.activation(lft[0:80, 4, 0:48], lt[0:80, 4, 0:48], ACT.Copy).then_inc(t_act, 1)

            def stage(i, n):
                k = n - 1
                if 0 <= k < JOBS:
                    t = k % 5
                    m, nb = ROWS[t], key_blocks(t)
                    act.wait_ge(p_T, i * JOBS + (k + 1))
                    if k >= 2:
                        act.wait_ge(pv_ready, i * JOBS + (k - 1))
                    act.activation(pt[:, k % 2, :].rearrange("p (b q) -> p b q", b=TILES)[:, 0:nb, 0:m],
                                   bank(6, TILES * P).rearrange("p (b q) -> p b q", b=TILES)[:, 0:nb, 0:m],
                                   ACT.Copy).then_inc(pt_ready, 1)
                if n < JOBS:
                    t = n % 5
                    m = ROWS[t]
                    act.wait_ge(mx_ready, i * JOBS + (n + 1))
                    if n >= 4:
                        act.wait_ge(o_ready, i * JOBS + (n - 3))
                    act.activation(scores(t), scores(t), ACT.Exp, bias=mx[0:m, n % 4:n % 4 + 1],
                                   accum_out=rsum[0:m, n % 4:n % 4 + 1]).then_inc(p_ready, 1)

            def mid(now, steps):
                for step in flat(steps):
                    i, kind, g = now, step[0], step[1] if len(step) > 1 else 0
                    if kind == "half" and g % 2 == 0:
                        stage(i, g // 2)
                    elif kind == "split":
                        split_quarter(1 - MID_SLOT[g], step[2], st.out(-step[3]), split_cols(g))
                    elif kind == "lin":
                        i = now + step[3]
                        k, t, n, g = MID[g], step[2], g, g // 3
                        b, m = lin_bank(n, t), ROWS[t]
                        act.wait_ge(lin_out, st.out.up())
                        if k == "z":
                            zb = (g + t) % 2
                            if steps is FIRST_STEPS and t == 0:
                                act.wait_ge(heads_left, 1)
                            act.wait_ge(z_used, i * 10 + (PRIMED + 5 * g + t - 1))
                            act.activation(zt[0:m, zb, :], bank(b, 256, m), ACT.Tanh, scale=0.5)
                            act.activation(zr[0:m, zb, :], bank(b, 256, m), ACT.Copy).then_inc(act_free, 1)
                        elif k in ("x", "bc"):
                            j = t + (2 if k == "bc" else 0)
                            if j == 0:
                                act.wait_ge(taps_done, i * 8 + (PRIMED + 4 * g))
                                act.wait_ge(cst_T, i * 2 + (PRIMED + g))
                            act.activation(xp[:, j, CS_:CS_ + SAMPLE], bank(b, SAMPLE), ACT.Copy)
                            act.activation(xp[:, j, CP_:CP_ + HALF - SAMPLE], bank(b, HALF - SAMPLE, at=SAMPLE), ACT.Copy)
                            act.activation(xp[:, j, CP_ + HALF - SAMPLE:CW], bank(b + 1, HALF), ACT.Copy).then_inc(act_free, 1)
                        elif k == "v":
                            act.activation(vt[0:m, t, :], bank(b, 256, m), ACT.Copy).then_inc(act_free, 1)
                        elif k in ("q0", "q1"):
                            p = int(k == "q1")
                            act.activation(in_halves(qz[0:HD, 2 * p, :]), halves(b)[0:HD], ACT.Copy)
                            act.activation(in_halves(qz[HD:P, 2 * p + 1, :]), halves(b)[HD:P], ACT.Copy).then_inc(act_free, 1)
                        else:
                            act.activation(in_halves(kT[:, t, :]), halves(b), ACT.Copy).then_inc(act_free, 1)
                        st.act.up()
                        if t == OUTS[k] - 1:
                            st.duo.up()
                    elif kind == "prep":
                        act.wait_ge(sraw_T, i * 2 + (PRIMED + g + 1))
                        act.wait_ge(yo_ready, i * 10 + (PRIMED + 5 * g))
                        act.wait_ge(s_ready, i * 10 + (PRIMED + 5 * g))
                        act.activation(sini[:, :], bank(6, 256), ACT.Copy).then_inc(sini_ready, 1)
                        act.wait_ge(brow_in, i * 32 + 16 * (g + 1))
                        act.activation(dec[:, :, 0], brow[:, :, SAMPLE - 1], ACT.Exp)
                        act.activation(dec[:, :, 1:4], brow[:, :, 255:512:128], ACT.Exp)
                        act.activation(dec[:, :, 4], brow[:, :, TOK - 1], ACT.Exp).then_inc(dec_ready, 1)
                    elif kind == "convA":
                        i, j = now + step[3], step[2]
                        act.wait_ge(hist_ready, i * 2 + (g + 1))
                        act.wait_ge(act_free, conv_in(i, g, j))
                        act.wait_ge(cv_done, i * 8 + (PRIMED + 4 * g + j - 1))
                        col = conv_tile(i, g, j)
                        act.activation(cvt[:, j % 2, :], xp[:, j, 0:CO], ACT.Identity, scale=parh[:, bass.ds(col, 1)],
                                       bias=parh[:, bass.ds(col + PC_CONVB, 1)]).then_inc(tap0_ready, 1)
                    elif kind == "convB":
                        i, j = now + step[3], step[2]
                        act.wait_ge(taps_done, i * 8 + (PRIMED + 4 * g + j + 1))
                        act.wait_ge(cv_done, i * 8 + (PRIMED + 4 * g + j))
                        act.activation(th[:, :], cvt[:, j % 2, :], ACT.Tanh).then_inc(tanh_ready, 1)
                    elif kind == "cst":
                        act.wait_ge(cst_T, i * 2 + (PRIMED + g + 1))
                        if g == 0:
                            act.wait_ge(heads_left, i + 1)
                        else:
                            act.wait_ge(yT_out, i * 32 + 16)
                        act.activation(cst[:, :, :], bank(6, 1024, 3).rearrange("p (k c) -> p k c", k=2), ACT.Copy).then_inc(cst_ready, 1)
                    elif kind == "s1":
                        t = step[2]
                        m, b, tau = ROWS[t], (t + g) % 2, 5 * g + t
                        act.wait_ge(xb_T, i * 10 + (tau + 1))
                        act.wait_ge(st_ready, i * 10 + (PRIMED + tau - 1))
                        act.activation(xbt[0:m, b, :], bank(4, 384, m), ACT.Copy).then_inc(xb_ready, 1)
                        act.wait_ge(seg_ready, i * 10 + (PRIMED + tau + 1))
                        act.activation(eb[0:m, :, 0:m], eb[0:m, :, 0:m], ACT.Exp).then_inc(e_ready, 1)
                    elif kind == "s2":
                        t = step[2]
                        m, tau = ROWS[t], 5 * g + t
                        act.wait_ge(yg_ready, i * 10 + (PRIMED + tau + 1))
                        act.wait_ge(sq_done, i * 10 + (PRIMED + tau))
                        act.activation(junk[0:m, :], yg[0:m, t, :], ACT.Square, accum_out=ssq[0:m, t:t + 1]).then_inc(sq_done, 1)
                    elif kind == "s3":
                        act.wait_ge(rv_ready, i * 2 + (g + 1))
                        act.activation(ssq[:, 0:4], ssq[:, 0:4], ACT.Sqrt)
                        act.activation(ssq[0:80, 4:5], ssq[0:80, 4:5], ACT.Sqrt).then_inc(rt_ready, 1)
                        for j, b in enumerate((6, 4)):
                            act.wait_ge(yT_T, i * 4 + (PRIMED + 2 * g + j + 1))
                            if j == 0:
                                act.wait_ge(cst_out, i * 192 + 96 * (g + 1))
                            act.activation(yT[:, j, :], bank(b, TOK), ACT.Copy,
                                           scale=par[:, bass.ds(i * 4 + (PC_SSMN + 2 * g + j), 1)]).then_inc(yT_ready, 1)
                    elif kind == "s4":
                        act.wait_ge(sf_T, i * 2 + (PRIMED + g + 1))
                        if g:
                            act.wait_ge(sto_out, i * 64 + 32)
                        act.activation(sto[:, :, :].rearrange("p a b -> p (a b)"), bank(6, 512), ACT.Copy).then_inc(sto_ready, 1)
                    elif kind == "enter":
                        act.wait_ge(ssd_left, i + 1)
                        for n in range(3):
                            act.wait_ge(ktok_T, i * 3 + (n + 1))
                            m, t1 = ROWS[2 * n], min(2 * n + 2, TILES)
                            act.activation(ktok[0:m, 2 * n:t1, :].rearrange("p t c -> p (t c)"), bank(4 + n, 256 * (t1 - 2 * n), m),
                                           ACT.Copy).then_inc(ktok_ready, 1)
                    elif kind == "cache":
                        for p in range(2):
                            act.wait_ge(kc_T, i * 2 + (p + 1))
                            act.activation(kcT[:, p, :], bank(7 - 3 * p, PAST), ACT.Copy).then_inc(kc_ready, 1)
                    elif kind == "leave":
                        for p in range(2):
                            act.wait_ge(o_T, i * 2 + (p + 1))
                            act.activation(oT[:, p, :], bank(4 + 2 * p, TOK), ACT.Copy).then_inc(oT_ready, 1)

            mid(0, FIRST_STEPS)
            with looped(act, 3, st.all() + [chain], MID_PER + [0]) as i:
                mid(i, LOOP_STEPS)
            mid(3, LAST_STEPS)

            G = G2
            stage = [Count(), Count()]

            def x_upper(dst, k, b):
                u = stage[b]
                u.up()
                act.wait_ge(stage_in[b], u.n * 16 if u.i is None else u.i * (16 * u.per) + u.n * 16)
                act.activation(dst[:, bass.ds(k, 1), :], G["full"][:, b:b + 1, :], ACT.Copy).then_inc(xhi_ready, 1)

            act.wait_ge(heads_left, 5)
            for part in range(2):
                with looped(act, 2, st.all() + stage, [2, 1, 1, 4, 4, 0, 1, 1]) as i:
                    for n, s in enumerate((1, 0)):
                        split(1 - s, st.out())
                        st.duo.up()
                        for u in range(2):
                            act.wait_ge(lin_out, st.out.up())
                            act.activation(in_halves(gates[:, bass.ds(i * 4 + (8 * part + 2 * n + u), 1), :]
                                                     .rearrange("p o t -> p (o t)")),
                                           halves(2 * (2 * n + u)), ACT.Tanh, scale=0.5).then_inc(act_free, 1)
                            st.act.up()
                        x_upper(G["xbh"], i * 2 + (4 * part + n), n)
            for part, dst in enumerate((xah, G["xbh"], xah, None)):
                if dst is not None:
                    act.wait_ge(lin_out, st.out())
                loads = part < 2
                with looped(act, 2, st.all() + stage, [2, 1, 1, 4, 0, 4] + [2 * loads, 2 * loads]) as i:
                    for n, s in enumerate((1, 0)):
                        split(1 - s, st.out())
                        st.duo.up()
                        for u in range(2):
                            m = i * 4 + (2 * n + u)
                            st.out.up()
                            st.dve.up()
                            if loads:
                                x_upper(dst, m, u)
                            elif dst is not None:
                                act.wait_ge(dve_free, PRIMED + 3 * KT + st.dve())
                                act.activation(dst[:, bass.ds(m, 1), :], G["h"][:, bass.ds(m, 1), :], ACT.Copy).then_inc(xhi_ready, 1)
            act.wait_ge(dve_free, PRIMED + 7 * KT)
            act.wait_ge(x_ready, X_MIX + 4 * KT)
            norm(xah)
            ffn((1, 0), last=True)
            act.wait_ge(dve_free, PRIMED + 7 * KT + 3 * KT)
            norm(None)
            for f in range(KT):
                act.wait_ge(fin_T, PRIMED + f + 1)
                pv = bank(2 * (f % 4), TILES * P).rearrange("p (t c) -> p t c", t=TILES)
                act.activation(ytok[:, 0:4, f * P:(f + 1) * P], pv[:, 0:4, :], ACT.Copy)
                act.activation(ytok[0:80, 4, f * P:(f + 1) * P], pv[0:80, 4, :], ACT.Copy).then_inc(fin_ready, 1)

        @block.vector
        def _(dve):
            st = Stream()
            chain, full, xhi, summed, nsplit = Count(), Count(), Count(), Count(PRIMED), Count()

            for s in (split_done, dve_free, taps_done, cv_done, seg_ready, cbm_ready, m_ready, s_ready, y_used, yg_ready, s_free):
                dve.sem_inc(s, PRIMED)

            def link(ins):
                ins.then_inc(dch, 1)
                dve.wait_ge(dch, chain.up())

            def split(slot, cols=256):
                dve.wait_ge(hi_ready, nsplit.up())
                dve.tensor_tensor(wl[:, slot, :, 0:cols], raw[:, slot, :, 0:cols], wh[:, slot, :, 0:cols].bitcast(F32), ALU.subtract)\
                    .then_inc(split_done, 1)

            def x_lower(dst, k, src, hi):
                dve.wait_ge(xhi_ready, xhi.up())
                dve.tensor_tensor(dst[:, bass.ds(k, 1), :], src, hi[:, bass.ds(k, 1), :].bitcast(F32), ALU.subtract)\
                    .then_inc(x_ready, 1)

            def norm(which, split_it=True):
                dve.wait_ge(sq_summed, summed.up(KT))
                link(dve.tensor_scalar(in_halves(G["rs"][:, :]), halves(0), 1.0 / D, EPS, ALU.mult, ALU.add))
                dve.reciprocal(G["rs"][:, :], G["rs"][:, :]).then_inc(rinv_ready, 1)
                dve.wait_ge(rs_ready, roots.up())

                def scaled(i, k):
                    dve.scalar_tensor_tensor(out=G["full"][:, k % 2, :], in0=G["h"][:, bass.ds(i * 2 + k, 1), :].rearrange("p o t -> p (o t)"),
                                             scalar=par[:, bass.ds(i * 2 + (PC_NORM + KT * which + k), 1)],
                                             in1=G["rs"][:, :], op0=ALU.mult, op1=ALU.mult).then_inc(full_ready, 1)
                    full.up()

                if not split_it:
                    with looped(dve, KT // 2, [full], [2]) as i:
                        for b in range(2):
                            dve.wait_ge(fin_T, i * 2 + (PRIMED + b - 1))
                            scaled(i, b)
                    return
                scaled(0, 0)
                scaled(0, 1)
                with looped(dve, KT // 2 - 1, [full, xhi], [2, 2]) as i:
                    for b in range(2):
                        x_lower(xal, i * 2 + b, G["full"][:, b:b + 1, :], xah)
                        dve.wait_ge(x_ready, xhi())
                        scaled(i, b + 2)
                x_lower(xal, KT - 2, G["full"][:, 0:1, :], xah)
                x_lower(xal, KT - 1, G["full"][:, 1:2, :], xah)

            def add_to_h(m, b, again):
                dve.wait_ge(lin_out, st.out.up())
                if again:
                    dve.wait_ge(dve_free, st.dve(PRIMED + 1 - KT))
                hm = in_halves(G["h"][:, bass.ds(m, 1), :].rearrange("p o t -> p (o t)"))
                dve.scalar_tensor_tensor(out=hm, in0=halves(b), scalar=0.5, in1=hm, op0=ALU.mult, op1=ALU.add)\
                    .then_inc(dve_free, 1)
                st.dve.up()

            def ffn(slots, last=False):
                for t0, nt in THIRDS:
                    with looped(dve, nt // 2, st.all() + [full, xhi, nsplit, hid], [2, 1, 1, 4, 0, 0, 2, 2, 2, 2]) as i:
                        for n, s in enumerate(slots):
                            split(1 - s)
                            st.duo.up()
                            st.uses[s].up()
                            st.out.up(2)
                            dve.wait_ge(gated, PRIMED + hid.up())
                            dve.tensor_tensor(in_halves(G["full"][:, n, :]), in_halves(G["act"][:, :]), halves(4 * n + 2), ALU.mult)\
                                .then_inc(full_ready, 1)
                            full.up()
                            dve.wait_ge(full_ready, full())
                            x_lower(G["xbl"], i * 2 + n, G["full"][:, n:n + 1, :], G["xbh"])
                    if last and t0 + nt == FF // P:
                        for n, s in enumerate(slots * 2):
                            if n < 3:
                                split(1 - s)
                            for u in range(2):
                                add_to_h(2 * n + u, 2 * ((2 * n + u) % 4), True)
                        return
                    with looped(dve, 2, st.all() + [nsplit], [2, 1, 1, 4, 0, 4, 2]) as i:
                        for n, s in enumerate(slots):
                            split(1 - s)
                            st.duo.up()
                            st.uses[s].up()
                            for u in range(2):
                                add_to_h(i * 4 + (2 * n + u), 2 * (2 * n + u), t0 > 0)

            roots, hid = Count(), Count()
            dve.wait_ge(consts, 2)

            G = F1
            split(0)
            norm(NORM_FFN1)
            ffn((0, 1))
            dve.wait_ge(dve_free, PRIMED + 3 * KT)
            norm(NORM_MIX)

            split(1)
            st.duo.up()
            st.out.up()
            dve.wait_ge(act_free, KT + 1)
            link(dve.tensor_scalar(tx[:, :], tx[:, :], tcol[:, 0:1], tcol[:, 2:3], ALU.add, ALU.mult))
            dve.scalar_tensor_tensor(out=tb[:, :], in0=tx[:, :], scalar=-1.0, in1=tx[:, :], op0=ALU.mult, op1=ALU.min)\
                .then_inc(t_dve, 1)
            dve.wait_ge(t_act, 2)
            dve.tensor_scalar(tcol[0:32, 3:4], tcol[0:32, 4:5], -1.0, None, ALU.mult)
            link(dve.scalar_tensor_tensor(out=tx[:, :], in0=tx[:, :], scalar=0.0, in1=tb[:, :], op0=ALU.max, op1=ALU.add))
            link(dve.tensor_scalar(tsteps[:, :], tx[:, :], tcol[:, 3:4], None, ALU.mult))
            link(dve.tensor_tensor_scan(tsum[:, :], scanm[:, :], tsteps[:, :], 0.0, ALU.mult, ALU.add))
            for n, (c0, c1) in enumerate(CHUNKS):
                last = dve.tensor_scalar(tdec[:, c0:c1], tsum[0:32, c0:c1], -1.0, tsum[0:32, c1 - 1:c1], ALU.mult, ALU.add)
            last.then_inc(t_dve, 1)
            dve.tensor_copy(tstack[0:32, :], tsum[0:32, :])
            dve.tensor_copy(tstack[32:64, :], tx[0:32, :])
            dve.wait_ge(t_act, 3)
            dve.memset(tstack[96:128, SAMPLE:P], 0.0)
            dve.tensor_tensor(tstack[64:96, :], tdec[:, :], tx[0:32, :], ALU.mult).then_inc(t_dve, 1)
            link(dve.tensor_copy(tcm[:, :], tsum[32:48, 0:SAMPLE + META]))
            dve.wait_ge(t_pe, 1)
            link(dve.tensor_tensor_scan(tcs[:, 0:PAST], one16[:, :], bank(5, PAST, 16), tcm[:, SAMPLE + META - 1:SAMPLE + META],
                                        ALU.mult, ALU.add))
            dve.tensor_scalar(tcs[:, PAST:PAST + SAMPLE], tcm[:, 0:SAMPLE], tcs[:, PAST - 1:PAST], None, ALU.add)
            link(dve.tensor_copy(tcs[:, PAST + SAMPLE:], tcm[:, SAMPLE:]))
            dve.tensor_scalar(nb0[:, 0, 0:PAST + SAMPLE + META], tcs[:, :], -1.0, None, ALU.mult)
            dve.tensor_scalar(nb0[:, 1, PAST + SAMPLE:], tsum[32:48, SAMPLE:P], -1.0, None, ALU.mult)
            dve.tensor_scalar(nbp[:, :], tsum[32:48, SAMPLE:], -1.0, None, ALU.mult).then_inc(t_dve, 1)

            def heads4(ap, m):
                return ap.unsqueeze(2).to_broadcast([m, 4, HD])

            def by_head(ap):
                return ap.rearrange("p (h c) -> p h c", h=4)

            def stage(i, n):
                k = n - 2
                if k >= 0:
                    hh, t = k // 5, k % 5
                    m = ROWS[t]
                    dve.wait_ge(pv_ready, i * JOBS + (k + 1))
                    link(dve.reciprocal(rinv[0:m, k % 4:k % 4 + 1], rsum[0:m, k % 4:k % 4 + 1]))
                    dve.tensor_scalar(otok[0:m, t, HD * hh:HD * hh + HD], bank(7, HD, m, at=256),
                                      rinv[0:m, k % 4:k % 4 + 1], None, ALU.mult).then_inc(o_ready, 1)
                if n < JOBS:
                    hh, t = n // 5, n % 5
                    m, (before, w) = ROWS[t], score_span(t)
                    dve.wait_ge(bias_in[hh % 2], i * 96 + 48 * (hh // 2 + 1))
                    dve.wait_ge(qk_ready, i * JOBS + (n + 1))
                    if n >= 2:
                        dve.wait_ge(p_T, i * JOBS + (n - 1))
                    bs = bias[0:m, hh % 2, 0:PAST + P] if t == 0 else bias[0:m, hh % 2, PAST + P:PAST + P + w]
                    dve.scalar_tensor_tensor(out=scores(t), in0=bank(4, w, m, at=BANK - before), scalar=SCALE, in1=bs,
                                             op0=ALU.mult, op1=ALU.add).then_inc(s_free, 1)
                    dve.wait_ge(s_free, i * JOBS + (PRIMED + n + 1))
                    dve.tensor_reduce(mx[0:m, n % 4:n % 4 + 1], scores(t), AX.X, ALU.max, negate=True).then_inc(mx_ready, 1)

            def mid(now, steps):
                for step in flat(steps):
                    i, kind, g = now, step[0], step[1] if len(step) > 1 else 0
                    if kind == "half" and g % 2 == 0:
                        stage(i, g // 2)
                    elif kind == "split":
                        nsplit.up(step[2] == 3)
                    elif kind == "convA":
                        i, j = now + step[3], step[2]
                        dve.wait_ge(tap0_ready, i * 8 + (4 * g + j + 1))
                        c = cvt[:, j % 2, :]
                        for tap in range(1, 4):
                            ins = dve.scalar_tensor_tensor(out=c, in0=xp[:, j, tap:tap + CO],
                                                           scalar=parh[:, bass.ds(conv_tile(i, g, j) + 32 * tap, 1)],
                                                           in1=c, op0=ALU.mult, op1=ALU.add)
                            if tap < 3:
                                link(ins)
                        ins.then_inc(taps_done, 1)
                    elif kind == "convB":
                        i, j = now + step[3], step[2]
                        dve.wait_ge(tanh_ready, i * 8 + (4 * g + j + 1))
                        if j == 0:
                            dve.wait_ge(yd_ready, i * 10 + (PRIMED + 5 * g))
                        for c0, c1, to in ((0, SAMPLE, 0), (CP_ - CS_, CO, SAMPLE)):
                            ins = dve.scalar_tensor_tensor(out=cv[:, j, to:to + c1 - c0], in0=th[:, c0:c1], scalar=1.0,
                                                           in1=cvt[:, j % 2, c0:c1], op0=ALU.add, op1=ALU.mult)
                        ins.then_inc(cv_done, 1)
                    elif kind == "s1":
                        t = step[2]
                        m, tau, c = ROWS[t], 5 * g + t, t * P
                        if t == 0:
                            dve.wait_ge(brow_in, i * 32 + 16 * (g + 1))
                        if tau == 0:
                            dve.wait_ge(heads_left, i + 1)
                        dve.wait_ge(m_ready, i * 10 + (PRIMED + tau))
                        for r in range(4):
                            ins = dve.tensor_scalar(eb[0:m, r, 0:m], brow[0:m, r, c:c + m],
                                                    tokt[0:m, t, bass.ds(i * 8 + (4 * g + r), 1)], 0.0, ALU.subtract, ALU.min)
                        ins.then_inc(seg_ready, 1)
                        dve.wait_ge(cb_ready, i * 10 + (tau + 1))
                        dve.tensor_tensor(cbm[0:m, 0:m], bank(5, m, m), mask01[0:m, min(t, 1), 0:m], ALU.mult).then_inc(cbm_ready, 1)
                        dve.wait_ge(cbm_ready, i * 10 + (PRIMED + tau + 1))
                        dve.wait_ge(e_ready, i * 10 + (tau + 1))
                        dve.wait_ge(yd_ready, i * 10 + (PRIMED + tau - 1))
                        dve.tensor_tensor(mb[0:m, tau % 2, :, 0:m], eb[0:m, :, 0:m],
                                          cbm[0:m, 0:m].unsqueeze(1).to_broadcast([m, 4, m]), ALU.mult).then_inc(m_ready, 1)
                    elif kind == "s2":
                        t = step[2]
                        m, tau = ROWS[t], 5 * g + t
                        dve.wait_ge(st_ready, i * 10 + (PRIMED + tau + 1))
                        if t == 0:
                            dve.wait_ge(dec_ready, i * 2 + (PRIMED + g + 1))
                            dve.wait_ge(sini_ready, i * 2 + (g + 1))
                            dve.wait_ge(sf_T, i * 2 + (g + PRIMED))
                            for r in range(4):
                                h = slice(HD * r, HD * r + HD)
                                dve.scalar_tensor_tensor(out=sfin[:, h], in0=sini[:, h], scalar=dec[:, r, 0:1],
                                                         in1=bank(7, HD, at=HD * r), op0=ALU.mult, op1=ALU.add)
                            dve.tensor_copy(spr[:, 0, :], bank(7, 256, at=256)).then_inc(s_ready, 1)
                        else:
                            dve.wait_ge(s_ready, i * 10 + (PRIMED + tau))
                            for r in range(4):
                                h = slice(HD * r, HD * r + HD)
                                ins = dve.scalar_tensor_tensor(out=spr[:, t % 2, h], in0=spr[:, (t - 1) % 2, h],
                                                               scalar=dec[:, r, t:t + 1], in1=bank(7, HD, at=HD * r),
                                                               op0=ALU.mult, op1=ALU.add)
                            ins.then_inc(s_ready, 1)
                        dve.wait_ge(yd_ready, i * 10 + (PRIMED + tau + 1))
                        dve.wait_ge(yg_ready, i * 10 + (PRIMED + tau))
                        dve.tensor_tensor(by_head(y1[0:m, :]), by_head(bank(6, 256, m)),
                                          heads4(tokt[0:m, t, bass.ds(i * 8 + (96 + 4 * g), 4)], m), ALU.mult)
                        dve.wait_ge(xd_ready, i * 10 + (tau + 1))
                        dve.tensor_tensor(y2[0:m, :], bank(6, 256, m, at=256), xsk[0:m, tau % 2, :], ALU.add).then_inc(y_used, 1)
                        dve.wait_ge(y_used, i * 10 + (PRIMED + tau + 1))
                        link(dve.tensor_tensor(y1[0:m, :], y1[0:m, :], y2[0:m, :], ALU.add))
                        if t == 0:
                            dve.wait_ge(z_used, i * 10 + (PRIMED + 5 * g + 5))
                            dve.wait_ge(yT_T, i * 4 + (PRIMED + 2 * g))
                        dve.scalar_tensor_tensor(out=yg[0:m, t, :], in0=y1[0:m, :], scalar=0.5, in1=zs[0:m, g, t, :],
                                                 op0=ALU.mult, op1=ALU.mult).then_inc(yg_ready, 1)
                    elif kind == "s3":
                        dve.wait_ge(sq_done, i * 10 + (PRIMED + 5 * g + 5))
                        parts = (ssq[:, 0:4], ssq[0:80, 4:5])
                        for a in parts:
                            ins = dve.tensor_scalar(a, a, 1.0 / 256, EPS, ALU.mult, ALU.add)
                        link(ins)
                        for a in parts:
                            ins = dve.reciprocal(a, a)
                        ins.then_inc(rv_ready, 1)
                        dve.wait_ge(rt_ready, i * 2 + (g + 1))
                        for t in range(TILES):
                            a = yg[0:ROWS[t], t, :]
                            ins = dve.tensor_scalar(a, a, ssq[0:ROWS[t], t:t + 1], None, ALU.mult)
                        ins.then_inc(yn_ready, 1)
                    elif kind == "enter":
                        dve.wait_ge(ssd_left, i + 1)

            mid(0, FIRST_STEPS)
            with looped(dve, 3, [chain, nsplit], [48, 10]) as i:
                mid(i, LOOP_STEPS)
            mid(3, LAST_STEPS)
            st.out.up(4 * MID_OUTS)

            G = G2
            for part in range(2):
                with looped(dve, 2, [nsplit, xhi, st.out], [2, 2, 4]) as i:
                    for n, s in enumerate((1, 0)):
                        split(1 - s)
                        st.out.up(2)
                        x_lower(G["xbl"], i * 2 + (4 * part + n), G["full"][:, n:n + 1, :], G["xbh"])
            dve.wait_ge(act_free, KT + 1 + 4 * MID_OUTS + 2 * KT)
            for part, (hi, lo) in enumerate(((xah, xal), (G["xbh"], G["xbl"]), (xah, xal), (None, None))):
                if part == 3:
                    dve.wait_ge(h_back, 16)
                with looped(dve, 2, [nsplit, xhi, st.out, st.dve, chain], [2, 4 * (part < 3), 4, 4, 4 * (part in (1, 2))]) as i:
                    for n, s in enumerate((1, 0)):
                        split(1 - s)
                        for u in range(2):
                            m, b = i * 4 + (2 * n + u), 2 * (2 * n + u)
                            if part == 3:
                                add_to_h(m, b, False)
                                continue
                            dve.wait_ge(lin_out, st.out.up())
                            hm = in_halves(G["h"][:, bass.ds(m, 1), :].rearrange("p o t -> p (o t)"))
                            gt = in_halves(gates[:, bass.ds(m + 8 * (part > 0), 1), :].rearrange("p o t -> p (o t)"))
                            to = hm if part == 0 else in_halves(G["act"][:, :])
                            if part:
                                dve.wait_ge(dve_free, st.dve(PRIMED))
                            ins = dve.scalar_tensor_tensor(out=to, in0=gt, scalar=1.0, in1=halves(b), op0=ALU.add, op1=ALU.mult)
                            if part:
                                link(ins)
                                ins = dve.tensor_tensor(hm, hm, to, ALU.add)
                            ins.then_inc(dve_free, 1)
                            st.dve.up()
                            if part == 2:
                                dve.wait_ge(dve_free, st.dve(PRIMED))
                            src = G["h"][:, bass.ds(m, 1), :] if part == 2 else G["full"][:, u:u + 1, :]
                            x_lower(lo, m, src, hi)

            dve.wait_ge(dve_free, PRIMED + 7 * KT)
            norm(NORM_FFN2)
            ffn((1, 0), last=True)
            dve.wait_ge(dve_free, PRIMED + 7 * KT + 3 * KT)
            norm(NORM_FINAL, split_it=False)

        @block.tensor
        def _(pe):
            st = Stream()
            nsq, xr, full, hid = Count(), Count(), Count(), Count()

            for s in (sq_summed, cst_T, sraw_T, st_ready, yo_ready, yd_ready, yT_T, sf_T, fin_T):
                pe.sem_inc(s, PRIMED)

            def duo_split():
                pe.wait_ge(split_done, st.duo(PRIMED + 1))
                st.duo.up()

            def unit(slot, j, xh, xl, nk, b, before_last=None, between=lambda at: None, tiles_after=None):
                for k in range(nk):
                    if tiles_after is not None:
                        pe.wait_ge(x_ready, tiles_after + k + 1)
                    if before_last is not None and k == nk - 1:
                        before_last()
                    for w, x in ((wh, xh), (wh, xl), (wl, xh)):
                        for a in range(2):
                            ins = pe.matmul(bank(b + a, HALF), w[:, slot, k, j * P:(j + 1) * P], x[:, k, a * HALF:(a + 1) * HALF],
                                            start=(k == 0 and w is wh and x is xh), stop=(k == nk - 1 and w is wl))
                        if k == nk - 1 and w is wl:
                            ins.then_inc(lin_out, 1)
                        between(3 * k + (w is wl) + (x is xl or w is wl))
                st.out.up()

            def token_tile(slot, t, b, between):
                m = ROWS[t]
                for k in range(KT):
                    for w, x in ((wh, xah), (wh, xal), (wl, xah)):
                        ins = pe.matmul(bank(b, 256, m), x[:, k, t * P:t * P + m], w[:, slot, k, :],
                                        start=(k == 0 and w is wh and x is xah), stop=(k == KT - 1 and w is wl))
                        if k == KT - 1 and w is wl:
                            ins.then_inc(lin_out, 1)
                        between(3 * k + (w is wl) + (x is xal or w is wl))
                st.out.up()

            def norm():
                def square(b, first=False, last=False):
                    pe.wait_ge(sq_ready, nsq.up())
                    for a in range(2):
                        ins = pe.matmul(bank(a, HALF), ones[:, :], G["full"][:, b, a * HALF:(a + 1) * HALF],
                                        start=first, stop=last)
                    ins.then_inc(sq_summed, 1)

                square(0, first=True)
                square(1)
                with looped(pe, KT // 2 - 2, [nsq], [2]) as i:
                    for b in range(2):
                        square(b)
                square(0)
                square(1, last=True)

            def ffn(slots, last=False):
                for t0, nt in THIRDS:
                    with looped(pe, nt // 2, st.all() + [full, hid], [2, 0, 0, 4, 0, 0, 2, 2]) as i:
                        for n, s in enumerate(slots):
                            duo_split()
                            pe.wait_ge(dve_free, st.dve(PRIMED - 2 * (n == 0)))
                            pe.wait_ge(gated, hid(PRIMED - 1))
                            hid.up()
                            unit(s, 0, xah, xal, KT, 4 * n, tiles_after=xr() - KT if t0 == n == 0 else None)
                            pe.wait_ge(full_ready, full(-1))
                            unit(s, 1, xah, xal, KT, 4 * n + 2)
                            full.up()
                    xr.up(nt)
                    with looped(pe, 2, st.all(), [2, 0, 0, 4, 0, 4]) as i:
                        for n, s in enumerate(slots):
                            duo_split()
                            for u in range(2):
                                pe.wait_ge(x_ready, xr() - 1)
                                pe.wait_ge(dve_free, st.dve(PRIMED - 1))
                                unit(s, u, G["xbh"], G["xbl"], nt, 2 * (2 * n + u),
                                     before_last=lambda: pe.wait_ge(x_ready, xr()))
                                st.dve.up()

            def turn(out, in_):
                k = in_.shape[0]
                return pe.transpose(out, in_, ident[0:k, 0:k])

            G = F1
            pe.wait_ge(consts, 2)
            pe.wait_ge(par_in, 16 * 9)
            turn(bank(7, P), prow[:, 0, :])
            turn(bank(7, 80, at=P), prow[0:80, 1, :])
            turn(bank(7, 96, at=208), prow[0:96, 2, :]).then_inc(par_T, 1)
            for f in range(KT):
                if f % 4 == 0:
                    pe.wait_ge(x_in[f // 4], 16 * 5)
                if f >= 3:
                    pe.wait_ge(act_free, f - 2)
                for t in range(TILES):
                    ins = turn(bank(2 * (f % 3), ROWS[t], at=t * P), xin[0:ROWS[t], t, (f % 4) * P:(f % 4 + 1) * P])
                ins.then_inc(lin_out, 1)
            norm()
            full.up(KT)
            xr.up(KT)
            ffn((0, 1))
            norm()
            full.up(KT)
            xr.up(KT)

            duo_split()
            unit(0, 0, xah, xal, KT, 0, tiles_after=xr() - KT)
            pe.wait_ge(t_in, 16 * 4)
            for a in range(4):
                ins = turn(bank(5, P, 16, at=a * P), clf[:, a, :])
            ins.then_inc(t_pe, 1)
            pe.wait_ge(t_dve, 3)
            pe.wait_ge(t_act, 3)
            for t in range(TILES):
                m = ROWS[t]
                turn(bank(6, P, m, at=t * P), tstack[:, t * P:t * P + m])
                ins = turn(bank(4, 48, m, at=64 * t), tsteps[:, t * P:t * P + m])
            ins.then_inc(t_pe, 1)
            st.act.up()

            def give(i, k):
                hh, t = k // 5, k % 5
                m, nb = ROWS[t], key_blocks(t)
                pe.wait_ge(pt_ready, i * JOBS + (k + 1))
                if k == 0:
                    pe.wait_ge(vc_in, i * 16 + 16)
                for b in range(nb):
                    c = slice(HD * hh, HD * hh + HD)
                    if t == 0:
                        kw, v = P, vc[:, b, c] if b < 4 else vt[:, 0, c]
                    else:
                        kw = P if b < 4 else ROWS[4]
                        v = vt[0:kw, b, c]
                    ins = pe.matmul(bank(7, HD, m, at=256), pt[0:kw, k % 2, b * P:b * P + m], v, start=(b == 0), stop=(b == nb - 1))
                ins.then_inc(pv_ready, 1)

            def score(i, n):
                hh, t = n // 5, n % 5
                p = hh // 2
                m, (before, w) = ROWS[t], score_span(t)
                if n == 0:
                    pe.wait_ge(ktok_ready, i * 3 + 3)
                    pe.wait_ge(kc_ready, i * 2 + 2)
                else:
                    pe.wait_ge(s_free, i * JOBS + (PRIMED + n))
                q = qz[:, hh, t * P:t * P + m]
                pe.matmul(bank(4, before, m, at=BANK - before), q, kcT[:, p, :] if t == 0 else kT[:, p, SAMPLE:t * P],
                          start=True, stop=True)
                pe.matmul(bank(5, m, m), q, kT[:, p, t * P:t * P + m], start=True, stop=False)
                pe.matmul(bank(5, m, m), identb[0:m, 0:m], negmask[0:m, min(t, 1), 0:m], start=False, stop=True).then_inc(qk_ready, 1)

            def turn_probs(i, k):
                t = k % 5
                m = ROWS[t]
                pe.wait_ge(p_ready, i * JOBS + (k + 1))
                if k == 1:
                    pe.wait_ge(pz_ready, i + 1)
                if k >= 1:
                    pe.wait_ge(pt_ready, i * JOBS + k)
                    pe.wait_ge(o_ready, i * JOBS + k)
                for b in range(key_blocks(t)):
                    kw = P if b < 4 or t == 0 else ROWS[4]
                    src = p0[:, b * P:b * P + P] if t == 0 else pp[0:m, t % 2, b * P:b * P + kw]
                    ins = turn(bank(6, m, kw, at=b * P), src)
                ins.then_inc(p_T, 1)

            def half_stage(i, h):
                n = h // 2
                if h % 2:
                    if 0 <= n - 1 < JOBS:
                        turn_probs(i, n - 1)
                    return
                if n >= 2:
                    give(i, n - 2)
                if n < JOBS:
                    score(i, n)

            def mid(i, steps):
                for step in steps:
                    kind, g = step[0], step[1] if len(step) > 1 else 0
                    if kind == "half":
                        half_stage(i, g)
                    elif kind == "lin":
                        n, t = step[1], step[2]

                        def between(now, within=step[4]):
                            mid(i, [inner for at, inner in within if at == now])
                        k, b = MID[n], lin_bank(n, t)
                        if t == 0:
                            duo_split()
                        if n == 0 and t == 0:
                            pe.wait_ge(act_free, st.act(-1 if step[3] else 0))
                            pe.wait_ge(t_act, 4)
                        else:
                            pe.wait_ge(act_free, st.act(-1))
                        st.act.up()
                        if k in ("z", "v"):
                            token_tile(MID_SLOT[n], t, b, between)
                        else:
                            unit(MID_SLOT[n], t, xah, xal, KT, b, between=between)
                    elif kind == "prep":
                        pe.wait_ge(oT_ready, i * 2 + PRIMED)
                        pe.wait_ge(sto_ready, i * 2 + (PRIMED + g))
                        pe.wait_ge(sraw_in, i * 32 + 16 * (g + 1))
                        turn(bank(6, P), sraw[:, 0, :])
                        turn(bank(6, P, at=P), sraw[:, 1, :]).then_inc(sraw_T, 1)
                    elif kind == "cst":
                        pe.wait_ge(act_free, conv_in(i, g, 3))
                        pe.wait_ge(sini_ready, i * 2 + (g + 1))
                        for j in range(4):
                            turn(bank(6, P, 3, at=j * P), xp[:, j, CS_ + SAMPLE - 3:CS_ + SAMPLE])
                            ins = turn(bank(7, P, 3, at=j * P), xp[:, j, CW - 3:CW])
                        ins.then_inc(cst_T, 1)
                    elif kind == "s1":
                        t = step[2]
                        m, tau, c = ROWS[t], 5 * g + t, slice(t * P, t * P + ROWS[t])
                        if t == 0:
                            pe.wait_ge(cv_done, i * 8 + (PRIMED + 4 * g + 4))
                            pe.wait_ge(cst_ready, i * 2 + (PRIMED + g + 1))
                        pe.wait_ge(xb_ready, i * 10 + (PRIMED + tau))
                        for j in range(3):
                            ins = turn(bank(4, P, m, at=j * P), cv[:, j, c])
                        ins.then_inc(xb_T, 1)
                        pe.wait_ge(cbm_ready, i * 10 + (PRIMED + tau))
                        pe.matmul(bank(5, m, m), cv[:, 2, c], cv[:, 3, c], start=True, stop=True).then_inc(cb_ready, 1)
                    elif kind == "s2":
                        t = step[2]
                        m, tau, c = ROWS[t], 5 * g + t, slice(t * P, t * P + ROWS[t])
                        b = tau % 2
                        if t:
                            pe.wait_ge(s_ready, i * 10 + (PRIMED + tau))
                        pe.wait_ge(y_used, i * 10 + (PRIMED + tau))
                        pe.matmul(bank(6, 256, m), cv[:, 3, c], spr[:, (t - 1) % 2, :] if t else sini[:, :],
                                  start=True, stop=True).then_inc(yo_ready, 1)
                        pe.wait_ge(xd_ready, i * 10 + (tau + 1))
                        pe.wait_ge(xb_ready, i * 10 + (PRIMED + tau + 1))
                        pe.wait_ge(s_ready, i * 10 + (PRIMED + tau))
                        if t == 0:
                            pe.matmul(bank(7, 256), xbt[0:64, b, 256:384], xdd[0:64, b, :], start=True, stop=True)\
                                .then_inc(st_sample, 1)
                            pe.wait_ge(st_sample, i * 2 + (g + 1))
                            pe.matmul(bank(7, 256, at=256), xbt[64:128, b, 256:384], xdd[64:128, b, :], start=True, stop=True)\
                                .then_inc(st_ready, 1)
                        else:
                            pe.matmul(bank(7, 256), xbt[0:m, b, 256:384], xdd[0:m, b, :], start=True, stop=True)\
                                .then_inc(st_ready, 1)
                        pe.wait_ge(m_ready, i * 10 + (PRIMED + tau + 1))
                        for r in range(4):
                            ins = pe.matmul(bank(6, HD, m, at=256 + HD * r), mb[0:m, b, r, 0:m], xd[0:m, b, HD * r:HD * r + HD],
                                            start=True, stop=True)
                        ins.then_inc(yd_ready, 1)
                    elif kind == "s3":
                        pe.wait_ge(yn_ready, i * 2 + (g + 1))
                        pe.wait_ge(y_used, i * 10 + (PRIMED + 5 * g + 5))
                        pe.wait_ge(s_ready, i * 10 + (PRIMED + 5 * g + 5))
                        for j, b in enumerate((6, 4)):
                            for t in range(TILES):
                                ins = turn(bank(b, ROWS[t], at=t * P), yg[0:ROWS[t], t, j * P:(j + 1) * P])
                            ins.then_inc(yT_T, 1)
                    elif kind == "s4":
                        pe.wait_ge(yT_ready, i * 4 + (PRIMED + 2 * g + 1))
                        for k, s in enumerate((sfin[:, :], spr[:, 0, :])):
                            for j in range(2):
                                ins = turn(bank(6, P, at=256 * k + j * P), s[:, j * P:(j + 1) * P])
                        ins.then_inc(sf_T, 1)
                    elif kind == "enter":
                        pe.wait_ge(act_free, i * MID_OUTS + (KT + 1 + MID_OUTS))
                        pe.wait_ge(sto_ready, i * 2 + (PRIMED + 2))
                        pe.wait_ge(yT_ready, i * 4 + (PRIMED + 4))
                        for n in range(3):
                            for t in range(2 * n, min(2 * n + 2, TILES)):
                                for p in range(2):
                                    ins = turn(bank(4 + n, P, ROWS[t], at=t % 2 * 256 + p * P), kT[:, p, t * P:t * P + ROWS[t]])
                            ins.then_inc(ktok_T, 1)
                    elif kind == "cache":
                        pe.wait_ge(kc_in, i * 16 + 16)
                        pe.wait_ge(ktok_ready, i * 3 + 1)
                        for p in range(2):
                            for a in range(4):
                                ins = turn(bank(7 - 3 * p, P, at=a * P), kcr[:, a, p * P:(p + 1) * P])
                            ins.then_inc(kc_T, 1)
                    elif kind == "leave":
                        pe.wait_ge(o_ready, i * JOBS + JOBS)
                        for p in range(2):
                            for t in range(TILES):
                                ins = turn(bank(4 + 2 * p, ROWS[t], at=t * P), otok[0:ROWS[t], t, p * P:(p + 1) * P])
                            ins.then_inc(o_T, 1)

            mid(0, FIRST_STEPS)
            with looped(pe, 3, st.all(), [10, 0, 0, MID_OUTS, MID_OUTS, 0]) as i:
                mid(i, LOOP_STEPS)
            mid(3, LAST_STEPS)

            G = G2
            pe.wait_ge(oT_ready, PRIMED + 8)
            pe.wait_ge(s_free, PRIMED + 4 * JOBS)
            for part in range(2):
                with looped(pe, 2, st.all(), [2, 0, 0, 4, 4, 0]) as i:
                    for n, s in enumerate((1, 0)):
                        duo_split()
                        for u in range(2):
                            pe.wait_ge(act_free, st.act(-1))
                            unit(s, u, xah, xal, KT, 2 * (2 * n + u))
                            st.act.up()
            pe.wait_ge(act_free, st.act())
            for xh, xl in ((G["xbh"], G["xbl"]), (xah, xal), (G["xbh"], G["xbl"]), (xah, xal)):
                xr.up(KT)
                pe.wait_ge(x_ready, xr())
                with looped(pe, 2, st.all(), [2, 0, 0, 4, 0, 4]) as i:
                    for n, s in enumerate((1, 0)):
                        duo_split()
                        for u in range(2):
                            pe.wait_ge(dve_free, st.dve(PRIMED - 1))
                            unit(s, u, xh, xl, KT, 2 * (2 * n + u))
                            st.dve.up()
            norm()
            full.up(KT)
            xr.up(KT)
            ffn((1, 0))
            norm()
            for f in range(KT):
                pe.wait_ge(full_ready, full.up())
                if f >= 4:
                    pe.wait_ge(fin_ready, f - 3)
                for t in range(TILES):
                    ins = turn(bank(2 * (f % 4), P, ROWS[t], at=t * P), G["full"][:, f % 2, t * P:t * P + ROWS[t]])
                ins.then_inc(fin_T, 1)


_INS = ["x_prompt", "x_sample", "cache_k", "cache_v", "cache_logf", "state_ssm", "state_conv", "meta_tokens",
        "norm_ffn1", "ffn1_w_in", "ffn1_w_out", "norm_mix", "w_in", "conv_w", "conv_b", "dt_bias", "a_log", "d_skip",
        "f_bias", "ssm_norm", "w_br_ssm", "w_br_attn", "w_out", "norm_ffn2", "ffn2_w_in", "ffn2_w_out", "norm_final"]
_OUTS = [(1, SEQ, D), (1, SAMPLE, D), (1, 1, PROMPT, HEADS, HD), (1, 1, PROMPT, HEADS, HD), (1, 1, PROMPT, HEADS),
         (1, 1, SSM_HEADS, HD, NSTATE), (1, 1, 3, D_CONV), (1, 1, SAMPLE, HEADS, HD), (1, 1, SAMPLE, HEADS, HD),
         (1, 1, SAMPLE, HEADS), (1, 1, SSM_HEADS, HD, NSTATE), (1, 1, 3, D_CONV)]


def kernel(**inputs):
    import numpy as _np
    import concourse.bacc as _bacc
    from concourse import mybir as _mybir
    from concourse.bass_utils import run_bass_kernel_spmd as _run

    nc = _bacc.Bacc("TRN2", target_bir_lowering=False, num_devices=1)
    arrays, args = {}, []
    for name in _INS:
        a = _np.ascontiguousarray(inputs[name])
        arrays[f"in_{name}_dram"] = a
        args.append(nc.dram_tensor(f"in_{name}_dram", a.shape, _mybir.dt.from_np(a.dtype), kind="ExternalInput").ap())
    for i, shape in enumerate(_OUTS):
        args.append(nc.dram_tensor(f"out_{i}_dram", shape, _mybir.dt.float32, kind="ExternalOutput").ap())
    fox_ssd_hybrid_kernel(nc, *args)
    r = _run(nc, [arrays], core_ids=[0])
    return tuple(r.results[0][f"out_{i}_dram"] for i in range(len(_OUTS)))
```
